# Optimizing a Trainium2 kernel written in Bass

```python
import math
import jax, jax.numpy as jnp
from jax import lax
import numpy as np

D_MODEL = 1024
BATCH = 1
SEQ = 512
DEPTH = 2

GRID_W = 64
CTX_LEN = 256
EPS = 1e-6
N_HEADS = 8
N_KV_HEADS = 2
GQA_GROUP = N_HEADS // N_KV_HEADS
HEAD_DIM = 64
AXIS_DIM = HEAD_DIM // 2
ATT_W = N_HEADS * HEAD_DIM
KV_W = N_KV_HEADS * HEAD_DIM
ATT_SCALE = HEAD_DIM ** -0.5
ROPE_THETA = 10000.0
Q_BLOCK = 128
SC_W = 512
CONV_K = 3
HY_W = 512
HY_ORDER = 2
HY_BANDS = 16
HY_EMB = 1 + 2 * HY_BANDS
HY_FH = 64
HY_FAST_DECAY = 0.3
HY_SLOW_DECAY = 1.5
HY_DECAY_TARGET = 1e-2
PEER_HEADS = 8
PEER_NKEYS = 128
PEER_N = PEER_NKEYS * PEER_NKEYS
PEER_DK = 128
PEER_TOPK = 16
PEER_CHUNK = 128
Q0 = 0
K0 = Q0 + ATT_W
V0 = K0 + KV_W
SC0 = V0 + KV_W
HY0 = SC0 + 3 * SC_W
GT0 = HY0 + (HY_ORDER + 1) * HY_W
IN_W = GT0 + 3 * D_MODEL

kernel_name = 'hybrid_attn_conv_hyena_peer_dit'

def _rmsnorm(x, g):
    xf = x.astype(jnp.float32)
    y = xf * lax.rsqrt(jnp.mean(xf * xf, axis=-1, keepdims=True) + EPS)
    return (y * g.astype(jnp.float32)).astype(x.dtype)

def _dwconv3(u, w):
    up = jnp.pad(u, ((0, 0), (1, 1), (0, 0)))
    return up[:, :-2] * w[0] + up[:, 1:-1] * w[1] + up[:, 2:] * w[2]

def _axial_rope(x):
    L = x.shape[1]
    pos = jnp.arange(L, dtype=jnp.int32)
    row = (pos // GRID_W).astype(jnp.float32)
    col = (pos % GRID_W).astype(jnp.float32)
    inv = jnp.power(ROPE_THETA, -jnp.arange(0, AXIS_DIM, 2, dtype=jnp.float32) / AXIS_DIM)

    def rot(xa, p):
        ang = p[:, None] * inv[None, :]
        cos = jnp.cos(ang)[None, :, None, :]
        sin = jnp.sin(ang)[None, :, None, :]
        x1, x2 = jnp.split(xa.astype(jnp.float32), 2, axis=-1)
        return jnp.concatenate([x1 * cos - x2 * sin, x2 * cos + x1 * sin], axis=-1)

    xr, xc = jnp.split(x, 2, axis=-1)
    return jnp.concatenate([rot(xr, row), rot(xc, col)], axis=-1).astype(x.dtype)

def _attend(q, k, v):
    s = jnp.einsum('bqhgd,bkhd->bhgqk', q, k, preferred_element_type=jnp.float32) * ATT_SCALE
    p = jax.nn.softmax(s, axis=-1).astype(v.dtype)
    return jnp.einsum('bhgqk,bkhd->bqhgd', p, v)

def _latent_attention(q, k_all, v_all):
    B, S = q.shape[:2]
    nb = S // Q_BLOCK
    qb = q.reshape(B, nb, Q_BLOCK, N_KV_HEADS, GQA_GROUP, HEAD_DIM).transpose(1, 0, 2, 3, 4, 5)
    ob = lax.map(lambda qi: _attend(qi, k_all, v_all), qb)
    return ob.transpose(1, 0, 2, 3, 4, 5).reshape(B, S, ATT_W)

def _short_conv(p, w):
    bg, cg, xs = jnp.split(p, 3, axis=-1)
    return bg * _dwconv3(cg * xs, w)

def _hyena_filter_fft(L, w1, b1, f1, w2, b2, f2, w3, decay):
    t = jnp.linspace(0.0, 1.0, L, dtype=jnp.float32)[:, None]
    w = 2.0 * math.pi * jnp.arange(L, dtype=jnp.float32)[:, None] / L
    bands = jnp.linspace(1e-4, HY_BANDS - 1, HY_BANDS, dtype=jnp.float32)[None, :]
    z = jnp.concatenate([t, jnp.cos(bands * w), -jnp.sin(bands * w)], axis=-1)
    h = jnp.sin(f1.astype(jnp.float32) * (z @ w1.astype(jnp.float32) + b1.astype(jnp.float32)))
    h = jnp.sin(f2.astype(jnp.float32) * (h @ w2.astype(jnp.float32) + b2.astype(jnp.float32)))
    h = (h @ w3.astype(jnp.float32)).reshape(L, HY_ORDER, 2, HY_W)
    window = jnp.exp(-t[:, :, None] * jnp.abs(decay.astype(jnp.float32)))
    h = h * window[:, :, None, :]
    h = h / jnp.sum(jnp.abs(h), axis=(0, 2), keepdims=True)
    hf, hb = h[:, :, 0], h[:, :, 1]
    k = jnp.concatenate([hf, jnp.zeros_like(hf[:1]), hb[:0:-1]], axis=0)
    return jnp.fft.rfft(k, axis=0)

def _long_conv(u, kf, bias):
    L = u.shape[1]
    uf = u.astype(jnp.float32)
    y = jnp.fft.irfft(jnp.fft.rfft(uf, n=2 * L, axis=1) * kf[None], n=2 * L, axis=1)[:, :L]
    return (y + uf * bias.astype(jnp.float32)).astype(u.dtype)

def _hyena(p, conv_w, conv_b, kf, bias):
    u = _dwconv3(p, conv_w) + conv_b
    v, x1, x2 = jnp.split(u, HY_ORDER + 1, axis=-1)
    z = v
    for o, gate in enumerate((x1, x2)):
        z = gate * _long_conv(z, kf[:, o], bias[o])
    return z

def _merge(gate_pre, y_att, y_sc, y_hy, w_att, w_sc, w_hy, w_o):
    g_att, g_sc, g_hy = jnp.split(jax.nn.sigmoid(gate_pre), 3, axis=-1)
    m = g_att * (y_att @ w_att) + g_sc * (y_sc @ w_sc) + g_hy * (y_hy @ w_hy)
    return m @ w_o

def _peer(tok, wq, subkeys, u_tab, v_tab):
    T, D = tok.shape

    def chunk(hc):
        q = (hc @ wq).reshape(PEER_CHUNK, PEER_HEADS, 2, PEER_DK // 2)
        s = jnp.einsum('chpd,hpnd->chpn', q, subkeys, preferred_element_type=jnp.float32)
        s1, i1 = lax.top_k(s[:, :, 0], PEER_TOPK)
        s2, i2 = lax.top_k(s[:, :, 1], PEER_TOPK)
        cand = (s1[..., :, None] + s2[..., None, :]).reshape(PEER_CHUNK, PEER_HEADS, PEER_TOPK * PEER_TOPK)
        sc, ic = lax.top_k(cand, PEER_TOPK)
        e = (jnp.take_along_axis(i1, ic // PEER_TOPK, axis=-1) * PEER_NKEYS
             + jnp.take_along_axis(i2, ic % PEER_TOPK, axis=-1))
        g = jax.nn.softmax(sc, axis=-1)
        a = jax.nn.gelu(jnp.einsum('chkd,cd->chk', u_tab[e], hc, preferred_element_type=jnp.float32),
                        approximate=False)
        return jnp.einsum('chk,chkd->cd', (g * a).astype(v_tab.dtype), v_tab[e])

    out = lax.map(chunk, tok.reshape(T // PEER_CHUNK, PEER_CHUNK, D))
    return out.reshape(T, D)

def setup_inputs(seed: int = 0) -> dict:
    key = jax.random.key(seed)
    ks = list(jax.random.split(key, 40))
    cnt = [0]

    def nrm(shape, scale):
        k = ks[cnt[0]]
        cnt[0] += 1
        return jax.random.normal(k, shape, jnp.float32) * scale

    L = DEPTH
    D = D_MODEL
    dec = jnp.linspace(math.log(HY_DECAY_TARGET) / HY_SLOW_DECAY, math.log(HY_DECAY_TARGET) / HY_FAST_DECAY,
                       HY_W, dtype=jnp.float32)
    return {
        'x': nrm((BATCH, SEQ, D), 1.0),
        'c': nrm((BATCH, D), 1.0),
        'ctx': nrm((BATCH, CTX_LEN, D), 1.0),
        'c_ctx': nrm((D,), 1.0),
        'w_mod': nrm((L, D, 6 * D), D ** -0.5),
        'b_mod': nrm((L, 6 * D), 0.02),
        'g_norm1': 1.0 + nrm((L, D), 0.02),
        'g_norm2': 1.0 + nrm((L, D), 0.02),
        'w_in': nrm((L, D, IN_W), D ** -0.5),
        'q_gain': 1.0 + nrm((L, HEAD_DIM), 0.02),
        'k_gain': 1.0 + nrm((L, HEAD_DIM), 0.02),
        'sc_conv_w': nrm((L, CONV_K, SC_W), CONV_K ** -0.5),
        'hy_conv_w': nrm((L, CONV_K, (HY_ORDER + 1) * HY_W), CONV_K ** -0.5),
        'hy_conv_b': nrm((L, (HY_ORDER + 1) * HY_W), 0.02),
        'hy_w1': nrm((L, HY_EMB, HY_FH), HY_EMB ** -0.5),
        'hy_b1': nrm((L, HY_FH), 0.02),
        'hy_f1': 1.0 + nrm((L, HY_FH), 0.02),
        'hy_w2': nrm((L, HY_FH, HY_FH), HY_FH ** -0.5),
        'hy_b2': nrm((L, HY_FH), 0.02),
        'hy_f2': 1.0 + nrm((L, HY_FH), 0.02),
        'hy_w3': nrm((L, HY_FH, HY_ORDER * 2 * HY_W), HY_FH ** -0.5),
        'hy_decay': dec[None, None, :] + nrm((L, HY_ORDER, HY_W), 0.1),
        'hy_bias': nrm((L, HY_ORDER, HY_W), 1.0),
        'w_br_att': nrm((L, ATT_W, D), ATT_W ** -0.5),
        'w_br_sc': nrm((L, SC_W, D), SC_W ** -0.5),
        'w_br_hy': nrm((L, HY_W, D), HY_W ** -0.5),
        'w_out': nrm((L, D, D), D ** -0.5),
        'peer_wq': nrm((L, D, PEER_HEADS * PEER_DK), D ** -0.5),
        'peer_subkeys': nrm((L, PEER_HEADS, 2, PEER_NKEYS, PEER_DK // 2), (PEER_DK // 2) ** -0.5),
        'peer_u': nrm((L, PEER_N, D), D ** -0.5),
        'peer_v': nrm((L, PEER_N, D), PEER_HEADS ** -0.5),
        'g_final': 1.0 + nrm((D,), 0.02),
    }

def reference(x, c, ctx, c_ctx, w_mod, b_mod, g_norm1, g_norm2, w_in, q_gain, k_gain, sc_conv_w,
              hy_conv_w, hy_conv_b, hy_w1, hy_b1, hy_f1, hy_w2, hy_b2, hy_f2, hy_w3, hy_decay, hy_bias,
              w_br_att, w_br_sc, w_br_hy, w_out, peer_wq, peer_subkeys, peer_u, peer_v, g_final):
    B, S, D = x.shape
    Lc = ctx.shape[1]
    cond_lat = jax.nn.silu(c)
    cond_ctx = jax.nn.silu(c_ctx)
    for l in range(DEPTH):
        need_ctx = l < DEPTH - 1
        mod_lat = (cond_lat @ w_mod[l] + b_mod[l])[:, None, :]
        mod_ctx = cond_ctx @ w_mod[l] + b_mod[l]
        sh1, sc1, gt1, sh2, sc2, gt2 = jnp.split(mod_lat, 6, axis=-1)
        csh1, csc1, cgt1, csh2, csc2, cgt2 = jnp.split(mod_ctx, 6, axis=-1)
        hy_params = (hy_w1[l], hy_b1[l], hy_f1[l], hy_w2[l], hy_b2[l], hy_f2[l], hy_w3[l], hy_decay[l])

        h = _rmsnorm(x, g_norm1[l]) * (1.0 + sc1) + sh1
        hc = _rmsnorm(ctx, g_norm1[l]) * (1.0 + csc1) + csh1
        p = h @ w_in[l]
        q = _axial_rope(_rmsnorm(p[..., Q0:K0].reshape(B, S, N_HEADS, HEAD_DIM), q_gain[l]))
        k = _axial_rope(_rmsnorm(p[..., K0:V0].reshape(B, S, N_KV_HEADS, HEAD_DIM), k_gain[l]))
        v = p[..., V0:SC0].reshape(B, S, N_KV_HEADS, HEAD_DIM)
        if need_ctx:
            pc = hc @ w_in[l]
            kvc = pc[..., K0:SC0]
        else:
            kvc = hc @ w_in[l][:, K0:SC0]
        kc = _rmsnorm(kvc[..., :KV_W].reshape(B, Lc, N_KV_HEADS, HEAD_DIM), k_gain[l])
        vc = kvc[..., KV_W:].reshape(B, Lc, N_KV_HEADS, HEAD_DIM)
        k_all = jnp.concatenate([kc, k], axis=1)
        v_all = jnp.concatenate([vc, v], axis=1)

        y_att = _latent_attention(q, k_all, v_all)
        y_sc = _short_conv(p[..., SC0:HY0], sc_conv_w[l])
        y_hy = _hyena(p[..., HY0:GT0], hy_conv_w[l], hy_conv_b[l], _hyena_filter_fft(S, *hy_params), hy_bias[l])
        x = x + gt1 * _merge(p[..., GT0:], y_att, y_sc, y_hy, w_br_att[l], w_br_sc[l], w_br_hy[l], w_out[l])

        if need_ctx:
            qc = _rmsnorm(pc[..., Q0:K0].reshape(B, Lc, N_HEADS, HEAD_DIM), q_gain[l])
            yc_att = _attend(qc.reshape(B, Lc, N_KV_HEADS, GQA_GROUP, HEAD_DIM), kc, vc).reshape(B, Lc, ATT_W)
            yc_sc = _short_conv(pc[..., SC0:HY0], sc_conv_w[l])
            yc_hy = _hyena(pc[..., HY0:GT0], hy_conv_w[l], hy_conv_b[l], _hyena_filter_fft(Lc, *hy_params),
                           hy_bias[l])
            ctx = ctx + cgt1 * _merge(pc[..., GT0:], yc_att, yc_sc, yc_hy, w_br_att[l], w_br_sc[l], w_br_hy[l],
                                      w_out[l])

        h2 = _rmsnorm(x, g_norm2[l]) * (1.0 + sc2) + sh2
        if need_ctx:
            h2c = _rmsnorm(ctx, g_norm2[l]) * (1.0 + csc2) + csh2
            tok = jnp.concatenate([h2.reshape(B * S, D), h2c.reshape(B * Lc, D)], axis=0)
            f = _peer(tok, peer_wq[l], peer_subkeys[l], peer_u[l], peer_v[l])
            x = x + gt2 * f[:B * S].reshape(B, S, D)
            ctx = ctx + cgt2 * f[B * S:].reshape(B, Lc, D)
        else:
            f = _peer(h2.reshape(B * S, D), peer_wq[l], peer_subkeys[l], peer_u[l], peer_v[l])
            x = x + gt2 * f.reshape(B, S, D)
    return _rmsnorm(x, g_final)


_drawn_inputs = setup_inputs


def setup_inputs(seed=0):
    import zlib

    import numpy as np

    out = dict(_drawn_inputs(seed))
    spreads = {}
    factors = {'g_norm2': 2.696,
     'q_gain': 8.0,
     'k_gain': 8.0,
     'hy_b1': 3.53,
     'hy_f1': 7.195,
     'hy_b2': 3.219,
     'hy_f2': 8.0,
     'g_final': 2.873}
    for name, (base, spread) in spreads.items():
        noise = np.random.default_rng([zlib.crc32(name.encode()), seed]).standard_normal(out[name].shape)
        drawn = base * np.exp(spread * noise) if base else spread * noise
        out[name] = __import__('jax').numpy.asarray(drawn.astype(out[name].dtype))
    for name, factor in factors.items():
        out[name] = (out[name] * factor).astype(out[name].dtype)
    return out
```

```python
import math
from contextlib import ExitStack

import numpy as np

import concourse.bass as bass
from concourse import mybir

F32 = mybir.dt.float32
U32 = mybir.dt.uint32
I32 = mybir.dt.int32
ALU = mybir.AluOpType
ACT = mybir.ActivationFunctionType
AX = mybir.AxisListType

P = 128
D = 1024
DEPTH = 2
L_LAT, L_CTX = 512, 256
T_ALL = L_LAT + L_CTX
KD = D // P
NT_LAT, NT_CTX = L_LAT // P, L_CTX // P
NT = NT_LAT + NT_CTX
GRID_W = 64
HEADS, KV_HEADS, HD = 8, 2, 64
PAIRS = HEADS // 2
W_BR = 512
KB_BR = W_BR // P
EPS = 1e-6
FH = 64
BANDS = 16
EMB = 1 + 2 * BANDS
B_Q, B_K, B_V = 0, 4, 5
B_SC, B_HY, B_GATE = 6, 18, 30
N_IN = 54
SH1, SC1, GT1, SH2, SC2, GT2 = (KD * i for i in range(6))
N_MOD = 6 * KD
PH, NK, DK, TOPK = 8, 128, 64, 16
N_EXP = NK * NK
RING = 8
C_BMOD, C_G1, C_G2 = 0, N_MOD, N_MOD + KD
C_SCW = C_G2 + KD
C_HYW = C_SCW + 3 * KB_BR
C_HYB = C_HYW + 3 * 3 * KB_BR
C_FIL = C_HYB + 3 * KB_BR
N_COLS = C_FIL + 4

TWO_PI = 2.0 * math.pi
PI_HI = 6.28125
PI_MID = float(np.float32(np.frombuffer(np.array([np.float32(TWO_PI - PI_HI)]).view(np.uint32) & np.uint32(0xFFFFF000), np.float32)[0]))
PI_LO = TWO_PI - PI_HI - PI_MID
ROUND = 1.5 * 2.0 ** 23
PI_F32 = float(np.nextafter(np.float32(math.pi), np.float32(0)))


def dft_tables(length):
    n = np.arange(length)
    ang = np.pi * ((n[:, None] * n[None, :]) % (2 * length)) / length
    cos, sin = np.cos(ang), -np.sin(ang)
    alt = (-1.0) ** n
    fwd, inv, cos_b = sin.copy(), sin.copy(), cos[:, :P].copy()
    fwd[:, 0] = alt
    inv[0, :] = alt
    cos_b[:, 0] = alt
    parts = [cos, fwd, inv, sin[:, :P], cos_b]
    rows = [a.reshape(length // P, P, -1).transpose(1, 0, 2).reshape(P, -1) for a in parts]
    return np.ascontiguousarray(np.concatenate(rows, axis=1).astype(np.float32))


def filter_features(length):
    t = np.linspace(0.0, 1.0, length, dtype=np.float32)[:, None]
    w = (2.0 * math.pi * np.arange(length, dtype=np.float32)[:, None] / length).astype(np.float32)
    bands = np.linspace(1e-4, BANDS - 1, BANDS, dtype=np.float32)[None, :]
    z = np.concatenate([t, np.cos(bands * w), -np.sin(bands * w)], axis=-1)
    return np.ascontiguousarray(z.T.astype(np.float32))


def rope_table():
    pos = np.arange(L_LAT)
    inv = np.power(np.float32(10000.0), -np.arange(0, 32, 2, dtype=np.float32) / 32)
    ang = np.stack([(pos // GRID_W)[:, None] * inv, (pos % GRID_W)[:, None] * inv], axis=1)
    t = np.stack([np.cos(ang), np.sin(ang)], axis=1).reshape(NT_LAT, P, 64)
    return np.ascontiguousarray(t.transpose(1, 0, 2).reshape(P, NT_LAT * 64).astype(np.float32))


def shape_constants():
    out = np.zeros((P, 8), np.float32)
    for a, length in ((0, L_LAT), (4, L_CTX)):
        t = np.linspace(0.0, 1.0, length, dtype=np.float32).reshape(-1, P).T
        out[:, a:a + t.shape[1]] = -t
    w = np.zeros((P, 2), np.float32)
    w[:, 0], w[:, 1] = 1.0 / L_LAT, 1.0 / L_CTX
    w[0] *= 0.5
    return np.concatenate([out, w], axis=1)


class Steps:

    def __init__(self, eng, sem):
        self.eng, self.sem, self.n = eng, sem, 0

    def do(self, ins):
        ins.then_inc(self.sem, 1)
        self.n += 1
        return self.n

    def wait(self, n=None):
        self.eng.wait_ge(self.sem, self.n if n is None else n)


class Phase:

    count = 0

    def __init__(self, nc):
        self.nc, self.sems = nc, []
        Phase.count += 1
        self.tag = f"p{Phase.count}"

    def sem(self, name):
        s = self.nc.alloc_semaphore(f"{name}_{self.tag}")
        self.sems.append(s)
        return s

    def __enter__(self):
        self.stack = ExitStack()
        self.block = self.stack.enter_context(self.nc.Block())
        return self

    def __exit__(self, *err):
        self.stack.__exit__(*err)
        if err[0] is None:
            self.nc.clear_and_free_semaphores(self.sems)
            self.nc.all_engine_barrier(sem_only=True)


class Chip:

    def __init__(self, nc, ctx, io):
        self.nc, self.io = nc, io
        self.arena = ctx.enter_context(nc.sbuf_tensor("arena", [P, 201 * 256], F32))
        sb = lambda n, s: ctx.enter_context(nc.sbuf_tensor(n, s, F32))
        self.ident = sb("ident", [P, P])
        self.ones = sb("ones", [P, P])
        self.rope = sb("rope", [P, NT_LAT, 2, 2, 16])
        self.cond = sb("cond", [P, KD, 2])
        self.cols = sb("cols", [P, N_COLS])
        self.consts = sb("consts", [P, 10])
        self.mod = sb("mod", [P, N_MOD, 2])
        self.ab = sb("ab", [P, 2, KD, 2])
        self.stat = sb("stat", [P, 2, 16])
        self.psum = ctx.enter_context(nc.psum_tensor("psum", [P, 8 * 512], F32))
        self.xs = self.at(0, NT, D)
        self.hT = self.at(24, KD, T_ALL)
        self.wring = self.at(48, RING, KD, P)

    def at(self, kib, *shape):
        n = int(np.prod(shape))
        v = self.arena[:, int(kib * 256):int(kib * 256) + n]
        if len(shape) == 2:
            return v.rearrange("p (a b) -> p a b", a=shape[0])
        if len(shape) == 3:
            return v.rearrange("p (a b c) -> p a b c", a=shape[0], b=shape[1])
        return v

    def bank(self, b, width=512, parts=P):
        return self.psum[0:parts, b * 512:b * 512 + width]


def phase_load(c):
    nc, io = c.nc, c.io
    with Phase(nc) as ph:
        landed, made, made_ones, cond_in, cond_done = (ph.sem(s) for s in (
            "inputs_landed", "identity_made", "ones_made", "cond_landed", "cond_done"))

        @ph.block.sync
        def _(sp):
            sp.dma_start(c.cond[:], io["cond"]).then_inc(cond_in, 16)
            sp.dma_start(c.xs[:, 0:NT_LAT, :], io["x"]).then_inc(landed, 16)
            sp.dma_start(c.xs[:, NT_LAT:NT, :], io["ctx"]).then_inc(landed, 16)
            sp.dma_start(c.rope[:], io["rope"]).then_inc(landed, 16)
            sp.dma_start(c.consts[:], io["consts"]).then_inc(landed, 16)
            sp.wait_ge(landed, 64)

        @ph.block.gpsimd
        def _(pool):
            nc.gpsimd.memset(c.ident[:], 0.0).then_inc(made, 1)
            pool.wait_ge(made, 1)
            nc.gpsimd.affine_select(out=c.ident[:], in_=c.ident[:], compare_op=ALU.not_equal, fill=1.0,
                                    base=0, pattern=[[-1, P]], channel_multiplier=1).then_inc(made, 1)

        @ph.block.vector
        def _(dve):
            nc.vector.memset(c.ones[:], 1.0).then_inc(made_ones, 1)

        @ph.block.scalar
        def _(act):
            act.wait_ge(cond_in, 16)
            nc.scalar.activation(c.cond[:], c.cond[:], ACT.Silu).then_inc(cond_done, 1)


def phase_mod(c, layer):
    nc, io = c.nc, c.io
    rounds = N_MOD // RING
    with Phase(nc) as ph:
        w_landed = [ph.sem(f"w_landed{s}") for s in range(RING)]
        w_used, cols_in, dve_done = (ph.sem(s) for s in ("w_used", "cols_landed", "dve_steps"))

        @ph.block.sync
        def _(sp):
            sp.dma_start(c.cols[:], io["cols"][layer]).then_inc(cols_in, 16)
            with sp.Fori(0, rounds) as i:
                for s in range(RING):
                    sp.wait_ge(w_used, i * RING + (s + 1))
                    sp.dma_start(c.wring[:, s], io["w_mod"][layer][bass.ds(i * RING + s, 1)].rearrange(
                        "a p k n -> p (a k) n")).then_inc(w_landed[s], 16)

        @ph.block.tensor
        def _(pe):
            pe.sem_inc(w_used, RING)
            with pe.Fori(0, rounds) as i:
                for s in range(RING):
                    pe.wait_ge(w_landed[s], i * 16 + 16)
                    for k in range(KD):
                        last = nc.tensor.matmul(c.psum[:, bass.ds(i * (2 * RING) + 2 * s, 2)], c.wring[:, s, k],
                                                c.cond[:, k], start=(k == 0), stop=(k == KD - 1))
                    last.then_inc(w_used, 1)

        @ph.block.vector
        def _(dve):
            st = Steps(dve, dve_done)
            dve.wait_ge(cols_in, 16)
            dve.wait_ge(w_used, RING + N_MOD)
            st.do(nc.vector.tensor_tensor(
                c.mod[:], c.psum[:, 0:2 * N_MOD].rearrange("p (j s) -> p j s", s=2),
                c.cols[:, C_BMOD:C_BMOD + N_MOD].unsqueeze(2).to_broadcast([P, N_MOD, 2]), ALU.add))
            st.wait()
            for n, (sc, g) in enumerate(((SC1, C_G1), (SC2, C_G2))):
                st.do(nc.vector.scalar_tensor_tensor(
                    out=c.ab[:, n], in0=c.mod[:, sc:sc + KD], scalar=1.0,
                    in1=c.cols[:, g:g + KD].unsqueeze(2).to_broadcast([P, KD, 2]), op0=ALU.add, op1=ALU.mult))


def norm_sems(ph):
    return [ph.sem(s) for s in ("squares_summed", "means_ready", "roots_ready", "dve_steps")]


def act_norm(c, act, tiles, sq, ms, root):
    nc, junk = c.nc, c.at(185, 2, D)
    for i, t in enumerate(tiles):
        if i >= 2:
            act.wait_ge(sq, i - 1)
        nc.scalar.activation(junk[:, i % 2], c.xs[:, t], ACT.Square, accum_out=c.stat[:, 0, i:i + 1]).then_inc(sq, 1)
    act.wait_ge(ms, 1)
    nc.scalar.activation(c.stat[:, 1, 0:len(tiles)], c.stat[:, 1, 0:len(tiles)], ACT.Sqrt).then_inc(root, 1)


def dve_norm(c, dve, st, tiles, sq, ms, root):
    nc = c.nc
    n = len(tiles)
    dve.wait_ge(sq, n)
    nc.vector.tensor_scalar(c.stat[:, 1, 0:n], c.stat[:, 0, 0:n], 1.0 / D, EPS, ALU.mult, ALU.add).then_inc(ms, 1)
    dve.wait_ge(root, 1)
    st.do(nc.vector.reciprocal(c.stat[:, 0, 0:n], c.stat[:, 1, 0:n]))
    st.wait()


def phase_norm1(c, tiles):
    nc = c.nc
    n = len(tiles)
    xn = c.at(116, NT, D)
    jobs = [(k, s) for k in range(KD) for s in range(2)]
    with Phase(nc) as ph:
        sq, ms, root, steps = norm_sems(ph)
        xn_ready, turned, out_a, out_d = (ph.sem(s) for s in ("xn_ready", "transposed", "evacuated_act", "evacuated_dve"))

        @ph.block.scalar
        def _(act):
            act_norm(c, act, tiles, sq, ms, root)
            for j, (k, s) in enumerate(jobs):
                if s == 1:
                    act.wait_ge(turned, j + 1)
                    nc.scalar.activation(c.hT[:, k, L_LAT:T_ALL], c.bank(j % 8, L_CTX), ACT.Identity,
                                         bias=c.mod[:, SH1 + k, 1:2], scale=c.ab[:, 0, k, 1:2]).then_inc(out_a, 1)

        @ph.block.vector
        def _(dve):
            st = Steps(dve, steps)
            dve_norm(c, dve, st, tiles, sq, ms, root)
            for i, t in enumerate(tiles):
                nc.vector.tensor_scalar(xn[:, t], c.xs[:, t], c.stat[:, 0, i:i + 1], None, ALU.mult).then_inc(xn_ready, 1)
            for j, (k, s) in enumerate(jobs):
                if s == 0:
                    dve.wait_ge(turned, j + 1)
                    nc.vector.tensor_scalar(c.hT[:, k, 0:L_LAT], c.bank(j % 8), c.ab[:, 0, k, 0:1],
                                            c.mod[:, SH1 + k, 0:1], ALU.mult, ALU.add).then_inc(out_d, 1)

        @ph.block.tensor
        def _(pe):
            pe.wait_ge(xn_ready, n)
            for j, (k, s) in enumerate(jobs):
                if j >= 8:
                    pe.wait_ge(out_a if s else out_d, (j - 8) // 2 + 1)
                span = range(NT_LAT) if s == 0 else range(NT_LAT, NT)
                for i, t in enumerate(span):
                    last = nc.tensor.transpose(c.psum[:, (j % 8) * 512 + i * P:(j % 8) * 512 + (i + 1) * P],
                                               xn[:, t, k * P:(k + 1) * P], c.ident[:])
                last.then_inc(turned, 1)


def phase_qkv(c, layer, full):
    nc, io = c.nc, c.io
    qT, kT, vN = c.at(116, PAIRS, T_ALL), c.at(128, KV_HEADS, T_ALL), c.at(134, NT, P)
    sqb = c.at(143, 2, 640)
    qn = c.at(148, 2, 640)
    qr = c.at(153, 2, 640)
    kd = c.at(158, 2, 256)
    tmp = c.at(160, 4, 320)
    gain = c.at(166, 640)
    ssq = c.at(169, 2, 16)
    rr = c.at(169.5, 2, 16)
    tiles = list(range(NT))
    with Phase(nc) as ph:
        w_in, gain_in, proj, sq_d, ms, root, vd, steps, ready, turned, evac = (ph.sem(s) for s in (
            "w_landed", "gain_landed", "projected", "squared", "means_ready", "roots_ready", "v_kept",
            "dve_steps", "qk_ready", "transposed", "evacuated"))
        qk_read = ph.sem("qk_psum_read")

        def q_cols(t):
            return (0 if t < NT_LAT or full else 512, 640)

        @ph.block.sync
        def _(sp):
            sp.dma_start(c.wring[:, 0:6].rearrange("p b k n -> p b (k n)"), io["w_in"][layer][0:6].rearrange(
                "b p k n -> p b (k n)")).then_inc(w_in, 16)
            sp.dma_start(gain, io["gains"][layer:layer + 1].to_broadcast([P, 640])).then_inc(gain_in, 16)

        @ph.block.tensor
        def _(pe):
            def project(t):
                b = (t % 2) * 2
                if t >= 2:
                    pe.wait_ge(qk_read, t - 1)
                    pe.wait_ge(vd, t - 1)
                w = c.wring
                if q_cols(t)[0] == 0:
                    for k in range(KD):
                        nc.tensor.matmul(c.bank(b), c.hT[:, k, t * P:(t + 1) * P], w[:, 0:4, k, :],
                                         start=(k == 0), stop=(k == KD - 1))
                for k in range(KD):
                    last = nc.tensor.matmul(c.bank(b + 1, 256), c.hT[:, k, t * P:(t + 1) * P], w[:, 4:6, k, :],
                                            start=(k == 0), stop=(k == KD - 1))
                last.then_inc(proj, 1)

            def turn(t):
                b = 4 + (t % 2) * 2
                pe.wait_ge(ready, t + 1)
                if t >= 2:
                    pe.wait_ge(evac, t - 1)
                if q_cols(t)[0] == 0:
                    for j in range(PAIRS):
                        nc.tensor.transpose(c.psum[:, b * 512 + j * P:b * 512 + (j + 1) * P],
                                            qr[:, t % 2, j * P:(j + 1) * P], c.ident[:])
                for j in range(KV_HEADS):
                    last = nc.tensor.transpose(c.psum[:, (b + 1) * 512 + j * P:(b + 1) * 512 + (j + 1) * P],
                                               kd[:, t % 2, j * P:(j + 1) * P], c.ident[:])
                last.then_inc(turned, 1)

            pe.wait_ge(w_in, 16)
            for t in tiles:
                project(t)
                if t >= 1:
                    turn(t - 1)
            turn(NT - 1)

        @ph.block.scalar
        def _(act):
            def keep(t):
                b = 4 + (t % 2) * 2
                act.wait_ge(turned, t + 1)
                if q_cols(t)[0] == 0:
                    nc.scalar.activation(qT[:, :, t * P:(t + 1) * P], c.bank(b).rearrange("p (a b) -> p a b", a=PAIRS), ACT.Copy)
                nc.scalar.activation(kT[:, :, t * P:(t + 1) * P], c.bank(b + 1, 256).rearrange("p (a b) -> p a b", a=2),
                                     ACT.Copy).then_inc(evac, 1)

            for t in tiles:
                b = (t % 2) * 2
                lo, hi = q_cols(t)
                act.wait_ge(proj, t + 1)
                if t >= 2:
                    act.wait_ge(ms, t - 1)
                nc.scalar.activation(sqb[:, t % 2, lo:hi], c.psum[:, b * 512 + lo:b * 512 + hi], ACT.Square).then_inc(sq_d, 1)
                nc.scalar.activation(vN[:, t], c.psum[:, b * 512 + 640:b * 512 + 768], ACT.Copy).then_inc(vd, 1)
                act.wait_ge(ms, t + 1)
                nc.scalar.activation(ssq[:, t % 2, lo // HD:10], ssq[:, t % 2, lo // HD:10], ACT.Sqrt).then_inc(root, 1)
                if t >= 1:
                    keep(t - 1)
            keep(NT - 1)

        @ph.block.vector
        def _(dve):
            st = Steps(dve, steps)
            dve.wait_ge(gain_in, 16)
            for t in tiles:
                b, p = (t % 2) * 2, t % 2
                lo, hi = q_cols(t)
                h0, nh = lo // HD, (hi - lo) // HD
                heads = lambda v: v[:, lo:hi].rearrange("p (h d) -> p h d", d=HD)
                dve.wait_ge(sq_d, t + 1)
                if t >= 2:
                    dve.wait_ge(root, t - 1)
                st.wait()
                st.do(nc.vector.tensor_reduce(ssq[:, p, h0:10], heads(sqb[:, p]), AX.X, ALU.add))
                st.wait()
                nc.vector.tensor_scalar(ssq[:, p, h0:10], ssq[:, p, h0:10], 1.0 / HD, EPS, ALU.mult, ALU.add).then_inc(ms, 1)
                dve.wait_ge(root, t + 1)
                st.do(nc.vector.reciprocal(rr[:, p, h0:10], ssq[:, p, h0:10]))
                st.wait()
                if h0 == 0:
                    st.do(nc.vector.tensor_scalar(rr[:, p, 0:HEADS], rr[:, p, 0:HEADS], HD ** -0.5, None, ALU.mult))
                    st.wait()
                nc.vector.tensor_tensor(heads(qn[:, p]), c.psum[:, b * 512 + lo:b * 512 + hi].rearrange("p (h d) -> p h d", d=HD),
                                        rr[:, p, h0:10].unsqueeze(2).to_broadcast([P, nh, HD]), ALU.mult).then_inc(qk_read, 1)
                dve.wait_ge(qk_read, t + 1)
                if t >= 2:
                    dve.wait_ge(turned, t - 1)
                target = qn if t < NT_LAT else qr
                st.do(nc.vector.tensor_tensor(target[:, p, lo:hi], qn[:, p, lo:hi], gain[:, lo:hi], ALU.mult))
                st.wait()
                if t < NT_LAT:
                    half = lambda v, i: v.rearrange("p (g r c) -> p g r c", r=2, c=16)[:, :, i, :].rearrange(
                        "p (h a) c -> p h a c", a=2)
                    table = lambda i: c.rope[:, t, i].unsqueeze(1).to_broadcast([P, 10, 2, 16])
                    w4 = [tmp[:, i].rearrange("p (h a c) -> p h a c", a=2, c=16) for i in range(4)]
                    for i, (h, s) in enumerate(((0, 0), (1, 1), (1, 0), (0, 1))):
                        st.do(nc.vector.tensor_tensor(w4[i], half(qn[:, p], h), table(s), ALU.mult))
                    st.wait()
                    st.do(nc.vector.tensor_tensor(half(qr[:, p], 0), w4[0], w4[1], ALU.subtract))
                    st.do(nc.vector.tensor_tensor(half(qr[:, p], 1), w4[2], w4[3], ALU.add))
                    st.wait()
                nc.vector.tensor_copy(kd[:, p].rearrange("p (v r d) -> p v r d", r=2, d=HD),
                                      qr[:, p, 512:640].rearrange("p (v d) -> p v d", d=HD).unsqueeze(2).to_broadcast(
                                          [P, KV_HEADS, 2, HD])).then_inc(ready, 1)


def phase_attention(c, full):
    nc = c.nc
    qT, kT, vN = c.at(116, PAIRS, T_ALL), c.at(128, KV_HEADS, T_ALL), c.at(134, NT, P)
    prob = c.at(137, 2, T_ALL)
    pT = c.at(143, 2, NT, L_LAT)
    yT = c.at(80, KB_BR, T_ALL)
    nmax, rsum, rinv = c.at(168, 4), c.at(168.25, 4), c.at(168.5, 4)
    groups = []
    for pair in range(PAIRS):
        for hh in range(2):
            groups.append((pair, hh, list(range(NT_LAT)), list(range(NT))))
    if full:
        for pair in range(PAIRS):
            for hh in range(2):
                groups.append((pair, hh, list(range(NT_LAT, NT)), list(range(NT_LAT, NT))))
    units = [(g, i, q) for g, (_, _, qs, _) in enumerate(groups) for i, q in enumerate(qs)]
    last_unit = [max(u for u, x in enumerate(units) if x[0] == g) for g in range(len(groups))]
    with Phase(nc) as ph:
        scored, maxed, exped, normed, turned, kept, summed, y_kept, steps = (ph.sem(s) for s in (
            "scores_ready", "max_ready", "exp_done", "probs_ready", "probs_turned", "turned_kept",
            "values_summed", "y_kept", "dve_steps"))

        @ph.block.tensor
        def _(pe):
            def score(u):
                g, _, q = units[u]
                pair, hh, _, keys = groups[g]
                kv = (2 * pair + hh) // (HEADS // KV_HEADS)
                if u >= 2:
                    pe.wait_ge(exped, u - 1)
                b = (u % 2) * 1024
                r = slice(64 * hh, 64 * hh + 64)
                if keys[0] == 0:
                    nc.tensor.matmul(c.psum[:, b:b + 512], qT[r, pair, q * P:(q + 1) * P], kT[r, kv, 0:512], start=True, stop=True)
                nc.tensor.matmul(c.psum[:, b + 512:b + 768], qT[r, pair, q * P:(q + 1) * P], kT[r, kv, 512:768],
                                 start=True, stop=True).then_inc(scored, 1)

            def turn(u):
                g = units[u][0]
                pe.wait_ge(normed, u + 1)
                if u >= 1:
                    pe.wait_ge(kept, u)
                for kt in groups[g][3]:
                    last = nc.tensor.transpose(c.psum[:, 2048 + kt * P:2048 + (kt + 1) * P], prob[:, u % 2, kt * P:(kt + 1) * P], c.ident[:])
                last.then_inc(turned, 1)

            def values(g):
                pair, hh, qs, keys = groups[g]
                kv = (2 * pair + hh) // (HEADS // KV_HEADS)
                w = len(qs) * P
                pe.wait_ge(kept, last_unit[g] + 1)
                if hh == 0 and g >= 4:
                    pe.wait_ge(y_kept, g // 2 - 1)
                bank = 6 + (g // 2) % 2
                for i, kt in enumerate(keys):
                    last = nc.tensor.matmul(c.psum[64 * hh:64 * hh + 64, bank * 512:bank * 512 + w], vN[:, kt, kv * HD:(kv + 1) * HD],
                                            pT[:, g % 2, kt, 0:w], start=(i == 0), stop=(i == len(keys) - 1))
                last.then_inc(summed, 1)

            for u in range(len(units) + 2):
                if u < len(units):
                    score(u)
                if 1 <= u <= len(units):
                    turn(u - 1)
                if u >= 2 and (u - 2) in last_unit:
                    values(last_unit.index(u - 2))

        @ph.block.vector
        def _(dve):
            st = Steps(dve, steps)
            for u in range(len(units) + 1):
                if u < len(units):
                    lo = groups[units[u][0]][3][0] * P
                    dve.wait_ge(scored, u + 1)
                    nc.vector.tensor_reduce(nmax[:, u % 4:u % 4 + 1], c.psum[:, (u % 2) * 1024 + lo:(u % 2) * 1024 + 768],
                                            AX.X, ALU.max, negate=True).then_inc(maxed, 1)
                if u >= 1:
                    v = u - 1
                    lo = groups[units[v][0]][3][0] * P
                    dve.wait_ge(exped, v + 1)
                    st.do(nc.vector.reciprocal(rinv[:, v % 4:v % 4 + 1], rsum[:, v % 4:v % 4 + 1]))
                    st.wait()
                    nc.vector.tensor_scalar(prob[:, v % 2, lo:768], prob[:, v % 2, lo:768], rinv[:, v % 4:v % 4 + 1], None,
                                            ALU.mult).then_inc(normed, 1)

        @ph.block.scalar
        def _(act):
            def keep(u):
                g, i, q = units[u]
                _, hh, qs, keys = groups[g]
                act.wait_ge(turned, u + 1)
                if g >= 2:
                    act.wait_ge(summed, g - 1)
                nc.scalar.activation(pT[:, g % 2, keys[0]:NT, i * P:(i + 1) * P],
                                     c.psum[:, 2048 + keys[0] * P:2048 + 768].rearrange("p (k q) -> p k q", q=P),
                                     ACT.Copy).then_inc(kept, 1)

            def keep_y(pr):
                pair, _, qs, _ = groups[2 * pr]
                w, q0 = len(qs) * P, qs[0] * P
                act.wait_ge(summed, 2 * pr + 2)
                nc.scalar.activation(yT[:, pair, q0:q0 + w], c.bank(6 + pr % 2, w), ACT.Copy).then_inc(y_kept, 1)

            pairs_done = 0
            for u in range(len(units) + 3):
                if u < len(units):
                    lo = groups[units[u][0]][3][0] * P
                    act.wait_ge(maxed, u + 1)
                    if u >= 2:
                        act.wait_ge(turned, u - 1)
                    nc.scalar.activation(prob[:, u % 2, lo:768], c.psum[:, (u % 2) * 1024 + lo:(u % 2) * 1024 + 768], ACT.Exp,
                                         bias=nmax[:, u % 4:u % 4 + 1], accum_out=rsum[:, u % 4:u % 4 + 1]).then_inc(exped, 1)
                if 1 <= u <= len(units):
                    keep(u - 1)
                if u >= 3 and (u - 3) in last_unit and last_unit.index(u - 3) % 2 == 1:
                    keep_y(pairs_done)
                    pairs_done += 1


def dwconv(c, st, u, src, streams, w0, w2, done):
    nc = c.nc
    for a, n in streams:
        st.do(nc.vector.scalar_tensor_tensor(out=u[:, a + 1:a + n], in0=src[:, a:a + n - 1], scalar=w0,
                                             in1=u[:, a + 1:a + n], op0=ALU.mult, op1=ALU.add))
    st.wait()
    for i, (a, n) in enumerate(streams):
        ins = nc.vector.scalar_tensor_tensor(out=u[:, a:a + n - 1], in0=src[:, a + 1:a + n], scalar=w2,
                                             in1=u[:, a:a + n - 1], op0=ALU.mult, op1=ALU.add)
        if i < len(streams) - 1:
            st.do(ins)
    ins.then_inc(done, 1)


def feature_job(c, w, bank, width, kt, rhs):
    nc = c.nc
    for lo, hi in ((0, 512), (512, width)):
        if hi <= lo:
            continue
        for k in range(kt):
            last = nc.tensor.matmul(c.psum[:, bank * 512 + lo:bank * 512 + hi], w[:, k], rhs[:, k, lo:hi],
                                    start=(k == 0), stop=(k == kt - 1))
    return last


def phase_conv_branches(c, layer, full):
    nc, io = c.nc, c.io
    width = T_ALL if full else L_LAT
    streams = [(0, L_LAT), (L_LAT, L_CTX)][:2 if full else 1]
    nt = width // P
    ysc = c.at(92, KB_BR, T_ALL)
    x2T = c.at(140, KB_BR, T_ALL)
    vN, x1N = c.at(116, NT, W_BR), c.at(128, NT, W_BR)
    cgs, cx, yc = c.at(152, 2, T_ALL), c.at(158, 2, T_ALL), c.at(164, 2, T_ALL)
    uu = c.at(170, 2, T_ALL)
    jobs = []
    for j in range(KB_BR):
        jobs += [("cg", j, B_SC + KB_BR + j), ("xs", j, B_SC + 2 * KB_BR + j), ("bg", j, B_SC + j)]
    for j in range(KB_BR):
        jobs += [(q, j, B_HY + q * KB_BR + j) for q in range(3)]
    H0 = 3 * KB_BR
    turns = [n for n, x in enumerate(jobs) if x[0] in (0, 1)]
    acts = [sum(x[0] != "bg" for x in jobs[:n + 1]) for n in range(len(jobs))]
    SLOTS = 3
    TB = 3072
    with Phase(nc) as ph:
        w_landed = [ph.sem(f"w_landed{s}") for s in range(RING)]
        proj, a_done, cx_ready, sc_done, conv_done, turned, kept, steps = (ph.sem(s) for s in (
            "projected", "act_done", "cx_ready", "sc_done", "conv_done", "transposed", "turned_kept", "dve_steps"))

        def cols(base, tap, tile, tiles):
            i = base + tap * tiles + tile
            return c.cols[:, i:i + 1]

        def psum_read(n):
            kind, j, _ = jobs[n]
            return {"cg": (a_done, acts[n]), "xs": (cx_ready, j + 1), "bg": (sc_done, j + 1)}.get(
                kind, (conv_done, n - H0 + 1))

        def slot(n):
            return c.psum[:, (n % SLOTS) * 1024:(n % SLOTS) * 1024 + width]

        @ph.block.sync
        def _(sp):
            for n, (_, _, b) in enumerate(jobs):
                if n >= RING:
                    sp.wait_ge(proj, n - RING + 1)
                sp.dma_start(c.wring[:, n % RING], io["w_in"][layer][b]).then_inc(w_landed[n % RING], 16)

        @ph.block.tensor
        def _(pe):
            def turn(m):
                pe.wait_ge(conv_done, turns[m] - H0 + 1)
                if m >= 1:
                    pe.wait_ge(kept, m)
                for t in range(nt):
                    last = nc.tensor.transpose(c.psum[:, TB + t * P:TB + (t + 1) * P], uu[:, m % 2, t * P:(t + 1) * P], c.ident[:])
                last.then_inc(turned, 1)

            m = 0
            for n in range(len(jobs)):
                pe.wait_ge(w_landed[n % RING], 16 * (n // RING + 1))
                if n >= SLOTS:
                    pe.wait_ge(*psum_read(n - SLOTS))
                feature_job(c, c.wring[:, n % RING], 2 * (n % SLOTS), width, KD, c.hT).then_inc(proj, 1)
                while m < len(turns) and turns[m] <= n - 2:
                    turn(m)
                    m += 1
            while m < len(turns):
                turn(m)
                m += 1

        @ph.block.scalar
        def _(act):
            def keep(m):
                kind, j, _ = jobs[turns[m]]
                act.wait_ge(turned, m + 1)
                nc.scalar.activation((vN if kind == 0 else x1N)[:, 0:nt, j * P:(j + 1) * P],
                                     c.psum[:, TB:TB + nt * P].rearrange("p (t q) -> p t q", q=P), ACT.Copy).then_inc(kept, 1)

            m = 0
            for n, (kind, j, b) in enumerate(jobs):
                if kind == "cg":
                    act.wait_ge(proj, n + 1)
                    if j >= 2:
                        act.wait_ge(cx_ready, j - 1)
                    nc.scalar.activation(cgs[:, j % 2, 0:width], slot(n), ACT.Copy).then_inc(a_done, 1)
                elif kind == "xs":
                    act.wait_ge(cx_ready, j + 1)
                    if j >= 2:
                        act.wait_ge(sc_done, j - 1)
                    nc.scalar.activation(yc[:, j % 2, 0:width], cx[:, j % 2, 0:width], ACT.Copy,
                                         scale=cols(C_SCW, 1, j, KB_BR)).then_inc(a_done, 1)
                elif kind != "bg":
                    act.wait_ge(proj, n + 1)
                    out = x2T[:, j, 0:width]
                    if kind < 2:
                        i = turns.index(n)
                        out = uu[:, i % 2, 0:width]
                        if i >= 2:
                            act.wait_ge(turned, i - 1)
                    i = kind * KB_BR + j
                    nc.scalar.activation(out, slot(n), ACT.Identity, scale=cols(C_HYW, 1, i, 3 * KB_BR),
                                         bias=c.cols[:, C_HYB + i:C_HYB + i + 1]).then_inc(a_done, 1)
                while m < len(turns) and turns[m] <= n - 2:
                    keep(m)
                    m += 1
            while m < len(turns):
                keep(m)
                m += 1

        @ph.block.vector
        def _(dve):
            st = Steps(dve, steps)
            for n, (kind, j, b) in enumerate(jobs):
                if kind == "xs":
                    dve.wait_ge(proj, n + 1)
                    dve.wait_ge(a_done, acts[n - 1])
                    nc.vector.tensor_tensor(cx[:, j % 2, 0:width], cgs[:, j % 2, 0:width], slot(n), ALU.mult).then_inc(cx_ready, 1)
                    dve.wait_ge(cx_ready, j + 1)
                    dve.wait_ge(a_done, acts[n])
                    dwconv(c, st, yc[:, j % 2], cx[:, j % 2], streams, cols(C_SCW, 0, j, KB_BR), cols(C_SCW, 2, j, KB_BR), steps)
                    st.n += 1
                elif kind == "bg":
                    dve.wait_ge(proj, n + 1)
                    st.wait()
                    nc.vector.tensor_tensor(ysc[:, j, 0:width], yc[:, j % 2, 0:width], slot(n), ALU.mult).then_inc(sc_done, 1)
                elif kind != "cg":
                    out = x2T[:, j] if kind == 2 else uu[:, turns.index(n) % 2]
                    i = kind * KB_BR + j
                    dve.wait_ge(a_done, acts[n])
                    dwconv(c, st, out, slot(n), streams, cols(C_HYW, 0, i, 3 * KB_BR), cols(C_HYW, 2, i, 3 * KB_BR), conv_done)


def phase_filter_mlp(c, layer, length):
    nc, io = c.nc, c.io
    z, h1, h2 = c.at(194, length), c.at(196, length), c.at(186, length)
    a, r = c.at(198, length), c.at(192, length)
    w1, w2 = c.at(200, FH), c.at(200.25, FH)
    with Phase(nc) as ph:
        landed, mm, reduced, sined, steps = (ph.sem(s) for s in ("landed", "products", "reduced", "sines", "dve_steps"))

        @ph.block.sync
        def _(sp):
            sp.dma_start(z[0:EMB, :], io[f"feat{length}"]).then_inc(landed, 16)
            sp.dma_start(w1[0:EMB, :], io["hy_w1"][layer]).then_inc(landed, 16)
            sp.dma_start(w2[0:FH, :], io["hy_w2"][layer]).then_inc(landed, 16)

        @ph.block.tensor
        def _(pe):
            pe.wait_ge(landed, 48)
            nc.tensor.matmul(c.bank(0, length, FH), w1[0:EMB, :], z[0:EMB, :], start=True, stop=True).then_inc(mm, 1)
            pe.wait_ge(sined, 1)
            nc.tensor.matmul(c.bank(1, length, FH), w2[0:FH, :], h1[0:FH, :], start=True, stop=True).then_inc(mm, 1)

        @ph.block.scalar
        def _(act):
            for i, h in enumerate((h1, h2)):
                act.wait_ge(reduced, i + 1)
                nc.scalar.activation(h[0:FH, :], r[0:FH, :], ACT.Sin).then_inc(sined, 1)

        @ph.block.vector
        def _(dve):
            st = Steps(dve, steps)
            for i in range(2):
                b, f = C_FIL + 2 * i, C_FIL + 2 * i + 1
                dve.wait_ge(mm, i + 1)
                if i:
                    dve.wait_ge(sined, 1)
                st.do(nc.vector.tensor_scalar(a[0:FH, :], c.bank(i, length, FH), c.cols[0:FH, b:b + 1], c.cols[0:FH, f:f + 1],
                                              ALU.add, ALU.mult))
                st.wait()
                st.do(nc.vector.tensor_scalar(r[0:FH, :], a[0:FH, :], 1.0 / TWO_PI, ROUND, ALU.mult, ALU.add))
                st.wait()
                st.do(nc.vector.tensor_scalar(r[0:FH, :], r[0:FH, :], ROUND, None, ALU.subtract))
                st.wait()
                for part in (PI_HI, PI_MID, PI_LO):
                    st.do(nc.vector.scalar_tensor_tensor(out=a[0:FH, :], in0=r[0:FH, :], scalar=-part, in1=a[0:FH, :],
                                                         op0=ALU.mult, op1=ALU.add))
                    st.wait()
                nc.vector.tensor_scalar(r[0:FH, :], a[0:FH, :], PI_F32, -PI_F32, ALU.min, ALU.max).then_inc(reduced, 1)


def dft_views(c, length):
    nt = length // P
    at, out = 48, {}
    for name, w in (("cos", length), ("fwd", length), ("inv", length), ("sin0", P), ("cos_b", P)):
        out[name] = c.at(at, nt, w)
        at += nt * w / 256
    out["all"] = c.at(48, int((at - 48) * 256))
    return out


def spectrum_views(c, nt):
    return c.at(152, nt, W_BR), c.at(160, nt, W_BR), c.at(168, W_BR)


def spectrum_jobs(nt):
    return [(w, f) for f in range(nt) for w in ("re", "im")] + [("re_b", 0)]


def phase_spectrum(c, layer, length, order):
    nc, io = c.nc, c.io
    nt = length // P
    which = 0 if length == L_LAT else 1
    tab = dft_views(c, length)
    h2 = c.at(186, length)
    w3, absdec, win = c.at(76, 2 * W_BR), c.at(190, W_BR), c.at(188, W_BR)
    rnorm, bias, ab = c.at(192, W_BR), c.at(194, W_BR), c.at(196, 2 * W_BR)
    hw = c.at(170, nt, 2 * W_BR)
    kre, kim, kre_b = spectrum_views(c, nt)
    jobs = spectrum_jobs(nt)
    with Phase(nc) as ph:
        tab_in, w3_in, dec_in, bias_in, made, abs_d, win_d, hw_d, ab_d, normed, steps, folded, sums, kept = (ph.sem(s) for s in (
            "tables_landed", "w3_landed", "decay_landed", "bias_landed", "filter_made", "decay_abs", "window_done",
            "windowed", "abs_done", "norm_summed", "dve_steps", "folded", "spectrum_summed", "spectrum_kept"))

        @ph.block.sync
        def _(sp):
            sp.dma_start(w3[0:FH, :], io["hy_w3"][layer][:, order * 2 * W_BR:(order + 1) * 2 * W_BR]).then_inc(w3_in, 16)
            sp.dma_start(absdec, io["hy_decay"][layer][order:order + 1].to_broadcast([P, W_BR])).then_inc(dec_in, 16)
            sp.dma_start(bias[0:1, :], io["hy_bias"][layer][order:order + 1]).then_inc(bias_in, 16)
            if order == 0:
                sp.dma_start(tab["all"], io[f"dft{length}"]).then_inc(tab_in, 16)

        @ph.block.tensor
        def _(pe):
            def norm(t):
                pe.wait_ge(ab_d, t + 1)
                for d in range(2):
                    last = nc.tensor.matmul(c.bank(4), c.ones[:], ab[:, d * W_BR:(d + 1) * W_BR],
                                            start=(t == 0 and d == 0), stop=(t == nt - 1 and d == 1))
                last.then_inc(normed, 1)

            pe.wait_ge(w3_in, 16)
            for t in range(nt):
                if t >= 2:
                    pe.wait_ge(hw_d, t - 1)
                for d in range(2):
                    last = nc.tensor.matmul(c.bank(2 * (t % 2) + d), h2[0:FH, t * P:(t + 1) * P], w3[0:FH, d * W_BR:(d + 1) * W_BR],
                                            start=True, stop=True)
                last.then_inc(made, 1)
                if t >= 1:
                    norm(t - 1)
            norm(nt - 1)
            if order == 0:
                pe.wait_ge(tab_in, 16)
            pe.wait_ge(folded, nt)
            for n, (what, ft) in enumerate(jobs):
                if n >= 4:
                    pe.wait_ge(kept, n - 3)
                src = 1 if what == "im" else 0
                table = {"re": tab["cos"], "im": tab["fwd"] if ft else tab["sin0"], "re_b": tab["cos_b"]}[what]
                for t in range(nt):
                    last = nc.tensor.matmul(c.bank(n % 4), table[:, t, ft * P:(ft + 1) * P],
                                            hw[:, t, src * W_BR:(src + 1) * W_BR], start=(t == 0), stop=(t == nt - 1))
                last.then_inc(sums, 1)

        @ph.block.scalar
        def _(act):
            act.wait_ge(dec_in, 16)
            nc.scalar.activation(absdec, absdec, ACT.Abs).then_inc(abs_d, 1)
            act.wait_ge(abs_d, 1)
            for t in range(nt):
                if t >= 1:
                    act.wait_ge(hw_d, t)
                nc.scalar.activation(win, absdec, ACT.Exp, scale=c.consts[:, 4 * which + t:4 * which + t + 1]).then_inc(win_d, 1)
                act.wait_ge(hw_d, t + 1)
                if t >= 1:
                    act.wait_ge(normed, t)
                nc.scalar.activation(ab, hw[:, t], ACT.Abs).then_inc(ab_d, 1)

        @ph.block.vector
        def _(dve):
            st = Steps(dve, steps)
            for t in range(nt):
                dve.wait_ge(made, t + 1)
                dve.wait_ge(win_d, t + 1)
                nc.vector.tensor_tensor(hw[:, t].rearrange("p (d n) -> p d n", d=2),
                                        c.psum[:, (t % 2) * 1024:(t % 2) * 1024 + 1024].rearrange("p (d n) -> p d n", d=2),
                                        win.unsqueeze(1).to_broadcast([P, 2, W_BR]), ALU.mult).then_inc(hw_d, 1)
            dve.wait_ge(normed, nt)
            dve.wait_ge(bias_in, 16)
            st.do(nc.vector.reciprocal(rnorm, c.bank(4)))
            st.do(nc.vector.tensor_tensor(hw[0:1, 0, W_BR:2 * W_BR], c.bank(4, 512, 1), bias[0:1, :], ALU.mult))
            st.wait()
            for t in range(nt):
                st.do(nc.vector.tensor_tensor(hw[:, t, 0:W_BR], hw[:, t, 0:W_BR], hw[:, t, W_BR:2 * W_BR], ALU.add))
                st.wait()
                nc.vector.scalar_tensor_tensor(out=hw[:, t, W_BR:2 * W_BR], in0=hw[:, t, W_BR:2 * W_BR], scalar=-2.0,
                                               in1=hw[:, t, 0:W_BR], op0=ALU.mult, op1=ALU.add).then_inc(folded, 1)
            for n, (what, ft) in enumerate(jobs):
                dst = kre_b if what == "re_b" else (kre if what == "re" else kim)[:, ft]
                wf = c.consts[:, 8 + which:9 + which] if ft == 0 else 1.0 / length
                dve.wait_ge(sums, n + 1)
                nc.vector.scalar_tensor_tensor(out=dst, in0=c.bank(n % 4), scalar=wf, in1=rnorm,
                                               op0=ALU.mult, op1=ALU.mult).then_inc(kept, 1)


def phase_long_conv(c, length, order):
    nc = c.nc
    nt = length // P
    t0 = 0 if length == L_LAT else NT_LAT
    tab = dft_views(c, length)
    kre, kim, kre_b = spectrum_views(c, nt)
    vN, x1N, x2T = c.at(116, NT, W_BR), c.at(128, NT, W_BR), c.at(140, KB_BR, T_ALL)
    yhy = c.at(104, KB_BR, T_ALL)
    yre, yim = c.at(170, nt, W_BR), c.at(178, nt, W_BR)
    tmp = c.at(188, 4, W_BR)
    with Phase(nc) as ph:
        spec, read, prod, steps, back, kept = (ph.sem(s) for s in (
            "spectrum_ready", "spectrum_read", "product_ready", "dve_steps", "back_summed", "back_kept"))

        @ph.block.tensor
        def _(pe):
            for f in range(nt):
                if f >= 2:
                    pe.wait_ge(read, f - 1)
                for i, table in enumerate((tab["cos"], tab["fwd"])):
                    for t in range(nt):
                        last = nc.tensor.matmul(c.bank(2 * (f % 2) + i), table[:, t, f * P:(f + 1) * P], vN[:, t0 + t],
                                                start=(t == 0), stop=(t == nt - 1))
                last.then_inc(spec, 1)
            pe.wait_ge(prod, nt)
            for n in range(nt if order == 0 else KB_BR):
                out = c.bank(4 + n % 4, W_BR if order == 0 else length)
                for i, (y, table) in enumerate(((yre, tab["cos"]), (yim, tab["inv"]))):
                    for f in range(nt):
                        if order == 0:
                            a, b = table[:, f, n * P:(n + 1) * P], y[:, f]
                        else:
                            a, b = y[:, f, n * P:(n + 1) * P], table[:, f, :]
                        last = nc.tensor.matmul(out, a, b, start=(i == 0 and f == 0), stop=(i == 1 and f == nt - 1))
                last.then_inc(back, 1)

        @ph.block.vector
        def _(dve):
            st = Steps(dve, steps)
            for f in range(nt):
                ure, uim = c.bank(2 * (f % 2)), c.bank(2 * (f % 2) + 1)
                dve.wait_ge(spec, f + 1)
                if f:
                    dve.wait_ge(prod, f)
                st.do(nc.vector.tensor_tensor(tmp[:, 0], ure, kre[:, f], ALU.mult))
                st.do(nc.vector.tensor_tensor(tmp[:, 1], uim, kim[:, f], ALU.mult))
                st.do(nc.vector.tensor_tensor(tmp[:, 2], ure, kim[:, f], ALU.mult))
                nc.vector.tensor_tensor(tmp[:, 3], uim, kre[:, f] if f else kre_b, ALU.mult).then_inc(read, 1)
                st.wait()
                st.do(nc.vector.tensor_tensor(yre[:, f], tmp[:, 0], tmp[:, 1], ALU.subtract))
                dve.wait_ge(read, f + 1)
                nc.vector.tensor_tensor(yim[:, f], tmp[:, 2], tmp[:, 3], ALU.add).then_inc(prod, 1)
            for n in range(nt if order == 0 else KB_BR):
                dve.wait_ge(back, n + 1)
                if order == 0:
                    nc.vector.tensor_tensor(vN[:, t0 + n], c.bank(4 + n % 4), x1N[:, t0 + n], ALU.mult).then_inc(kept, 1)
                else:
                    lo = t0 * P
                    nc.vector.tensor_tensor(yhy[:, n, lo:lo + length], c.bank(4 + n % 4, length), x2T[:, n, lo:lo + length],
                                            ALU.mult).then_inc(kept, 1)


def phase_rows(c, wanted):
    nc = c.nc
    diag = c.at(197, 4, P)
    n_all = len(wanted) * KD
    with Phase(nc) as ph:
        made, spread, kept = (ph.sem(s) for s in ("diagonals_made", "rows_spread", "rows_kept"))

        @ph.block.vector
        def _(dve):
            for n in range(n_all):
                if n >= 4:
                    dve.wait_ge(spread, n - 3)
                nc.vector.tensor_scalar(diag[:, n % 4], c.ident[:], wanted[n // KD][0](n % KD), None, ALU.mult).then_inc(made, 1)

        @ph.block.tensor
        def _(pe):
            for n in range(n_all):
                w = n // KD
                pe.wait_ge(made, n + 1)
                if n % KD == 0 and w >= 4:
                    pe.wait_ge(kept, w - 3)
                at = (w % 4) * 1024 + (n % KD) * P
                nc.tensor.matmul(c.psum[:, at:at + P], c.ones[:], diag[:, n % 4], start=True, stop=True).then_inc(spread, 1)

        @ph.block.scalar
        def _(act):
            for w, (_, dst) in enumerate(wanted):
                act.wait_ge(spread, (w + 1) * KD)
                nc.scalar.activation(dst, c.psum[:, (w % 4) * 1024:(w % 4 + 1) * 1024], ACT.Copy).then_inc(kept, 1)


def phase_merge(c, layer, full):
    nc, io = c.nc, c.io
    width = T_ALL if full else L_LAT
    ys = [c.at(80, KB_BR, T_ALL), c.at(92, KB_BR, T_ALL), c.at(104, KB_BR, T_ALL)]
    mT = c.at(116, KD, T_ALL)
    sig, tmp = c.at(140, 2, T_ALL), c.at(146, 2, T_ALL)
    n_all = 2 * 3 * KD
    SLOTS = 4
    with Phase(nc) as ph:
        w_landed = [ph.sem(f"w_landed{s}") for s in range(RING)]
        proj, sig_d, gated, steps = (ph.sem(s) for s in ("projected", "sigmoid_done", "gated", "dve_steps"))

        @ph.block.sync
        def _(sp):
            for n in range(n_all):
                i, br, is_y = n // 6, n // 2 % 3, n % 2
                if n >= RING:
                    sp.wait_ge(proj, n - RING + 1)
                if is_y:
                    sp.dma_start(c.wring[:, n % RING, 0:KB_BR], io["w_br"][layer][br * KD + i]).then_inc(w_landed[n % RING], 16)
                else:
                    sp.dma_start(c.wring[:, n % RING], io["w_in"][layer][B_GATE + br * KD + i]).then_inc(w_landed[n % RING], 16)

        @ph.block.tensor
        def _(pe):
            for n in range(n_all):
                br, is_y = n // 2 % 3, n % 2
                pe.wait_ge(w_landed[n % RING], 16 * (n // RING + 1))
                if n >= SLOTS:
                    pe.wait_ge(gated if is_y else sig_d, (n - SLOTS) // 2 + 1)
                feature_job(c, c.wring[:, n % RING], 2 * (n % SLOTS), width, KB_BR if is_y else KD,
                            ys[br] if is_y else c.hT).then_inc(proj, 1)

        def slot(n):
            return c.psum[:, (n % SLOTS) * 1024:(n % SLOTS) * 1024 + width]

        @ph.block.scalar
        def _(act):
            for g in range(n_all // 2):
                act.wait_ge(proj, 2 * g + 1)
                if g >= 2:
                    act.wait_ge(gated, g - 1)
                nc.scalar.activation(sig[:, g % 2, 0:width], slot(2 * g), ACT.Sigmoid).then_inc(sig_d, 1)

        @ph.block.vector
        def _(dve):
            st = Steps(dve, steps)
            for g in range(n_all // 2):
                i, br = g // 3, g % 3
                dve.wait_ge(proj, 2 * g + 2)
                dve.wait_ge(sig_d, g + 1)
                if br and g >= 2:
                    st.wait()
                dst = tmp[:, g % 2, 0:width] if br else mT[:, i, 0:width]
                nc.vector.tensor_tensor(dst, sig[:, g % 2, 0:width], slot(2 * g + 1), ALU.mult).then_inc(gated, 1)
                if br:
                    dve.wait_ge(gated, g + 1)
                    st.do(nc.vector.tensor_tensor(mT[:, i, 0:width], mT[:, i, 0:width], dst, ALU.add))


def phase_out(c, layer, full):
    nc, io = c.nc, c.io
    mT = c.at(116, KD, T_ALL)
    rows = [c.at(160, D), c.at(164, D)]
    tmp = c.at(152, 2, D)
    nt = NT if full else NT_LAT
    with Phase(nc) as ph:
        w_landed, proj, scaled, steps = (ph.sem(s) for s in ("w_landed", "projected", "scaled", "dve_steps"))

        @ph.block.sync
        def _(sp):
            for h in range(2):
                sp.dma_start(c.wring[:, 4 * h:4 * h + 4].rearrange("p b k n -> p b (k n)"),
                             io["w_out"][layer][4 * h:4 * h + 4].rearrange("b p k n -> p b (k n)")).then_inc(w_landed, 16)

        @ph.block.tensor
        def _(pe):
            pe.wait_ge(w_landed, 32)
            for t in range(nt):
                if t >= 4:
                    pe.wait_ge(scaled, t - 3)
                for h in range(2):
                    for k in range(KD):
                        last = nc.tensor.matmul(c.bank(2 * (t % 4) + h), mT[:, k, t * P:(t + 1) * P],
                                                c.wring[:, 4 * h:4 * h + 4, k, :], start=(k == 0), stop=(k == KD - 1))
                last.then_inc(proj, 1)

        @ph.block.vector
        def _(dve):
            st = Steps(dve, steps)
            for t in range(nt):
                dve.wait_ge(proj, t + 1)
                if t >= 2:
                    st.wait()
                nc.vector.tensor_tensor(tmp[:, t % 2], c.psum[:, (t % 4) * 1024:(t % 4 + 1) * 1024],
                                        rows[0 if t < NT_LAT else 1], ALU.mult).then_inc(scaled, 1)
                dve.wait_ge(scaled, t + 1)
                st.do(nc.vector.tensor_tensor(c.xs[:, t], c.xs[:, t], tmp[:, t % 2], ALU.add))


def phase_norm2(c, full):
    nc = c.nc
    tiles = list(range(NT if full else NT_LAT))
    h2N = c.at(80, NT, D)
    rows_a, rows_b = [c.at(136, D), c.at(144, D)], [c.at(140, D), c.at(148, D)]
    with Phase(nc) as ph:
        sq, ms, root, steps = norm_sems(ph)
        ready, turned, kept = (ph.sem(s) for s in ("h2_ready", "transposed", "turned_kept"))

        @ph.block.scalar
        def _(act):
            act_norm(c, act, tiles, sq, ms, root)
            for t in tiles:
                act.wait_ge(turned, t + 1)
                nc.scalar.activation(c.hT[:, :, t * P:(t + 1) * P],
                                     c.psum[:, (t % 4) * 1024:(t % 4 + 1) * 1024].rearrange("p (k q) -> p k q", q=P),
                                     ACT.Copy).then_inc(kept, 1)

        @ph.block.vector
        def _(dve):
            st = Steps(dve, steps)
            dve_norm(c, dve, st, tiles, sq, ms, root)
            for t in tiles:
                s = 0 if t < NT_LAT else 1
                st.do(nc.vector.scalar_tensor_tensor(out=h2N[:, t], in0=c.xs[:, t], scalar=c.stat[:, 0, t:t + 1], in1=rows_a[s],
                                                     op0=ALU.mult, op1=ALU.mult))
                st.wait()
                nc.vector.tensor_tensor(h2N[:, t], h2N[:, t], rows_b[s], ALU.add).then_inc(ready, 1)

        @ph.block.tensor
        def _(pe):
            for t in tiles:
                pe.wait_ge(ready, t + 1)
                if t >= 4:
                    pe.wait_ge(kept, t - 3)
                for k in range(KD):
                    last = nc.tensor.transpose(c.psum[:, (t % 4) * 1024 + k * P:(t % 4) * 1024 + (k + 1) * P],
                                               h2N[:, t, k * P:(k + 1) * P], c.ident[:])
                last.then_inc(turned, 1)


def phase_query(c, layer, full):
    nc, io = c.nc, c.io
    width = T_ALL if full else L_LAT
    nt = width // P
    qT = c.at(104, PH, T_ALL)
    keys = c.at(185, PH, 2 * NK)
    scores = c.at(136, NT * PH + 1, 2 * NK)
    units = [(t, h) for t in range(nt) for h in range(PH)]
    with Phase(nc) as ph:
        w_in, keys_in, proj, kept, scored, score_kept, pad = (ph.sem(s) for s in (
            "w_landed", "keys_landed", "projected", "query_kept", "scored", "scores_kept", "pad_set"))

        @ph.block.sync
        def _(sp):
            for h in range(2):
                sp.dma_start(c.wring[:, 4 * h:4 * h + 4].rearrange("p b k n -> p b (k n)"),
                             io["wq"][layer][4 * h:4 * h + 4].rearrange("b p k n -> p b (k n)")).then_inc(w_in, 16)
            sp.dma_start(keys, io["keys"][layer]).then_inc(keys_in, 16)

        @ph.block.gpsimd
        def _(pool):
            nc.gpsimd.memset(scores[:, len(units)], 0.0).then_inc(pad, 1)

        @ph.block.tensor
        def _(pe):
            pe.wait_ge(w_in, 32)
            for h in range(PH):
                if h >= 2:
                    pe.wait_ge(kept, h - 1)
                feature_job(c, c.wring[:, h], 2 * (h % 2), width, KD, c.hT).then_inc(proj, 1)
            pe.wait_ge(keys_in, 16)
            pe.wait_ge(kept, PH)
            for u, (t, h) in enumerate(units):
                if u >= 8:
                    pe.wait_ge(score_kept, u // 2 - 3)
                at = 2048 + (u % 8) * 256
                nc.tensor.matmul(c.psum[:, at:at + 256], qT[:, h, t * P:(t + 1) * P], keys[:, h, :],
                                 start=True, stop=True).then_inc(scored, 1)

        @ph.block.scalar
        def _(act):
            for h in range(PH):
                act.wait_ge(proj, h + 1)
                nc.scalar.activation(qT[:, h, 0:width], c.psum[:, (h % 2) * 1024:(h % 2) * 1024 + width],
                                     ACT.Copy).then_inc(kept, 1)
            for u in range(0, len(units), 2):
                at = 2048 + (u % 8) * 256
                act.wait_ge(scored, u + 2)
                nc.scalar.activation(scores[:, u:u + 2], c.psum[:, at:at + 512].rearrange("p (u n) -> p u n", u=2),
                                     ACT.Copy).then_inc(score_kept, 1)


def phase_experts(c, layer, full):
    nc, io = c.nc, c.io
    nt = NT if full else NT_LAT
    h2N = c.at(80, NT, D)
    gate2 = c.at(128, 2, D)
    scores = c.at(136, NT * PH + 1, 2 * NK)
    slots = [c.at(24 + 8 * i, 2 * D) for i in range(7)] + [c.at(104, 2 * D)]
    junk = c.at(112, 2, D)
    dots, gelus, probs, exps = (c.at(120 + 0.25 * i, 2, TOPK) for i in range(4))
    diag = c.at(121, 4, P)
    top1, top2, topc, e1, e2, iota = (c.at(123 + 0.125 * i, TOPK) for i in range(6))
    idx1, idx2, idxc, hi, lo = (c.at(124 + 0.125 * i, TOPK).bitcast(U32) for i in range(5))
    small = c.at(124.75, 2, 8)
    eidx = c.at(125, 2, TOPK).bitcast(U32)
    sc, cut = c.at(126, 2 * NK), c.at(127, 2 * NK)
    cand, cand_cut, hot1, hot2 = (c.at(185 + i, TOPK, TOPK) for i in range(4))
    upd = c.at(189, D)
    LOWEST = -3.0e38
    table = io["uv"][layer]
    with Phase(nc) as ph:
        landed = [ph.sem(f"slot_landed{s}") for s in range(RING)]
        (iota_d, idx_ready, slot_used, turn, dotted, gelued, diag_ready, psum_used, x_added, exp_ready, exp_done,
         steps, order) = (ph.sem(s) for s in (
             "iota_made", "indices_ready", "slot_used", "turn", "dot_ready", "gelu_done", "diagonal_ready",
             "sum_taken", "x_added", "topk_ready", "exp_done", "dve_steps", "order"))

        @ph.block.gpsimd
        def _(pool):
            nc.gpsimd.iota(iota, pattern=[[1, TOPK]], base=0, channel_multiplier=0,
                           allow_small_or_imprecise_dtypes=True).then_inc(iota_d, 1)
            with pool.Fori(0, nt) as t:
                with pool.Fori(0, PH // 2) as i:
                    for p in range(2):
                        n = t * PH + i * 2 + p
                        pool.wait_ge(idx_ready, n + 1)
                        pool.sem_inc(turn, 1)
                        for k in range(TOPK):
                            pool.wait_ge(slot_used, n * TOPK + (k + 1))
                            pool.sem_inc(turn, 1)
                            nc.gpsimd.indirect_dma_start(
                                out=slots[k % RING], out_offset=None, in_=table,
                                in_offset=bass.IndirectOffsetOnAxis(ap=eidx[:, p, k:k + 1], axis=0)
                            ).then_inc(landed[k % RING], 16)

        @ph.block.tensor
        def _(pe):
            pe.sem_inc(slot_used, RING)
            with pe.Fori(0, nt) as t:
                with pe.Fori(0, PH // 2) as i:
                    for p in range(2):
                        n = t * PH + i * 2 + p
                        pe.wait_ge(psum_used, n + 1)
                        for k in range(TOPK):
                            pe.wait_ge(diag_ready, n * TOPK + (k + 1))
                            for h in range(2):
                                last = nc.tensor.matmul(c.bank(2 * p + h), diag[:, k % 4],
                                                        slots[k % RING][:, D + h * 512:D + (h + 1) * 512],
                                                        start=(k == 0), stop=(k == TOPK - 1))
                            last.then_inc(slot_used, 1)

        @ph.block.scalar
        def _(act):
            def softmax_exp(n, p):
                act.wait_ge(exp_ready, n + 1)
                nc.scalar.activation(exps[:, p], topc, ACT.Exp, bias=small[:, p, 0:1], accum_out=small[:, p, 1:2]).then_inc(exp_done, 1)

            softmax_exp(0, 0)
            with act.Fori(0, nt) as t:
                with act.Fori(0, PH // 2) as i:
                    for p in range(2):
                        n = t * PH + i * 2 + p
                        for k in range(TOPK):
                            act.wait_ge(dotted, n * TOPK + (k + 1))
                            nc.scalar.activation(gelus[:, p, k:k + 1], dots[:, p, k:k + 1], ACT.Gelu).then_inc(gelued, 1)
                            if k == 12:
                                softmax_exp(n + 1, 1 - p)

        @ph.block.vector
        def _(dve):
            base, cnt = [0], [0]

            def do(ins):
                ins.then_inc(steps, 1)
                cnt[0] += 1

            def wait(apart=False):
                dve.wait_ge(steps, base[0] + cnt[0])
                if apart:
                    dve.sem_inc(order, 1)

            def top16(vals, cutv, top, idx):
                do(nc.vector.max(top[:, 0:8], vals))
                wait(True)
                do(nc.vector.max_index(idx[:, 0:8], top[:, 0:8], vals))
                do(nc.vector.match_replace(cutv, top[:, 0:8], vals, LOWEST))
                wait(True)
                do(nc.vector.max(top[:, 8:16], cutv))
                wait(True)
                do(nc.vector.max_index(idx[:, 8:16], top[:, 8:16], cutv))

            def topk_parts(n, q):
                do(nc.vector.tensor_copy(sc, scores[:, bass.ds(n, 1)].rearrange("p a n -> p (a n)")))
                wait(True)
                top16(sc[:, 0:NK], cut[:, 0:NK], top1, idx1)
                yield
                top16(sc[:, NK:], cut[:, NK:], top2, idx2)
                wait()
                yield
                grid = [P, TOPK, TOPK]
                do(nc.vector.tensor_tensor(cand, top1.unsqueeze(2).to_broadcast(grid), top2.unsqueeze(1).to_broadcast(grid), ALU.add))
                wait(True)
                top16(cand.rearrange("p a b -> p (a b)"), cand_cut.rearrange("p a b -> p (a b)"), topc, idxc)
                wait()
                nc.vector.tensor_scalar(small[:, q, 0:1], topc[:, 0:1], -1.0, None, ALU.mult).then_inc(exp_ready, 1)
                yield
                do(nc.vector.tensor_scalar(hi, idxc, 4, None, ALU.logical_shift_right))
                do(nc.vector.tensor_scalar(lo, idxc, 15, None, ALU.bitwise_and))
                wait()
                places = iota.unsqueeze(1).to_broadcast(grid)
                do(nc.vector.tensor_tensor(hot1, places, hi.unsqueeze(2).to_broadcast(grid), ALU.is_equal))
                do(nc.vector.tensor_tensor(hot2, places, lo.unsqueeze(2).to_broadcast(grid), ALU.is_equal))
                wait()
                do(nc.vector.tensor_tensor(hot1, hot1, idx1.unsqueeze(1).to_broadcast(grid), ALU.mult))
                do(nc.vector.tensor_tensor(hot2, hot2, idx2.unsqueeze(1).to_broadcast(grid), ALU.mult))
                wait()
                do(nc.vector.tensor_reduce(e1, hot1, AX.X, ALU.add))
                do(nc.vector.tensor_reduce(e2, hot2, AX.X, ALU.add))
                wait()
                nc.vector.scalar_tensor_tensor(out=eidx[:, q], in0=e1, scalar=float(NK), in1=e2, op0=ALU.mult,
                                               op1=ALU.add).then_inc(idx_ready, 1)
                yield
                dve.wait_ge(exp_done, n + 1)
                do(nc.vector.reciprocal(small[:, q, 2:3], small[:, q, 1:2]))
                wait()
                do(nc.vector.tensor_scalar(probs[:, q], exps[:, q], small[:, q, 2:3], None, ALU.mult))
                wait()

            def dot(n, t, p, k):
                if k >= 2:
                    dve.wait_ge(dotted, n * TOPK + (k - 1))
                dve.wait_ge(landed[k % RING], n * 32 + 16 * (k // RING + 1))
                nc.vector.scalar_tensor_tensor(out=junk[:, k % 2], in0=slots[k % RING][:, 0:D], scalar=1.0,
                                               in1=h2N[:, bass.ds(t, 1)].rearrange("p a n -> p (a n)"), op0=ALU.mult,
                                               op1=ALU.mult, accum_out=dots[:, p, k:k + 1]).then_inc(dotted, 1)

            def weigh(n, p, k):
                dve.wait_ge(gelued, n * TOPK + (k + 1))
                dve.wait_ge(slot_used, n * TOPK + (k + RING - 3))
                nc.vector.tensor_scalar(diag[:, k % 4], c.ident[:], gelus[:, p, k:k + 1], probs[:, p, k:k + 1], ALU.mult,
                                        ALU.mult).then_inc(diag_ready, 1)

            dve.sem_inc(psum_used, 2)
            dve.sem_inc(x_added, 1)
            dve.wait_ge(iota_d, 1)
            for _ in topk_parts(0, 0):
                pass
            per_unit = cnt[0]
            with dve.Fori(0, nt) as t:
                with dve.Fori(0, PH // 2) as i:
                    for p in range(2):
                        n = t * PH + i * 2 + p
                        base[0], cnt[0] = (n + 1) * per_unit, 0
                        parts = topk_parts(n + 1, 1 - p)
                        for k in range(TOPK):
                            dot(n, t, p, k)
                            if k >= 1:
                                weigh(n, p, k - 1)
                            if k in (3, 5, 7, 9, 14):
                                next(parts, None)
                        weigh(n, p, TOPK - 1)
                        assert cnt[0] == per_unit
                        dve.wait_ge(slot_used, n * TOPK + (TOPK + RING))
                        dve.wait_ge(x_added, n + 1)
                        nc.vector.tensor_tensor(upd, c.psum[:, 1024 * p:1024 * p + D],
                                                gate2[:, bass.ds(t // NT_LAT, 1)].rearrange("p a n -> p (a n)"),
                                                ALU.mult).then_inc(psum_used, 1)
                        dve.wait_ge(psum_used, n + 3)
                        x = c.xs[:, bass.ds(t, 1)].rearrange("p a n -> p (a n)")
                        nc.vector.tensor_tensor(x, x, upd, ALU.add).then_inc(x_added, 1)


def phase_final(c, out):
    nc, io = c.nc, c.io
    tiles = list(range(NT_LAT))
    gain, y = c.at(136, D), c.at(140, NT_LAT, D)
    with Phase(nc) as ph:
        sq, ms, root, steps = norm_sems(ph)
        gain_in, ready, stored = (ph.sem(s) for s in ("gain_landed", "rows_ready", "rows_stored"))

        @ph.block.scalar
        def _(act):
            act_norm(c, act, tiles, sq, ms, root)

        @ph.block.vector
        def _(dve):
            st = Steps(dve, steps)
            dve_norm(c, dve, st, tiles, sq, ms, root)
            dve.wait_ge(gain_in, 16)
            for t in tiles:
                nc.vector.scalar_tensor_tensor(out=y[:, t], in0=c.xs[:, t], scalar=c.stat[:, 0, t:t + 1], in1=gain,
                                               op0=ALU.mult, op1=ALU.mult).then_inc(ready, 1)

        @ph.block.sync
        def _(sp):
            sp.dma_start(gain, io["g_final"].to_broadcast([P, D])).then_inc(gain_in, 16)
            for t in tiles:
                sp.wait_ge(ready, t + 1)
                sp.dma_start(out[t * P:(t + 1) * P, :], y[:, t]).then_inc(stored, 16)
            sp.wait_ge(stored, 16 * NT_LAT)


def build(nc, io, out):
    with ExitStack() as ctx:
        c = Chip(nc, ctx, io)
        phase_load(c)
        for layer in range(DEPTH):
            full = layer < DEPTH - 1
            streams = range(2 if full else 1)
            phase_mod(c, layer)
            phase_norm1(c, list(range(NT)))
            phase_qkv(c, layer, full)
            phase_attention(c, full)
            phase_conv_branches(c, layer, full)
            for length in (L_LAT, L_CTX)[:2 if full else 1]:
                phase_filter_mlp(c, layer, length)
                for order in range(2):
                    phase_spectrum(c, layer, length, order)
                    phase_long_conv(c, length, order)
            col = lambda base, s: lambda k: c.mod[:, base + k, s:s + 1]
            phase_rows(c, [(col(GT1, s), c.at(160 + 4 * s, D)) for s in streams])
            phase_merge(c, layer, full)
            phase_out(c, layer, full)
            rows = []
            for s in streams:
                rows += [((lambda s: lambda k: c.ab[:, 1, k, s:s + 1])(s), c.at(136 + 8 * s, D)),
                         (col(SH2, s), c.at(140 + 8 * s, D)), (col(GT2, s), c.at(128 + 4 * s, D))]
            phase_rows(c, rows)
            phase_norm2(c, full)
            phase_query(c, layer, full)
            phase_experts(c, layer, full)
        phase_final(c, out)


def blocks(w):
    n_l, k, n = w.shape
    return np.ascontiguousarray(w.reshape(n_l, k // P, P, n // P, P).transpose(0, 3, 2, 1, 4))


def columns(v):
    v = v.reshape(v.shape[0], -1, P)
    return v.transpose(0, 2, 1)


def layouts(a):
    a = {k: np.asarray(v) for k, v in a.items()}
    n_l = DEPTH
    tok = lambda v: np.ascontiguousarray(v.reshape(-1, P, D).transpose(1, 0, 2))
    fil = np.zeros((n_l, P, 4), np.float32)
    for i, k in enumerate(("hy_b1", "hy_f1", "hy_b2", "hy_f2")):
        fil[:, :FH, i] = a[k]
    keys = np.zeros((n_l, 2, DK, PH, 2, NK), np.float32)
    for p in range(2):
        keys[:, p, :, :, p, :] = a["peer_subkeys"][:, :, p].transpose(0, 3, 1, 2)
    out = {
        "x": tok(a["x"]), "ctx": tok(a["ctx"]),
        "cond": np.ascontiguousarray(np.stack([a["c"].reshape(KD, P).T, a["c_ctx"].reshape(KD, P).T], axis=2)),
        "rope": rope_table().reshape(P, NT_LAT, 2, 2, 16), "consts": shape_constants(),
        "cols": np.ascontiguousarray(np.concatenate(
            [columns(a["b_mod"]), columns(a["g_norm1"]), columns(a["g_norm2"]), columns(a["sc_conv_w"]),
             columns(a["hy_conv_w"]), columns(a["hy_conv_b"]), fil], axis=2)),
        "w_mod": blocks(a["w_mod"]), "w_in": blocks(a["w_in"]), "w_out": blocks(a["w_out"]),
        "w_br": np.concatenate([blocks(a[k]) for k in ("w_br_att", "w_br_sc", "w_br_hy")], axis=1),
        "wq": blocks(a["peer_wq"]),
        "keys": keys.reshape(n_l, P, PH, 2 * NK),
        "gains": np.ascontiguousarray(np.concatenate([a["q_gain"]] * HEADS + [a["k_gain"]] * KV_HEADS, axis=1)),
        "hy_w1": a["hy_w1"], "hy_w2": a["hy_w2"], "hy_w3": a["hy_w3"],
        "hy_decay": a["hy_decay"], "hy_bias": a["hy_bias"],
        "g_final": a["g_final"].reshape(1, D),
    }
    for length in (L_LAT, L_CTX):
        out[f"feat{length}"] = filter_features(length)
        out[f"dft{length}"] = dft_tables(length)
    for layer in range(n_l):
        out[f"uv{layer}"] = np.concatenate([a["peer_u"][layer], a["peer_v"][layer]], axis=1)
    return out


def kernel(**inputs):
    import concourse.bacc as bacc
    from concourse.bass_utils import run_bass_kernel_spmd

    nc = bacc.Bacc("TRN2", target_bir_lowering=False, num_devices=1)
    arrays, io = {}, {}
    for name, a in layouts(inputs).items():
        arrays[f"in_{name}"] = a
        io[name] = nc.dram_tensor(f"in_{name}", a.shape, mybir.dt.from_np(a.dtype), kind="ExternalInput").ap()
    io["uv"] = [io.pop(f"uv{layer}") for layer in range(DEPTH)]
    out = nc.dram_tensor("out", (L_LAT, D), F32, kind="ExternalOutput").ap()
    build(nc, io, out)
    r = run_bass_kernel_spmd(nc, [arrays], core_ids=[0])
    return r.results[0]["out"].reshape(1, L_LAT, D)
```

```python
import math
from contextlib import ExitStack

import numpy as np

import concourse.bass as bass
from concourse import mybir

F32 = mybir.dt.float32
F32R = mybir.dt.float32r
U32 = mybir.dt.uint32
I32 = mybir.dt.int32
ALU = mybir.AluOpType
ACT = mybir.ActivationFunctionType
AX = mybir.AxisListType

P = 128
D = 1024
DEPTH = 2
L_LAT, L_CTX = 512, 256
T_ALL = L_LAT + L_CTX
KD = D // P
NT_LAT, NT_CTX = L_LAT // P, L_CTX // P
NT = NT_LAT + NT_CTX
GRID_W = 64
HEADS, KV_HEADS, HD = 8, 2, 64
PAIRS = HEADS // 2
W_BR = 512
KB_BR = W_BR // P
EPS = 1e-6
FH = 64
BANDS = 16
EMB = 1 + 2 * BANDS
B_Q, B_K, B_V = 0, 4, 5
B_SC, B_HY, B_GATE = 6, 18, 30
N_IN = 54
SH1, SC1, GT1, SH2, SC2, GT2 = (KD * i for i in range(6))
N_MOD = 6 * KD
PH, NK, DK, TOPK = 8, 128, 64, 16
N_EXP = NK * NK
RING = 8
C_BMOD, C_G1, C_G2 = 0, N_MOD, N_MOD + KD
C_SCW = C_G2 + KD
C_HYW = C_SCW + 3 * KB_BR
C_HYB = C_HYW + 3 * 3 * KB_BR
C_FIL = C_HYB + 3 * KB_BR
N_COLS = C_FIL + 4

TWO_PI = 2.0 * math.pi
PI_HI = 6.28125
PI_MID = float(np.float32(np.frombuffer(np.array([np.float32(TWO_PI - PI_HI)]).view(np.uint32) & np.uint32(0xFFFFF000), np.float32)[0]))
PI_LO = TWO_PI - PI_HI - PI_MID
ROUND = 1.5 * 2.0 ** 23
PI_F32 = float(np.nextafter(np.float32(math.pi), np.float32(0)))


def dft_tables(length):
    n = np.arange(length)
    ang = np.pi * ((n[:, None] * n[None, :]) % (2 * length)) / length
    cos, sin = np.cos(ang), -np.sin(ang)
    alt = (-1.0) ** n
    fwd, inv, cos_b = sin.copy(), sin.copy(), cos[:, :P].copy()
    fwd[:, 0] = alt
    inv[0, :] = alt
    cos_b[:, 0] = alt
    parts = [cos, fwd, inv, sin[:, :P], cos_b]
    rows = [a.reshape(length // P, P, -1).transpose(1, 0, 2).reshape(P, -1) for a in parts]
    return np.ascontiguousarray(np.concatenate(rows, axis=1).astype(np.float32))


def filter_features(length):
    t = np.linspace(0.0, 1.0, length, dtype=np.float32)[:, None]
    w = (2.0 * math.pi * np.arange(length, dtype=np.float32)[:, None] / length).astype(np.float32)
    bands = np.linspace(1e-4, BANDS - 1, BANDS, dtype=np.float32)[None, :]
    z = np.concatenate([t, np.cos(bands * w), -np.sin(bands * w)], axis=-1)
    return np.ascontiguousarray(z.T.astype(np.float32))


def rope_table():
    pos = np.arange(L_LAT)
    inv = np.power(np.float32(10000.0), -np.arange(0, 32, 2, dtype=np.float32) / 32)
    ang = np.stack([(pos // GRID_W)[:, None] * inv, (pos % GRID_W)[:, None] * inv], axis=1)
    t = np.stack([np.cos(ang), np.sin(ang)], axis=1).reshape(NT_LAT, P, 64)
    return np.ascontiguousarray(t.transpose(1, 0, 2).reshape(P, NT_LAT * 64).astype(np.float32))


def shape_constants():
    out = np.zeros((P, 8), np.float32)
    for a, length in ((0, L_LAT), (4, L_CTX)):
        t = np.linspace(0.0, 1.0, length, dtype=np.float32).reshape(-1, P).T
        out[:, a:a + t.shape[1]] = -t
    w = np.zeros((P, 2), np.float32)
    w[:, 0], w[:, 1] = 1.0 / L_LAT, 1.0 / L_CTX
    w[0] *= 0.5
    return np.concatenate([out, w], axis=1)


class Steps:

    def __init__(self, eng, sem):
        self.eng, self.sem, self.n = eng, sem, 0

    def do(self, ins):
        ins.then_inc(self.sem, 1)
        self.n += 1
        return self.n

    def wait(self, n=None):
        self.eng.wait_ge(self.sem, self.n if n is None else n)


class Phase:

    count = 0

    def __init__(self, nc):
        self.nc, self.sems = nc, []
        Phase.count += 1
        self.tag = f"p{Phase.count}"

    def sem(self, name):
        s = self.nc.alloc_semaphore(f"{name}_{self.tag}")
        self.sems.append(s)
        return s

    def __enter__(self):
        self.stack = ExitStack()
        self.block = self.stack.enter_context(self.nc.Block())
        return self

    def __exit__(self, *err):
        self.stack.__exit__(*err)
        if err[0] is None:
            self.nc.clear_and_free_semaphores(self.sems)
            self.nc.all_engine_barrier(sem_only=True)


class Chip:

    def __init__(self, nc, ctx, io):
        self.nc, self.io = nc, io
        self.arena_at, self.views = (nc.sbuf_base + 31) // 32 * 32, {}
        self.arena = ctx.enter_context(nc.sbuf_tensor("arena", [P, 201 * 256], F32))
        sb = lambda n, s: ctx.enter_context(nc.sbuf_tensor(n, s, F32))
        self.ident = sb("ident", [P, P])
        self.ones = sb("ones", [P, P])
        self.rope = sb("rope", [P, NT_LAT, 2, 2, 16])
        self.cond = sb("cond", [P, KD, 2])
        self.cond4 = ctx.enter_context(nc.sbuf_tensor("cond4", [P, KD, 4], F32R))
        self.cols = sb("cols", [P, N_COLS])
        self.consts = sb("consts", [P, 10])
        self.mod = sb("mod", [P, N_MOD, 2])
        self.ab = sb("ab", [P, 2, KD, 2])
        self.stat = sb("stat", [P, 2, 16])
        self.psum = ctx.enter_context(nc.psum_tensor("psum", [P, 8 * 512], F32))
        self.xs = self.at(0, NT, D)
        self.hT = self.own(24, KD, T_ALL)
        self.wring = self.at(48, RING, KD, P)
        self.hT_low = self.rounded(24, KD, T_ALL)
        self.hT_high = self.rounded(176, KD, T_ALL)

    def at(self, kib, *shape):
        n = int(np.prod(shape))
        v = self.arena[:, int(kib * 256):int(kib * 256) + n]
        return self._shaped(v, shape)

    def own(self, kib, *shape, dtype=F32):
        key = (kib, shape, dtype == F32R)
        if key not in self.views:
            self.views[key] = self.nc.alloc_sbuf_tensor_at(
                f"view{len(self.views)}_at_{int(kib)}", [P, int(np.prod(shape))], dtype,
                offset=self.arena_at + int(kib * 1024))
        return self._shaped(self.views[key][:], shape)

    def rounded(self, kib, *shape):
        return self.own(kib, *shape, dtype=F32R)

    @staticmethod
    def _shaped(v, shape):
        if len(shape) == 2:
            return v.rearrange("p (a b) -> p a b", a=shape[0])
        if len(shape) == 3:
            return v.rearrange("p (a b c) -> p a b c", a=shape[0], b=shape[1])
        return v

    def bank(self, b, width=512, parts=P):
        return self.psum[0:parts, b * 512:b * 512 + width]


def phase_load(c):
    nc, io = c.nc, c.io
    with Phase(nc) as ph:
        landed, made, made_ones, cond_in, cond_done = (ph.sem(s) for s in (
            "inputs_landed", "identity_made", "ones_made", "cond_landed", "cond_done"))

        @ph.block.sync
        def _(sp):
            sp.dma_start(c.cond[:], io["cond"]).then_inc(cond_in, 16)
            sp.dma_start(c.xs[:, 0:NT_LAT, :], io["x"]).then_inc(landed, 16)
            sp.dma_start(c.xs[:, NT_LAT:NT, :], io["ctx"]).then_inc(landed, 16)
            sp.dma_start(c.rope[:], io["rope"]).then_inc(landed, 16)
            sp.dma_start(c.consts[:], io["consts"]).then_inc(landed, 16)
            sp.wait_ge(landed, 64)

        @ph.block.gpsimd
        def _(pool):
            nc.gpsimd.memset(c.ident[:], 0.0).then_inc(made, 1)
            pool.wait_ge(made, 1)
            nc.gpsimd.affine_select(out=c.ident[:], in_=c.ident[:], compare_op=ALU.not_equal, fill=1.0,
                                    base=0, pattern=[[-1, P]], channel_multiplier=1).then_inc(made, 1)

        @ph.block.vector
        def _(dve):
            nc.vector.memset(c.ones[:], 1.0).then_inc(made_ones, 1)

        @ph.block.scalar
        def _(act):
            act.wait_ge(cond_in, 16)
            nc.scalar.activation(c.cond[:], c.cond[:], ACT.Silu).then_inc(cond_done, 1)


def split(nc, eng, hi, lo, x):
    return eng.tensor_tensor(lo, x, hi.bitcast(F32), ALU.subtract)


def products(a, b):
    return ((a[0], b[0]), (a[0], b[1]), (a[1], b[0]))


class SplitRing:

    def __init__(self, c, ph, blocks, at=48, slots=4):
        self.c, self.blocks, self.slots = c, blocks, slots
        self.raw, self.low = c.own(at, slots, KD, P), c.rounded(at, slots, KD, P)
        self.high = c.rounded(at + 4 * slots, slots, KD, P)
        self.landed = [ph.sem(f"w_landed{s}") for s in range(slots)]
        self.high_ready, self.ready = ph.sem("w_high_ready"), ph.sem("w_split")

    def load(self, sp, used):
        for n, (block, kt) in enumerate(self.blocks):
            if n >= self.slots:
                sp.wait_ge(used, n - self.slots + 1)
            sp.dma_start(self.raw[:, n % self.slots, 0:kt], block).then_inc(self.landed[n % self.slots], 16)

    def _high(self, eng, op, n):
        s, kt = n % self.slots, self.blocks[n][1]
        eng.wait_ge(self.landed[s], 16 * (n // self.slots + 1))
        op(self.high[:, s, 0:kt], self.raw[:, s, 0:kt]).then_inc(self.high_ready, 1)

    def round_ahead(self, act, done, used):
        nc = self.c.nc
        if done >= 0:
            act.wait_ge(used, done + 1)
        for n in range(self.slots) if done < 0 else (done + self.slots,):
            if n < len(self.blocks):
                self._high(act, lambda out, x: nc.scalar.activation(out, x, ACT.Copy), n)

    def split(self, pool, rounds=False):
        nc = self.c.nc
        for n, (_, kt) in enumerate(self.blocks):
            s = n % self.slots
            x, high = self.raw[:, s, 0:kt], self.high[:, s, 0:kt]
            if rounds:
                self._high(pool, nc.gpsimd.tensor_copy, n)
            pool.wait_ge(self.high_ready, n + 1)
            split(nc, nc.gpsimd, high, self.low[:, s, 0:kt], x).then_inc(self.ready, 1)

    def parts(self, n):
        return self.high[:, n % self.slots], self.low[:, n % self.slots]


def phase_mod(c, layer):
    nc, io = c.nc, c.io
    HALF = KD // 2
    RAW = 4
    chunks = 6 * D // 512
    raw = c.own(48, RAW, HALF * 512)
    hi = c.rounded(80, 2, HALF * 512)
    lo = c.rounded(96, 2, HALF * 512)
    rows = c.at(116, 2, 512)
    sel = c.at(120, 2)
    with Phase(nc) as ph:
        w_landed = [ph.sem(f"w_landed{s}") for s in range(RAW)]
        w_split, hi_ready, halves_done, kept, turned, cols_in, cond_split, dve_done = (ph.sem(s) for s in (
            "weights_split", "high_ready", "halves_done", "rows_kept", "rows_turned", "cols_landed",
            "cond_split", "dve_steps"))

        @ph.block.sync
        def _(sp):
            sp.dma_start(c.cols[:], io["cols"][layer]).then_inc(cols_in, 16)
            for n in range(2 * chunks):
                if n >= RAW:
                    sp.wait_ge(w_split, n - RAW + 1)
                sp.dma_start(raw[:, n % RAW], io["w_mod"][layer][n]).then_inc(w_landed[n % RAW], 16)

        @ph.block.scalar
        def _(act):
            def keep(q):
                act.wait_ge(halves_done, 2 * q + 2)
                if q >= 2:
                    act.wait_ge(turned, q - 1)
                nc.scalar.activation(rows[0:4, q % 2], c.bank(q % 2, 512, 4), ACT.Copy).then_inc(kept, 1)

            for n in range(2 * chunks):
                act.wait_ge(w_landed[n % RAW], 16 * (n // RAW + 1))
                if n >= 2:
                    act.wait_ge(halves_done, n - 1)
                nc.scalar.activation(hi[:, n % 2], raw[:, n % RAW], ACT.Copy).then_inc(hi_ready, 1)
                if n >= 3 and n % 2:
                    keep((n - 3) // 2)
            keep(chunks - 1)

        @ph.block.tensor
        def _(pe):
            def turn(q):
                pe.wait_ge(kept, q + 1)
                for j in range(4):
                    at = 7 * 512 + 8 * q + 2 * j
                    last = nc.tensor.matmul(c.psum[:, at:at + 2], rows[0:4, q % 2, j * P:(j + 1) * P], sel[0:4],
                                            start=True, stop=True)
                last.then_inc(turned, 1)

            pe.wait_ge(cond_split, 4)
            for n in range(2 * chunks):
                q, half = n // 2, n % 2
                if half == 0 and q >= 2:
                    pe.wait_ge(kept, q - 1)
                for part, ready in ((hi, hi_ready), (lo, w_split)):
                    pe.wait_ge(ready, n + 1)
                    for k in range(HALF):
                        last = nc.tensor.matmul(c.bank(q % 2, 512, 4), c.cond4[:, half * HALF + k],
                                                part[:, n % 2, k * 512:(k + 1) * 512],
                                                start=(half == 0 and part is hi and k == 0),
                                                stop=(half == 1 and part is lo and k == HALF - 1))
                last.then_inc(halves_done, 1)
                if n >= 3 and half:
                    turn((n - 3) // 2)
            turn(chunks - 1)

        @ph.block.vector
        def _(dve):
            st = Steps(dve, dve_done)
            nc.vector.tensor_copy(c.cond4[:, :, 0:2], c.cond[:]).then_inc(cond_split, 1)
            dve.wait_ge(cond_split, 1)
            split(nc, nc.vector, c.cond4[:, :, 0:2], c.cond4[:, :, 2:4], c.cond[:]).then_inc(cond_split, 1)
            nc.vector.tensor_copy(sel[0:4], c.ident[0:4, 0:2]).then_inc(cond_split, 1)
            dve.wait_ge(cond_split, 3)
            nc.vector.tensor_tensor(sel[0:4], sel[0:4], c.ident[0:4, 2:4], ALU.add).then_inc(cond_split, 1)
            for n in range(2 * chunks):
                dve.wait_ge(hi_ready, n + 1)
                split(nc, nc.vector, hi[:, n % 2], lo[:, n % 2], raw[:, n % RAW]).then_inc(w_split, 1)
            dve.wait_ge(cols_in, 16)
            dve.wait_ge(turned, chunks)
            st.do(nc.vector.tensor_tensor(
                c.mod[:], c.psum[:, 7 * 512:7 * 512 + 2 * N_MOD].rearrange("p (j s) -> p j s", s=2),
                c.cols[:, C_BMOD:C_BMOD + N_MOD].unsqueeze(2).to_broadcast([P, N_MOD, 2]), ALU.add))
            st.wait()
            for n, (sc, g) in enumerate(((SC1, C_G1), (SC2, C_G2))):
                st.do(nc.vector.scalar_tensor_tensor(
                    out=c.ab[:, n], in0=c.mod[:, sc:sc + KD], scalar=1.0,
                    in1=c.cols[:, g:g + KD].unsqueeze(2).to_broadcast([P, KD, 2]), op0=ALU.add, op1=ALU.mult))


def norm_sems(ph):
    return [ph.sem(s) for s in ("squares_summed", "means_ready", "roots_ready", "dve_steps")]


def act_norm(c, act, tiles, sq, ms, root, scratch=185):
    nc, junk = c.nc, c.at(scratch, 2, D)
    for i, t in enumerate(tiles):
        if i >= 2:
            act.wait_ge(sq, i - 1)
        nc.scalar.activation(junk[:, i % 2], c.xs[:, t], ACT.Square, accum_out=c.stat[:, 0, i:i + 1]).then_inc(sq, 1)
    act.wait_ge(ms, 1)
    nc.scalar.activation(c.stat[:, 1, 0:len(tiles)], c.stat[:, 1, 0:len(tiles)], ACT.Sqrt).then_inc(root, 1)


def dve_norm(c, dve, st, tiles, sq, ms, root):
    nc = c.nc
    n = len(tiles)
    dve.wait_ge(sq, n)
    nc.vector.tensor_scalar(c.stat[:, 1, 0:n], c.stat[:, 0, 0:n], 1.0 / D, EPS, ALU.mult, ALU.add).then_inc(ms, 1)
    dve.wait_ge(root, 1)
    st.do(nc.vector.reciprocal(c.stat[:, 0, 0:n], c.stat[:, 1, 0:n]))
    st.wait()


def qkv_ring(c, ph, layer):
    return SplitRing(c, ph, [(c.io["w_in"][layer][b], KD) for b in range(6)], slots=6)


def phase_norm1(c, layer, tiles):
    nc = c.nc
    n = len(tiles)
    xn = c.at(116, NT, D)
    jobs = [(k, s) for k in range(KD) for s in range(2)]
    span = [slice(0, L_LAT), slice(L_LAT, T_ALL)]
    with Phase(nc) as ph:
        ring = qkv_ring(c, ph, layer)
        sq, ms, root, steps = norm_sems(ph)
        xn_ready, turned, high, value, low = (ph.sem(s) for s in (
            "xn_ready", "transposed", "high_ready", "value_ready", "low_ready"))

        @ph.block.sync
        def _(sp):
            ring.load(sp, None)

        @ph.block.gpsimd
        def _(pool):
            ring.split(pool, rounds=True)

        @ph.block.scalar
        def _(act):
            act_norm(c, act, tiles, sq, ms, root, scratch=148)
            for j, (k, s) in enumerate(jobs):
                act.wait_ge(value, j + 1)
                nc.scalar.activation(c.hT_high[:, k, span[s]], c.hT[:, k, span[s]], ACT.Copy).then_inc(high, 1)

        @ph.block.vector
        def _(dve):
            def low_part(j):
                k, s = jobs[j]
                dve.wait_ge(high, j + 1)
                split(nc, nc.vector, c.hT_high[:, k, span[s]], c.hT_low[:, k, span[s]], c.hT[:, k, span[s]]).then_inc(low, 1)

            st = Steps(dve, steps)
            dve_norm(c, dve, st, tiles, sq, ms, root)
            for i, t in enumerate(tiles):
                nc.vector.tensor_scalar(xn[:, t], c.xs[:, t], c.stat[:, 0, i:i + 1], None, ALU.mult).then_inc(xn_ready, 1)
            for j, (k, s) in enumerate(jobs):
                dve.wait_ge(turned, j + 1)
                nc.vector.tensor_scalar(c.hT[:, k, span[s]], c.bank(j % 8, (L_LAT, L_CTX)[s]), c.ab[:, 0, k, s:s + 1],
                                        c.mod[:, SH1 + k, s:s + 1], ALU.mult, ALU.add).then_inc(value, 1)
                if j:
                    low_part(j - 1)
            low_part(len(jobs) - 1)

        @ph.block.tensor
        def _(pe):
            pe.wait_ge(xn_ready, n)
            for j, (k, s) in enumerate(jobs):
                if j >= 8:
                    pe.wait_ge(value, j - 7)
                for i, t in enumerate(range(NT_LAT) if s == 0 else range(NT_LAT, NT)):
                    last = nc.tensor.transpose(c.psum[:, (j % 8) * 512 + i * P:(j % 8) * 512 + (i + 1) * P],
                                               xn[:, t, k * P:(k + 1) * P], c.ident[:])
                last.then_inc(turned, 1)


def phase_qkv(c, layer, full):
    nc, io = c.nc, c.io
    qT, kT, vN = c.at(116, PAIRS, T_ALL), c.at(128, KV_HEADS, T_ALL), c.at(134, NT, P)
    sqb = c.at(143, 2, 640)
    qn = c.at(148, 2, 640)
    qr = c.at(153, 2, 640)
    kd = c.at(158, 2, 256)
    tmp = c.at(160, 4, 320)
    gain = c.at(166, 640)
    w = c.rounded(72, 6, KD, P), c.rounded(48, 6, KD, P)
    ssq = c.at(169, 2, 16)
    rr = c.at(169.5, 2, 16)
    tiles = list(range(NT))
    with Phase(nc) as ph:
        gain_in, proj, sq_d, ms, root, vd, steps, ready, turned, evac = (ph.sem(s) for s in (
            "gain_landed", "projected", "squared", "means_ready", "roots_ready", "v_kept",
            "dve_steps", "qk_ready", "transposed", "evacuated"))
        qk_read = ph.sem("qk_psum_read")

        def q_cols(t):
            return (0 if t < NT_LAT or full else 512, 640)

        @ph.block.sync
        def _(sp):
            sp.dma_start(gain, io["gains"][layer:layer + 1].to_broadcast([P, 640])).then_inc(gain_in, 16)

        @ph.block.tensor
        def _(pe):
            def project(t):
                b = (t % 2) * 2
                if t >= 2:
                    pe.wait_ge(qk_read, t - 1)
                    pe.wait_ge(vd, t - 1)
                pairs = products((c.hT_high, c.hT_low), w)
                for out, lo, hi in ((c.bank(b), 0, 4), (c.bank(b + 1, 256), 4, 6))[0 if q_cols(t)[0] == 0 else 1:]:
                    for k in range(KD):
                        for i, (h, m) in enumerate(pairs):
                            last = nc.tensor.matmul(out, h[:, k, t * P:(t + 1) * P], m[:, lo:hi, k, :],
                                                    start=(k == 0 and i == 0), stop=(k == KD - 1 and i == 2))
                last.then_inc(proj, 1)

            def turn(t):
                b = 4 + (t % 2) * 2
                pe.wait_ge(ready, t + 1)
                if t >= 2:
                    pe.wait_ge(evac, t - 1)
                if q_cols(t)[0] == 0:
                    for j in range(PAIRS):
                        nc.tensor.transpose(c.psum[:, b * 512 + j * P:b * 512 + (j + 1) * P],
                                            qr[:, t % 2, j * P:(j + 1) * P], c.ident[:])
                for j in range(KV_HEADS):
                    last = nc.tensor.transpose(c.psum[:, (b + 1) * 512 + j * P:(b + 1) * 512 + (j + 1) * P],
                                               kd[:, t % 2, j * P:(j + 1) * P], c.ident[:])
                last.then_inc(turned, 1)

            for t in tiles:
                project(t)
                if t >= 1:
                    turn(t - 1)
            turn(NT - 1)

        @ph.block.scalar
        def _(act):
            def keep(t):
                b = 4 + (t % 2) * 2
                act.wait_ge(turned, t + 1)
                if q_cols(t)[0] == 0:
                    nc.scalar.activation(qT[:, :, t * P:(t + 1) * P], c.bank(b).rearrange("p (a b) -> p a b", a=PAIRS), ACT.Copy)
                nc.scalar.activation(kT[:, :, t * P:(t + 1) * P], c.bank(b + 1, 256).rearrange("p (a b) -> p a b", a=2),
                                     ACT.Copy).then_inc(evac, 1)

            for t in tiles:
                b = (t % 2) * 2
                lo, hi = q_cols(t)
                act.wait_ge(proj, t + 1)
                if t >= 2:
                    act.wait_ge(ms, t - 1)
                nc.scalar.activation(sqb[:, t % 2, lo:hi], c.psum[:, b * 512 + lo:b * 512 + hi], ACT.Square).then_inc(sq_d, 1)
                nc.scalar.activation(vN[:, t], c.psum[:, b * 512 + 640:b * 512 + 768], ACT.Copy).then_inc(vd, 1)
                act.wait_ge(ms, t + 1)
                nc.scalar.activation(ssq[:, t % 2, lo // HD:10], ssq[:, t % 2, lo // HD:10], ACT.Sqrt).then_inc(root, 1)
                if t >= 1:
                    keep(t - 1)
            keep(NT - 1)

        @ph.block.vector
        def _(dve):
            st = Steps(dve, steps)
            dve.wait_ge(gain_in, 16)
            for t in tiles:
                b, p = (t % 2) * 2, t % 2
                lo, hi = q_cols(t)
                h0, nh = lo // HD, (hi - lo) // HD
                heads = lambda v: v[:, lo:hi].rearrange("p (h d) -> p h d", d=HD)
                dve.wait_ge(sq_d, t + 1)
                if t >= 2:
                    dve.wait_ge(root, t - 1)
                st.wait()
                st.do(nc.vector.tensor_reduce(ssq[:, p, h0:10], heads(sqb[:, p]), AX.X, ALU.add))
                st.wait()
                nc.vector.tensor_scalar(ssq[:, p, h0:10], ssq[:, p, h0:10], 1.0 / HD, EPS, ALU.mult, ALU.add).then_inc(ms, 1)
                dve.wait_ge(root, t + 1)
                st.do(nc.vector.reciprocal(rr[:, p, h0:10], ssq[:, p, h0:10]))
                st.wait()
                if h0 == 0:
                    st.do(nc.vector.tensor_scalar(rr[:, p, 0:HEADS], rr[:, p, 0:HEADS], HD ** -0.5, None, ALU.mult))
                    st.wait()
                nc.vector.tensor_tensor(heads(qn[:, p]), c.psum[:, b * 512 + lo:b * 512 + hi].rearrange("p (h d) -> p h d", d=HD),
                                        rr[:, p, h0:10].unsqueeze(2).to_broadcast([P, nh, HD]), ALU.mult).then_inc(qk_read, 1)
                dve.wait_ge(qk_read, t + 1)
                if t >= 2:
                    dve.wait_ge(turned, t - 1)
                target = qn if t < NT_LAT else qr
                st.do(nc.vector.tensor_tensor(target[:, p, lo:hi], qn[:, p, lo:hi], gain[:, lo:hi], ALU.mult))
                st.wait()
                if t < NT_LAT:
                    half = lambda v, i: v.rearrange("p (g r c) -> p g r c", r=2, c=16)[:, :, i, :].rearrange(
                        "p (h a) c -> p h a c", a=2)
                    table = lambda i: c.rope[:, t, i].unsqueeze(1).to_broadcast([P, 10, 2, 16])
                    w4 = [tmp[:, i].rearrange("p (h a c) -> p h a c", a=2, c=16) for i in range(4)]
                    for i, (h, s) in enumerate(((0, 0), (1, 1), (1, 0), (0, 1))):
                        st.do(nc.vector.tensor_tensor(w4[i], half(qn[:, p], h), table(s), ALU.mult))
                    st.wait()
                    st.do(nc.vector.tensor_tensor(half(qr[:, p], 0), w4[0], w4[1], ALU.subtract))
                    st.do(nc.vector.tensor_tensor(half(qr[:, p], 1), w4[2], w4[3], ALU.add))
                    st.wait()
                nc.vector.tensor_copy(kd[:, p].rearrange("p (v r d) -> p v r d", r=2, d=HD),
                                      qr[:, p, 512:640].rearrange("p (v d) -> p v d", d=HD).unsqueeze(2).to_broadcast(
                                          [P, KV_HEADS, 2, HD])).then_inc(ready, 1)


def phase_attention(c, full):
    nc = c.nc
    qT, kT, vN = c.at(116, PAIRS, T_ALL), c.at(128, KV_HEADS, T_ALL), c.at(134, NT, P)
    prob = c.at(137, 3, T_ALL)
    pT = c.at(146, 2, NT, L_LAT)
    yT = c.own(80, KB_BR, T_ALL)
    nmax, rsum, rinv = c.at(170, 4), c.at(170.25, 4), c.at(170.5, 4)
    groups = []
    for pair in range(PAIRS):
        for hh in range(2):
            groups.append((pair, hh, list(range(NT_LAT)), list(range(NT))))
    if full:
        for pair in range(PAIRS):
            for hh in range(2):
                groups.append((pair, hh, list(range(NT_LAT, NT)), list(range(NT_LAT, NT))))
    units = [(g, i, q) for g, (_, _, qs, _) in enumerate(groups) for i, q in enumerate(qs)]
    last_unit = [max(u for u, x in enumerate(units) if x[0] == g) for g in range(len(groups))]
    with Phase(nc) as ph:
        scored, maxed, exped, normed, turned, kept, summed, y_kept, steps = (ph.sem(s) for s in (
            "scores_ready", "max_ready", "exp_done", "probs_ready", "probs_turned", "turned_kept",
            "values_summed", "y_kept", "dve_steps"))

        @ph.block.tensor
        def _(pe):
            def score(u):
                g, _, q = units[u]
                pair, hh, _, keys = groups[g]
                kv = (2 * pair + hh) // (HEADS // KV_HEADS)
                if u >= 2:
                    pe.wait_ge(exped, u - 1)
                b = (u % 2) * 1024
                r = slice(64 * hh, 64 * hh + 64)
                if keys[0] == 0:
                    nc.tensor.matmul(c.psum[:, b:b + 512], qT[r, pair, q * P:(q + 1) * P], kT[r, kv, 0:512], start=True, stop=True)
                nc.tensor.matmul(c.psum[:, b + 512:b + 768], qT[r, pair, q * P:(q + 1) * P], kT[r, kv, 512:768],
                                 start=True, stop=True).then_inc(scored, 1)

            def turn(u):
                g = units[u][0]
                pe.wait_ge(normed, u + 1)
                if u >= 1:
                    pe.wait_ge(kept, u)
                for kt in groups[g][3]:
                    last = nc.tensor.transpose(c.psum[:, 2048 + kt * P:2048 + (kt + 1) * P], prob[:, u % 3, kt * P:(kt + 1) * P], c.ident[:])
                last.then_inc(turned, 1)

            def values(g):
                pair, hh, qs, keys = groups[g]
                kv = (2 * pair + hh) // (HEADS // KV_HEADS)
                w = len(qs) * P
                pe.wait_ge(kept, last_unit[g] + 1)
                if hh == 0 and g >= 4:
                    pe.wait_ge(y_kept, g // 2 - 1)
                bank = 6 + (g // 2) % 2
                for i, kt in enumerate(keys):
                    last = nc.tensor.matmul(c.psum[64 * hh:64 * hh + 64, bank * 512:bank * 512 + w], vN[:, kt, kv * HD:(kv + 1) * HD],
                                            pT[:, g % 2, kt, 0:w], start=(i == 0), stop=(i == len(keys) - 1))
                last.then_inc(summed, 1)

            for u in range(len(units) + 3):
                if u < len(units):
                    score(u)
                if 2 <= u < len(units) + 2:
                    turn(u - 2)
                if u >= 3 and (u - 3) in last_unit:
                    values(last_unit.index(u - 3))

        @ph.block.vector
        def _(dve):
            st = Steps(dve, steps)
            for u in range(len(units) + 1):
                if u < len(units):
                    lo = groups[units[u][0]][3][0] * P
                    dve.wait_ge(scored, u + 1)
                    nc.vector.tensor_reduce(nmax[:, u % 4:u % 4 + 1], c.psum[:, (u % 2) * 1024 + lo:(u % 2) * 1024 + 768],
                                            AX.X, ALU.max, negate=True).then_inc(maxed, 1)
                if u >= 1:
                    v = u - 1
                    lo = groups[units[v][0]][3][0] * P
                    dve.wait_ge(exped, v + 1)
                    st.do(nc.vector.reciprocal(rinv[:, v % 4:v % 4 + 1], rsum[:, v % 4:v % 4 + 1]))
                    st.wait()
                    nc.vector.tensor_scalar(prob[:, v % 3, lo:768], prob[:, v % 3, lo:768], rinv[:, v % 4:v % 4 + 1], None,
                                            ALU.mult).then_inc(normed, 1)

        @ph.block.scalar
        def _(act):
            def keep(u):
                g, i, q = units[u]
                _, hh, qs, keys = groups[g]
                act.wait_ge(turned, u + 1)
                if g >= 2:
                    act.wait_ge(summed, g - 1)
                nc.scalar.activation(pT[:, g % 2, keys[0]:NT, i * P:(i + 1) * P],
                                     c.psum[:, 2048 + keys[0] * P:2048 + 768].rearrange("p (k q) -> p k q", q=P),
                                     ACT.Copy).then_inc(kept, 1)

            def keep_y(pr):
                pair, _, qs, _ = groups[2 * pr]
                w, q0 = len(qs) * P, qs[0] * P
                act.wait_ge(summed, 2 * pr + 2)
                nc.scalar.activation(yT[:, pair, q0:q0 + w], c.bank(6 + pr % 2, w), ACT.Copy).then_inc(y_kept, 1)

            pairs_done = 0
            for u in range(len(units) + 4):
                if u < len(units):
                    lo = groups[units[u][0]][3][0] * P
                    act.wait_ge(maxed, u + 1)
                    if u >= 3:
                        act.wait_ge(turned, u - 2)
                    nc.scalar.activation(prob[:, u % 3, lo:768], c.psum[:, (u % 2) * 1024 + lo:(u % 2) * 1024 + 768], ACT.Exp,
                                         bias=nmax[:, u % 4:u % 4 + 1], accum_out=rsum[:, u % 4:u % 4 + 1]).then_inc(exped, 1)
                if 2 <= u < len(units) + 2:
                    keep(u - 2)
                if u >= 4 and (u - 4) in last_unit and last_unit.index(u - 4) % 2 == 1:
                    keep_y(pairs_done)
                    pairs_done += 1


def dwconv(c, st, u, src, streams, w0, w2, done):
    nc = c.nc
    for a, n in streams:
        st.do(nc.vector.scalar_tensor_tensor(out=u[:, a + 1:a + n], in0=src[:, a:a + n - 1], scalar=w0,
                                             in1=u[:, a + 1:a + n], op0=ALU.mult, op1=ALU.add))
    st.wait()
    for i, (a, n) in enumerate(streams):
        ins = nc.vector.scalar_tensor_tensor(out=u[:, a:a + n - 1], in0=src[:, a + 1:a + n], scalar=w2,
                                             in1=u[:, a:a + n - 1], op0=ALU.mult, op1=ALU.add)
        if i < len(streams) - 1:
            st.do(ins)
    ins.then_inc(done, 1)


def feature_job(c, w, bank, width, kt, rhs, ahead=None):
    nc = c.nc
    for lo, hi in ((0, 512), (512, width)):
        if hi <= lo:
            continue
        for k in range(kt):
            if ahead is not None and lo == 0:
                ahead(k)
            for i, (a, b) in enumerate(products(w, rhs)):
                last = nc.tensor.matmul(c.psum[:, bank * 512 + lo:bank * 512 + hi], a[:, k], b[:, k, lo:hi],
                                        start=(k == 0 and i == 0), stop=(k == kt - 1 and i == 2))
    return last


def phase_conv_branches(c, layer, full):
    nc, io = c.nc, c.io
    width = T_ALL if full else L_LAT
    streams = [(0, L_LAT), (L_LAT, L_CTX)][:2 if full else 1]
    nt = width // P
    ysc = c.own(92, KB_BR, T_ALL)
    x2T = c.at(140, KB_BR, T_ALL)
    vN, x1N = c.at(116, NT, W_BR), c.at(128, NT, W_BR)
    cgs, cx, yc = c.at(152, 2, T_ALL), c.at(158, 2, T_ALL), c.at(164, 2, T_ALL)
    uu = c.at(170, 2, T_ALL)
    jobs = []
    for j in range(KB_BR):
        jobs += [("cg", j, B_SC + KB_BR + j), ("xs", j, B_SC + 2 * KB_BR + j), ("bg", j, B_SC + j)]
    for j in range(KB_BR):
        jobs += [(q, j, B_HY + q * KB_BR + j) for q in range(3)]
    H0 = 3 * KB_BR
    turns = [n for n, x in enumerate(jobs) if x[0] in (0, 1)]
    acts = [sum(x[0] != "bg" for x in jobs[:n + 1]) for n in range(len(jobs))]
    SLOTS = 3
    TB = 3072
    with Phase(nc) as ph:
        ring = SplitRing(c, ph, [(io["w_in"][layer][b], KD) for _, _, b in jobs])
        restored, proj, a_done, cx_ready, sc_done, conv_done, turned, kept, steps = (ph.sem(s) for s in (
            "restored", "projected", "act_done", "cx_ready", "sc_done", "conv_done", "transposed", "turned_kept", "dve_steps"))

        def cols(base, tap, tile, tiles):
            i = base + tap * tiles + tile
            return c.cols[:, i:i + 1]

        def psum_read(n):
            kind, j, _ = jobs[n]
            return {"cg": (a_done, acts[n]), "xs": (cx_ready, j + 1), "bg": (sc_done, j + 1)}.get(
                kind, (conv_done, n - H0 + 1))

        def slot(n):
            return c.psum[:, (n % SLOTS) * 1024:(n % SLOTS) * 1024 + width]

        @ph.block.sync
        def _(sp):
            ring.load(sp, proj)

        def restore(eng, ks):
            for k in ks:
                eng.tensor_tensor(c.hT[:, k], c.hT_low[:, k].bitcast(F32), c.hT_high[:, k].bitcast(F32), ALU.add).then_inc(restored, 1)

        @ph.block.gpsimd
        def _(pool):
            ring.split(pool)
            pool.wait_ge(proj, len(jobs))
            restore(nc.gpsimd, range(5, KD))

        @ph.block.tensor
        def _(pe):
            def turn(m):
                pe.wait_ge(conv_done, turns[m] - H0 + 1)
                if m >= 1:
                    pe.wait_ge(kept, m)
                for t in range(nt):
                    last = nc.tensor.transpose(c.psum[:, TB + t * P:TB + (t + 1) * P], uu[:, m % 2, t * P:(t + 1) * P], c.ident[:])
                last.then_inc(turned, 1)

            m = 0
            for n in range(len(jobs)):
                pe.wait_ge(ring.ready, n + 1)
                if n >= SLOTS:
                    pe.wait_ge(*psum_read(n - SLOTS))
                feature_job(c, ring.parts(n), 2 * (n % SLOTS), width, KD, (c.hT_high, c.hT_low)).then_inc(proj, 1)
                while m < len(turns) and turns[m] <= n - 2:
                    turn(m)
                    m += 1
            while m < len(turns):
                turn(m)
                m += 1

        @ph.block.scalar
        def _(act):
            def keep(m):
                kind, j, _ = jobs[turns[m]]
                act.wait_ge(turned, m + 1)
                nc.scalar.activation((vN if kind == 0 else x1N)[:, 0:nt, j * P:(j + 1) * P],
                                     c.psum[:, TB:TB + nt * P].rearrange("p (t q) -> p t q", q=P), ACT.Copy).then_inc(kept, 1)

            m = 0
            ring.round_ahead(act, -1, proj)
            for n, (kind, j, b) in enumerate(jobs):
                if kind == "cg":
                    act.wait_ge(proj, n + 1)
                    if j >= 2:
                        act.wait_ge(cx_ready, j - 1)
                    nc.scalar.activation(cgs[:, j % 2, 0:width], slot(n), ACT.Copy).then_inc(a_done, 1)
                elif kind == "xs":
                    act.wait_ge(cx_ready, j + 1)
                    if j >= 2:
                        act.wait_ge(sc_done, j - 1)
                    nc.scalar.activation(yc[:, j % 2, 0:width], cx[:, j % 2, 0:width], ACT.Copy,
                                         scale=cols(C_SCW, 1, j, KB_BR)).then_inc(a_done, 1)
                elif kind != "bg":
                    act.wait_ge(proj, n + 1)
                    out = x2T[:, j, 0:width]
                    if kind < 2:
                        i = turns.index(n)
                        out = uu[:, i % 2, 0:width]
                        if i >= 2:
                            act.wait_ge(turned, i - 1)
                    i = kind * KB_BR + j
                    nc.scalar.activation(out, slot(n), ACT.Identity, scale=cols(C_HYW, 1, i, 3 * KB_BR),
                                         bias=c.cols[:, C_HYB + i:C_HYB + i + 1]).then_inc(a_done, 1)
                ring.round_ahead(act, n, proj)
                while m < len(turns) and turns[m] <= n - 2:
                    keep(m)
                    m += 1
            while m < len(turns):
                keep(m)
                m += 1

        @ph.block.vector
        def _(dve):
            st = Steps(dve, steps)
            for n, (kind, j, b) in enumerate(jobs):
                if kind == "xs":
                    dve.wait_ge(proj, n + 1)
                    dve.wait_ge(a_done, acts[n - 1])
                    nc.vector.tensor_tensor(cx[:, j % 2, 0:width], cgs[:, j % 2, 0:width], slot(n), ALU.mult).then_inc(cx_ready, 1)
                    dve.wait_ge(cx_ready, j + 1)
                    dve.wait_ge(a_done, acts[n])
                    dwconv(c, st, yc[:, j % 2], cx[:, j % 2], streams, cols(C_SCW, 0, j, KB_BR), cols(C_SCW, 2, j, KB_BR), steps)
                    st.n += 1
                elif kind == "bg":
                    dve.wait_ge(proj, n + 1)
                    st.wait()
                    nc.vector.tensor_tensor(ysc[:, j, 0:width], yc[:, j % 2, 0:width], slot(n), ALU.mult).then_inc(sc_done, 1)
                elif kind != "cg":
                    out = x2T[:, j] if kind == 2 else uu[:, turns.index(n) % 2]
                    i = kind * KB_BR + j
                    dve.wait_ge(a_done, acts[n])
                    dwconv(c, st, out, slot(n), streams, cols(C_HYW, 0, i, 3 * KB_BR), cols(C_HYW, 2, i, 3 * KB_BR), conv_done)
            dve.wait_ge(proj, len(jobs))
            restore(nc.vector, range(5))


def phase_filter_mlp(c, layer, length):
    nc, io = c.nc, c.io
    z, h1, h2 = c.at(194, length), c.at(196, length), c.at(186, length)
    a, r = c.at(198, length), c.at(192, length)
    w1, w2 = c.at(200, FH), c.at(200.25, FH)
    with Phase(nc) as ph:
        landed, mm, reduced, sined, steps = (ph.sem(s) for s in ("landed", "products", "reduced", "sines", "dve_steps"))

        @ph.block.sync
        def _(sp):
            sp.dma_start(z[0:EMB, :], io[f"feat{length}"]).then_inc(landed, 16)
            sp.dma_start(w1[0:EMB, :], io["hy_w1"][layer]).then_inc(landed, 16)
            sp.dma_start(w2[0:FH, :], io["hy_w2"][layer]).then_inc(landed, 16)

        @ph.block.tensor
        def _(pe):
            pe.wait_ge(landed, 48)
            nc.tensor.matmul(c.bank(0, length, FH), w1[0:EMB, :], z[0:EMB, :], start=True, stop=True).then_inc(mm, 1)
            pe.wait_ge(sined, 1)
            nc.tensor.matmul(c.bank(1, length, FH), w2[0:FH, :], h1[0:FH, :], start=True, stop=True).then_inc(mm, 1)

        @ph.block.scalar
        def _(act):
            for i, h in enumerate((h1, h2)):
                act.wait_ge(reduced, i + 1)
                nc.scalar.activation(h[0:FH, :], r[0:FH, :], ACT.Sin).then_inc(sined, 1)

        @ph.block.vector
        def _(dve):
            st = Steps(dve, steps)
            for i in range(2):
                b, f = C_FIL + 2 * i, C_FIL + 2 * i + 1
                dve.wait_ge(mm, i + 1)
                if i:
                    dve.wait_ge(sined, 1)
                st.do(nc.vector.tensor_scalar(a[0:FH, :], c.bank(i, length, FH), c.cols[0:FH, b:b + 1], c.cols[0:FH, f:f + 1],
                                              ALU.add, ALU.mult))
                st.wait()
                st.do(nc.vector.tensor_scalar(r[0:FH, :], a[0:FH, :], 1.0 / TWO_PI, ROUND, ALU.mult, ALU.add))
                st.wait()
                st.do(nc.vector.tensor_scalar(r[0:FH, :], r[0:FH, :], ROUND, None, ALU.subtract))
                st.wait()
                for part in (PI_HI, PI_MID, PI_LO):
                    st.do(nc.vector.scalar_tensor_tensor(out=a[0:FH, :], in0=r[0:FH, :], scalar=-part, in1=a[0:FH, :],
                                                         op0=ALU.mult, op1=ALU.add))
                    st.wait()
                nc.vector.tensor_scalar(r[0:FH, :], a[0:FH, :], PI_F32, -PI_F32, ALU.min, ALU.max).then_inc(reduced, 1)


def dft_views(c, length):
    nt = length // P
    at, out = 48, {}
    for name, w in (("cos", length), ("fwd", length), ("inv", length), ("sin0", P), ("cos_b", P)):
        out[name] = c.at(at, nt, w)
        at += nt * w / 256
    out["all"] = c.at(48, int((at - 48) * 256))
    return out


def spectrum_views(c, nt):
    return c.at(152, nt, W_BR), c.at(160, nt, W_BR), c.at(168, W_BR)


def spectrum_jobs(nt):
    return [(w, f) for f in range(nt) for w in ("re", "im")] + [("re_b", 0)]


def phase_spectrum(c, layer, length, order):
    nc, io = c.nc, c.io
    nt = length // P
    which = 0 if length == L_LAT else 1
    tab = dft_views(c, length)
    h2 = c.at(186, length)
    w3, absdec, win = c.at(76, 2 * W_BR), c.at(190, W_BR), c.at(188, W_BR)
    rnorm, bias, ab = c.at(192, W_BR), c.at(194, W_BR), c.at(196, 2 * W_BR)
    hw = c.at(170, nt, 2 * W_BR)
    kre, kim, kre_b = spectrum_views(c, nt)
    jobs = spectrum_jobs(nt)
    with Phase(nc) as ph:
        tab_in, w3_in, dec_in, bias_in, made, abs_d, win_d, hw_d, ab_d, normed, steps, folded, sums, kept = (ph.sem(s) for s in (
            "tables_landed", "w3_landed", "decay_landed", "bias_landed", "filter_made", "decay_abs", "window_done",
            "windowed", "abs_done", "norm_summed", "dve_steps", "folded", "spectrum_summed", "spectrum_kept"))

        @ph.block.sync
        def _(sp):
            sp.dma_start(w3[0:FH, :], io["hy_w3"][layer][:, order * 2 * W_BR:(order + 1) * 2 * W_BR]).then_inc(w3_in, 16)
            sp.dma_start(absdec, io["hy_decay"][layer][order:order + 1].to_broadcast([P, W_BR])).then_inc(dec_in, 16)
            sp.dma_start(bias[0:1, :], io["hy_bias"][layer][order:order + 1]).then_inc(bias_in, 16)
            if order == 0:
                sp.dma_start(tab["all"], io[f"dft{length}"]).then_inc(tab_in, 16)

        @ph.block.tensor
        def _(pe):
            def norm(t):
                pe.wait_ge(ab_d, t + 1)
                for d in range(2):
                    last = nc.tensor.matmul(c.bank(4), c.ones[:], ab[:, d * W_BR:(d + 1) * W_BR],
                                            start=(t == 0 and d == 0), stop=(t == nt - 1 and d == 1))
                last.then_inc(normed, 1)

            pe.wait_ge(w3_in, 16)
            for t in range(nt):
                if t >= 2:
                    pe.wait_ge(hw_d, t - 1)
                for d in range(2):
                    last = nc.tensor.matmul(c.bank(2 * (t % 2) + d), h2[0:FH, t * P:(t + 1) * P], w3[0:FH, d * W_BR:(d + 1) * W_BR],
                                            start=True, stop=True)
                last.then_inc(made, 1)
                if t >= 1:
                    norm(t - 1)
            norm(nt - 1)
            if order == 0:
                pe.wait_ge(tab_in, 16)
            pe.wait_ge(folded, nt)
            for n, (what, ft) in enumerate(jobs):
                if n >= 4:
                    pe.wait_ge(kept, n - 3)
                src = 1 if what == "im" else 0
                table = {"re": tab["cos"], "im": tab["fwd"] if ft else tab["sin0"], "re_b": tab["cos_b"]}[what]
                for t in range(nt):
                    last = nc.tensor.matmul(c.bank(n % 4), table[:, t, ft * P:(ft + 1) * P],
                                            hw[:, t, src * W_BR:(src + 1) * W_BR], start=(t == 0), stop=(t == nt - 1))
                last.then_inc(sums, 1)

        @ph.block.scalar
        def _(act):
            act.wait_ge(dec_in, 16)
            nc.scalar.activation(absdec, absdec, ACT.Abs).then_inc(abs_d, 1)
            act.wait_ge(abs_d, 1)
            for t in range(nt):
                if t >= 1:
                    act.wait_ge(hw_d, t)
                nc.scalar.activation(win, absdec, ACT.Exp, scale=c.consts[:, 4 * which + t:4 * which + t + 1]).then_inc(win_d, 1)
                act.wait_ge(hw_d, t + 1)
                if t >= 1:
                    act.wait_ge(normed, t)
                nc.scalar.activation(ab, hw[:, t], ACT.Abs).then_inc(ab_d, 1)

        @ph.block.vector
        def _(dve):
            st = Steps(dve, steps)
            for t in range(nt):
                dve.wait_ge(made, t + 1)
                dve.wait_ge(win_d, t + 1)
                nc.vector.tensor_tensor(hw[:, t].rearrange("p (d n) -> p d n", d=2),
                                        c.psum[:, (t % 2) * 1024:(t % 2) * 1024 + 1024].rearrange("p (d n) -> p d n", d=2),
                                        win.unsqueeze(1).to_broadcast([P, 2, W_BR]), ALU.mult).then_inc(hw_d, 1)
            dve.wait_ge(normed, nt)
            dve.wait_ge(bias_in, 16)
            st.do(nc.vector.reciprocal(rnorm, c.bank(4)))
            st.do(nc.vector.tensor_tensor(hw[0:1, 0, W_BR:2 * W_BR], c.bank(4, 512, 1), bias[0:1, :], ALU.mult))
            st.wait()
            for t in range(nt):
                st.do(nc.vector.tensor_tensor(hw[:, t, 0:W_BR], hw[:, t, 0:W_BR], hw[:, t, W_BR:2 * W_BR], ALU.add))
                st.wait()
                nc.vector.scalar_tensor_tensor(out=hw[:, t, W_BR:2 * W_BR], in0=hw[:, t, W_BR:2 * W_BR], scalar=-2.0,
                                               in1=hw[:, t, 0:W_BR], op0=ALU.mult, op1=ALU.add).then_inc(folded, 1)
            for n, (what, ft) in enumerate(jobs):
                dst = kre_b if what == "re_b" else (kre if what == "re" else kim)[:, ft]
                wf = c.consts[:, 8 + which:9 + which] if ft == 0 else 1.0 / length
                dve.wait_ge(sums, n + 1)
                nc.vector.scalar_tensor_tensor(out=dst, in0=c.bank(n % 4), scalar=wf, in1=rnorm,
                                               op0=ALU.mult, op1=ALU.mult).then_inc(kept, 1)


def phase_long_conv(c, length, order):
    nc = c.nc
    nt = length // P
    t0 = 0 if length == L_LAT else NT_LAT
    tab = dft_views(c, length)
    kre, kim, kre_b = spectrum_views(c, nt)
    vN, x1N, x2T = c.at(116, NT, W_BR), c.at(128, NT, W_BR), c.at(140, KB_BR, T_ALL)
    yhy = c.own(104, KB_BR, T_ALL)
    yre, yim = c.at(170, nt, W_BR), c.at(178, nt, W_BR)
    tmp = c.at(188, 4, W_BR)
    with Phase(nc) as ph:
        spec, read, prod, steps, back, kept = (ph.sem(s) for s in (
            "spectrum_ready", "spectrum_read", "product_ready", "dve_steps", "back_summed", "back_kept"))

        @ph.block.tensor
        def _(pe):
            for f in range(nt):
                if f >= 2:
                    pe.wait_ge(read, f - 1)
                for i, table in enumerate((tab["cos"], tab["fwd"])):
                    for t in range(nt):
                        last = nc.tensor.matmul(c.bank(2 * (f % 2) + i), table[:, t, f * P:(f + 1) * P], vN[:, t0 + t],
                                                start=(t == 0), stop=(t == nt - 1))
                last.then_inc(spec, 1)
            pe.wait_ge(prod, nt)
            for n in range(nt if order == 0 else KB_BR):
                out = c.bank(4 + n % 4, W_BR if order == 0 else length)
                for i, (y, table) in enumerate(((yre, tab["cos"]), (yim, tab["inv"]))):
                    for f in range(nt):
                        if order == 0:
                            a, b = table[:, f, n * P:(n + 1) * P], y[:, f]
                        else:
                            a, b = y[:, f, n * P:(n + 1) * P], table[:, f, :]
                        last = nc.tensor.matmul(out, a, b, start=(i == 0 and f == 0), stop=(i == 1 and f == nt - 1))
                last.then_inc(back, 1)

        @ph.block.vector
        def _(dve):
            st = Steps(dve, steps)
            for f in range(nt):
                ure, uim = c.bank(2 * (f % 2)), c.bank(2 * (f % 2) + 1)
                dve.wait_ge(spec, f + 1)
                if f:
                    dve.wait_ge(prod, f)
                st.do(nc.vector.tensor_tensor(tmp[:, 0], ure, kre[:, f], ALU.mult))
                st.do(nc.vector.tensor_tensor(tmp[:, 1], uim, kim[:, f], ALU.mult))
                st.do(nc.vector.tensor_tensor(tmp[:, 2], ure, kim[:, f], ALU.mult))
                nc.vector.tensor_tensor(tmp[:, 3], uim, kre[:, f] if f else kre_b, ALU.mult).then_inc(read, 1)
                st.wait()
                st.do(nc.vector.tensor_tensor(yre[:, f], tmp[:, 0], tmp[:, 1], ALU.subtract))
                dve.wait_ge(read, f + 1)
                nc.vector.tensor_tensor(yim[:, f], tmp[:, 2], tmp[:, 3], ALU.add).then_inc(prod, 1)
            for n in range(nt if order == 0 else KB_BR):
                dve.wait_ge(back, n + 1)
                if order == 0:
                    nc.vector.tensor_tensor(vN[:, t0 + n], c.bank(4 + n % 4), x1N[:, t0 + n], ALU.mult).then_inc(kept, 1)
                else:
                    lo = t0 * P
                    nc.vector.tensor_tensor(yhy[:, n, lo:lo + length], c.bank(4 + n % 4, length), x2T[:, n, lo:lo + length],
                                            ALU.mult).then_inc(kept, 1)


def phase_rows(c, wanted):
    nc = c.nc
    diag = c.at(197, 4, P)
    n_all = len(wanted) * KD
    with Phase(nc) as ph:
        made, spread, kept = (ph.sem(s) for s in ("diagonals_made", "rows_spread", "rows_kept"))

        @ph.block.vector
        def _(dve):
            for n in range(n_all):
                if n >= 4:
                    dve.wait_ge(spread, n - 3)
                nc.vector.tensor_scalar(diag[:, n % 4], c.ident[:], wanted[n // KD][0](n % KD), None, ALU.mult).then_inc(made, 1)

        @ph.block.tensor
        def _(pe):
            for n in range(n_all):
                w = n // KD
                pe.wait_ge(made, n + 1)
                if n % KD == 0 and w >= 4:
                    pe.wait_ge(kept, w - 3)
                at = (w % 4) * 1024 + (n % KD) * P
                nc.tensor.matmul(c.psum[:, at:at + P], c.ones[:], diag[:, n % 4], start=True, stop=True).then_inc(spread, 1)

        @ph.block.scalar
        def _(act):
            for w, (_, dst) in enumerate(wanted):
                act.wait_ge(spread, (w + 1) * KD)
                nc.scalar.activation(dst, c.psum[:, (w % 4) * 1024:(w % 4 + 1) * 1024], ACT.Copy).then_inc(kept, 1)


def phase_merge(c, layer, full):
    nc, io = c.nc, c.io
    width = T_ALL if full else L_LAT
    ys = [c.own(at, KB_BR, T_ALL) for at in (80, 92, 104)]
    y_high = [c.rounded(at, KB_BR, T_ALL) for at in (152, 188, 152)]
    h_high = c.rounded(164, KD, T_ALL)
    y_low = [c.rounded(at, KB_BR, T_ALL) for at in (80, 92, 104)]
    mT = c.at(116, KD, T_ALL)
    sig, tmp = c.at(140, 2, T_ALL), c.at(146, 2, T_ALL)
    gates = [(br, i) for br in range(3) for i in range(KD)]
    n_all = 2 * len(gates)
    SLOTS = 4
    AHEAD = (0, 2, KD + 2)
    with Phase(nc) as ph:
        blocks = []
        for br, i in gates:
            blocks += [(io["w_in"][layer][B_GATE + br * KD + i], KD), (io["w_br"][layer][br * KD + i], KB_BR)]
        ring = SplitRing(c, ph, blocks)
        proj, sig_d, gated, steps, h_rounded, h_split, y_rounded, y_split = (ph.sem(s) for s in (
            "projected", "sigmoid_done", "gated", "dve_steps", "h_high_ready", "h_split", "y_high_ready", "y_split"))

        @ph.block.sync
        def _(sp):
            ring.load(sp, proj)

        @ph.block.gpsimd
        def _(pool):
            ring.split(pool)

        @ph.block.tensor
        def _(pe):
            for n in range(n_all):
                (br, i), is_y = gates[n // 2], n % 2
                pe.wait_ge(ring.ready, n + 1)
                if n >= SLOTS:
                    pe.wait_ge(gated if is_y else sig_d, (n - SLOTS) // 2 + 1)
                if is_y:
                    pe.wait_ge(y_split, br + 1)
                    job = feature_job(c, ring.parts(n), 2 * (n % SLOTS), width, KB_BR, (y_high[br], y_low[br]))
                else:
                    job = feature_job(c, ring.parts(n), 2 * (n % SLOTS), width, KD, (h_high, c.hT_low),
                                      (lambda k: pe.wait_ge(h_split, k + 1)) if n == 0 else None)
                job.then_inc(proj, 1)

        def slot(n):
            return c.psum[:, (n % SLOTS) * 1024:(n % SLOTS) * 1024 + width]

        @ph.block.scalar
        def _(act):
            def round_y(br):
                if br == 2:
                    act.wait_ge(proj, 2 * KD)
                nc.scalar.activation(y_high[br][:, :, 0:width], ys[br][:, :, 0:width], ACT.Copy).then_inc(y_rounded, 1)

            for k in range(KD):
                nc.scalar.activation(h_high[:, k, 0:width], c.hT[:, k, 0:width], ACT.Copy).then_inc(h_rounded, 1)
            ring.round_ahead(act, -1, proj)
            for g in range(len(gates)):
                if g in AHEAD:
                    round_y(AHEAD.index(g))
                act.wait_ge(proj, 2 * g + 1)
                if g >= 2:
                    act.wait_ge(gated, g - 1)
                nc.scalar.activation(sig[:, g % 2, 0:width], slot(2 * g), ACT.Sigmoid).then_inc(sig_d, 1)
                ring.round_ahead(act, 2 * g, proj)
                ring.round_ahead(act, 2 * g + 1, proj)

        @ph.block.vector
        def _(dve):
            def split_y(br):
                y = ys[br][:, :, 0:width]
                dve.wait_ge(y_rounded, br + 1)
                split(nc, nc.vector, y_high[br][:, :, 0:width], y_low[br][:, :, 0:width], y).then_inc(y_split, 1)

            st = Steps(dve, steps)
            for k in range(KD):
                dve.wait_ge(h_rounded, k + 1)
                split(nc, nc.vector, h_high[:, k, 0:width], c.hT_low[:, k, 0:width], c.hT[:, k, 0:width]).then_inc(h_split, 1)
            for g, (br, i) in enumerate(gates):
                if g in AHEAD:
                    split_y(AHEAD.index(g))
                dve.wait_ge(proj, 2 * g + 2)
                dve.wait_ge(sig_d, g + 1)
                if br:
                    st.wait()
                dst = tmp[:, g % 2, 0:width] if br else mT[:, i, 0:width]
                nc.vector.tensor_tensor(dst, sig[:, g % 2, 0:width], slot(2 * g + 1), ALU.mult).then_inc(gated, 1)
                if br:
                    dve.wait_ge(gated, g + 1)
                    st.do(nc.vector.tensor_tensor(mT[:, i, 0:width], mT[:, i, 0:width], dst, ALU.add))


def phase_out(c, layer, full):
    nc, io = c.nc, c.io
    mT = c.at(116, KD, T_ALL)
    rows = [c.at(160, D), c.at(164, D)]
    tmp = c.at(152, 2, D)
    nt = NT if full else NT_LAT
    with Phase(nc) as ph:
        w_landed, proj, scaled, steps = (ph.sem(s) for s in ("w_landed", "projected", "scaled", "dve_steps"))

        @ph.block.sync
        def _(sp):
            for h in range(2):
                sp.dma_start(c.wring[:, 4 * h:4 * h + 4].rearrange("p b k n -> p b (k n)"),
                             io["w_out"][layer][4 * h:4 * h + 4].rearrange("b p k n -> p b (k n)")).then_inc(w_landed, 16)

        @ph.block.tensor
        def _(pe):
            pe.wait_ge(w_landed, 32)
            for t in range(nt):
                if t >= 4:
                    pe.wait_ge(scaled, t - 3)
                for h in range(2):
                    for k in range(KD):
                        last = nc.tensor.matmul(c.bank(2 * (t % 4) + h), mT[:, k, t * P:(t + 1) * P],
                                                c.wring[:, 4 * h:4 * h + 4, k, :], start=(k == 0), stop=(k == KD - 1))
                last.then_inc(proj, 1)

        @ph.block.vector
        def _(dve):
            st = Steps(dve, steps)
            for t in range(nt):
                dve.wait_ge(proj, t + 1)
                if t >= 2:
                    st.wait()
                nc.vector.tensor_tensor(tmp[:, t % 2], c.psum[:, (t % 4) * 1024:(t % 4 + 1) * 1024],
                                        rows[0 if t < NT_LAT else 1], ALU.mult).then_inc(scaled, 1)
                dve.wait_ge(scaled, t + 1)
                st.do(nc.vector.tensor_tensor(c.xs[:, t], c.xs[:, t], tmp[:, t % 2], ALU.add))


def phase_norm2(c, full):
    nc = c.nc
    tiles = list(range(NT if full else NT_LAT))
    h2N = c.at(80, NT, D)
    high = c.rounded(160, KD, T_ALL)
    rows_a, rows_b = [c.at(136, D), c.at(144, D)], [c.at(140, D), c.at(148, D)]
    with Phase(nc) as ph:
        sq, ms, root, steps = norm_sems(ph)
        ready, turned, kept, low = (ph.sem(s) for s in ("h2_ready", "transposed", "high_kept", "low_kept"))

        def turned_tile(t):
            return c.psum[:, (t % 4) * 1024:(t % 4 + 1) * 1024].rearrange("p (k q) -> p k q", q=P)

        @ph.block.scalar
        def _(act):
            act_norm(c, act, tiles, sq, ms, root)
            for t in tiles:
                act.wait_ge(turned, t + 1)
                nc.scalar.activation(high[:, :, t * P:(t + 1) * P], turned_tile(t), ACT.Copy).then_inc(kept, 1)

        @ph.block.vector
        def _(dve):
            def low_part(t):
                dve.wait_ge(kept, t + 1)
                split(nc, nc.vector, high[:, :, t * P:(t + 1) * P], c.hT_low[:, :, t * P:(t + 1) * P],
                      turned_tile(t)).then_inc(low, 1)

            st = Steps(dve, steps)
            dve_norm(c, dve, st, tiles, sq, ms, root)
            for t in tiles:
                s = 0 if t < NT_LAT else 1
                st.do(nc.vector.scalar_tensor_tensor(out=h2N[:, t], in0=c.xs[:, t], scalar=c.stat[:, 0, t:t + 1], in1=rows_a[s],
                                                     op0=ALU.mult, op1=ALU.mult))
                st.wait()
                nc.vector.tensor_tensor(h2N[:, t], h2N[:, t], rows_b[s], ALU.add).then_inc(ready, 1)
                if t:
                    low_part(t - 1)
            low_part(tiles[-1])

        @ph.block.tensor
        def _(pe):
            for t in tiles:
                pe.wait_ge(ready, t + 1)
                if t >= 4:
                    pe.wait_ge(low, t - 3)
                for k in range(KD):
                    last = nc.tensor.transpose(c.psum[:, (t % 4) * 1024 + k * P:(t % 4) * 1024 + (k + 1) * P],
                                               h2N[:, t, k * P:(k + 1) * P], c.ident[:])
                last.then_inc(turned, 1)


def phase_query(c, layer, full):
    nc, io = c.nc, c.io
    width = T_ALL if full else L_LAT
    nt = width // P
    qT = c.at(104, PH, T_ALL)
    keys = c.at(185, PH, 2 * NK)
    scores = c.at(136, NT * PH + 1, 2 * NK)
    h2_high = c.rounded(160, KD, T_ALL)
    units = [(t, h) for t in range(nt) for h in range(PH)]
    with Phase(nc) as ph:
        ring = SplitRing(c, ph, [(io["wq"][layer][h], KD) for h in range(PH)])
        keys_in, proj, kept, scored, score_kept, pad = (ph.sem(s) for s in (
            "keys_landed", "projected", "query_kept", "scored", "scores_kept", "pad_set"))

        @ph.block.sync
        def _(sp):
            ring.load(sp, proj)
            sp.dma_start(keys, io["keys"][layer]).then_inc(keys_in, 16)

        @ph.block.gpsimd
        def _(pool):
            ring.split(pool)
            pool.wait_ge(proj, PH)
            nc.gpsimd.memset(scores[:, len(units)], 0.0).then_inc(pad, 1)

        @ph.block.tensor
        def _(pe):
            for h in range(PH):
                pe.wait_ge(ring.ready, h + 1)
                if h >= 2:
                    pe.wait_ge(kept, h - 1)
                feature_job(c, ring.parts(h), 2 * (h % 2), width, KD, (h2_high, c.hT_low)).then_inc(proj, 1)
            pe.wait_ge(keys_in, 16)
            pe.wait_ge(kept, PH)
            for u, (t, h) in enumerate(units):
                if u >= 8:
                    pe.wait_ge(score_kept, u // 2 - 3)
                at = 2048 + (u % 8) * 256
                nc.tensor.matmul(c.psum[:, at:at + 256], qT[:, h, t * P:(t + 1) * P], keys[:, h, :],
                                 start=True, stop=True).then_inc(scored, 1)

        @ph.block.scalar
        def _(act):
            ring.round_ahead(act, -1, proj)
            for h in range(PH):
                ring.round_ahead(act, h, proj)
                act.wait_ge(proj, h + 1)
                nc.scalar.activation(qT[:, h, 0:width], c.psum[:, (h % 2) * 1024:(h % 2) * 1024 + width],
                                     ACT.Copy).then_inc(kept, 1)
            for u in range(0, len(units), 2):
                at = 2048 + (u % 8) * 256
                act.wait_ge(scored, u + 2)
                nc.scalar.activation(scores[:, u:u + 2], c.psum[:, at:at + 512].rearrange("p (u n) -> p u n", u=2),
                                     ACT.Copy).then_inc(score_kept, 1)


def phase_experts(c, layer, full):
    nc, io = c.nc, c.io
    nt = NT if full else NT_LAT
    h2N = c.at(80, NT, D)
    gate2 = c.at(128, 2, D)
    scores = c.at(136, NT * PH + 1, 2 * NK)
    slots = [c.at(24 + 8 * i, 2 * D) for i in range(7)] + [c.at(104, 2 * D)]
    junk = c.at(112, 2, D)
    dots, gelus, probs, exps = (c.at(120 + 0.25 * i, 2, TOPK) for i in range(4))
    diag = c.at(121, 4, P)
    top1, top2, topc, e1, e2, iota = (c.at(123 + 0.125 * i, TOPK) for i in range(6))
    idx1, idx2, idxc, hi, lo = (c.at(124 + 0.125 * i, TOPK).bitcast(U32) for i in range(5))
    small = c.at(124.75, 2, 8)
    eidx = c.at(125, 2, TOPK).bitcast(U32)
    sc, cut = c.at(126, 2 * NK), c.at(127, 2 * NK)
    cand, cand_cut, hot1, hot2 = (c.at(185 + i, TOPK, TOPK) for i in range(4))
    upd = c.at(189, D)
    LOWEST = -3.0e38
    table = io["uv"][layer]
    with Phase(nc) as ph:
        landed = [ph.sem(f"slot_landed{s}") for s in range(RING)]
        (iota_d, idx_ready, slot_used, turn, dotted, gelued, diag_ready, psum_used, x_added, exp_ready, exp_done,
         steps, order) = (ph.sem(s) for s in (
             "iota_made", "indices_ready", "slot_used", "turn", "dot_ready", "gelu_done", "diagonal_ready",
             "sum_taken", "x_added", "topk_ready", "exp_done", "dve_steps", "order"))

        @ph.block.gpsimd
        def _(pool):
            nc.gpsimd.iota(iota, pattern=[[1, TOPK]], base=0, channel_multiplier=0,
                           allow_small_or_imprecise_dtypes=True).then_inc(iota_d, 1)
            with pool.Fori(0, nt) as t:
                with pool.Fori(0, PH // 2) as i:
                    for p in range(2):
                        n = t * PH + i * 2 + p
                        pool.wait_ge(idx_ready, n + 1)
                        pool.sem_inc(turn, 1)
                        for k in range(TOPK):
                            pool.wait_ge(slot_used, n * TOPK + (k + 1))
                            pool.sem_inc(turn, 1)
                            nc.gpsimd.indirect_dma_start(
                                out=slots[k % RING], out_offset=None, in_=table,
                                in_offset=bass.IndirectOffsetOnAxis(ap=eidx[:, p, k:k + 1], axis=0)
                            ).then_inc(landed[k % RING], 16)

        @ph.block.tensor
        def _(pe):
            pe.sem_inc(slot_used, RING)
            with pe.Fori(0, nt) as t:
                with pe.Fori(0, PH // 2) as i:
                    for p in range(2):
                        n = t * PH + i * 2 + p
                        pe.wait_ge(psum_used, n + 1)
                        for k in range(TOPK):
                            pe.wait_ge(diag_ready, n * TOPK + (k + 1))
                            for h in range(2):
                                last = nc.tensor.matmul(c.bank(2 * p + h), diag[:, k % 4],
                                                        slots[k % RING][:, D + h * 512:D + (h + 1) * 512],
                                                        start=(k == 0), stop=(k == TOPK - 1))
                            last.then_inc(slot_used, 1)

        @ph.block.scalar
        def _(act):
            def softmax_exp(n, p):
                act.wait_ge(exp_ready, n + 1)
                nc.scalar.activation(exps[:, p], topc, ACT.Exp, bias=small[:, p, 0:1], accum_out=small[:, p, 1:2]).then_inc(exp_done, 1)

            softmax_exp(0, 0)
            with act.Fori(0, nt) as t:
                with act.Fori(0, PH // 2) as i:
                    for p in range(2):
                        n = t * PH + i * 2 + p
                        for k in range(TOPK):
                            act.wait_ge(dotted, n * TOPK + (k + 1))
                            nc.scalar.activation(gelus[:, p, k:k + 1], dots[:, p, k:k + 1], ACT.Gelu).then_inc(gelued, 1)
                            if k == 12:
                                softmax_exp(n + 1, 1 - p)

        @ph.block.vector
        def _(dve):
            base, cnt = [0], [0]

            def do(ins):
                ins.then_inc(steps, 1)
                cnt[0] += 1

            def wait(apart=False):
                dve.wait_ge(steps, base[0] + cnt[0])
                if apart:
                    dve.sem_inc(order, 1)

            def top16(vals, cutv, top, idx):
                do(nc.vector.max(top[:, 0:8], vals))
                wait(True)
                do(nc.vector.max_index(idx[:, 0:8], top[:, 0:8], vals))
                do(nc.vector.match_replace(cutv, top[:, 0:8], vals, LOWEST))
                wait(True)
                do(nc.vector.max(top[:, 8:16], cutv))
                wait(True)
                do(nc.vector.max_index(idx[:, 8:16], top[:, 8:16], cutv))

            def topk_parts(n, q):
                do(nc.vector.tensor_copy(sc, scores[:, bass.ds(n, 1)].rearrange("p a n -> p (a n)")))
                wait(True)
                top16(sc[:, 0:NK], cut[:, 0:NK], top1, idx1)
                yield
                top16(sc[:, NK:], cut[:, NK:], top2, idx2)
                wait()
                yield
                grid = [P, TOPK, TOPK]
                do(nc.vector.tensor_tensor(cand, top1.unsqueeze(2).to_broadcast(grid), top2.unsqueeze(1).to_broadcast(grid), ALU.add))
                wait(True)
                top16(cand.rearrange("p a b -> p (a b)"), cand_cut.rearrange("p a b -> p (a b)"), topc, idxc)
                wait()
                nc.vector.tensor_scalar(small[:, q, 0:1], topc[:, 0:1], -1.0, None, ALU.mult).then_inc(exp_ready, 1)
                yield
                do(nc.vector.tensor_scalar(hi, idxc, 4, None, ALU.logical_shift_right))
                do(nc.vector.tensor_scalar(lo, idxc, 15, None, ALU.bitwise_and))
                wait()
                places = iota.unsqueeze(1).to_broadcast(grid)
                do(nc.vector.tensor_tensor(hot1, places, hi.unsqueeze(2).to_broadcast(grid), ALU.is_equal))
                do(nc.vector.tensor_tensor(hot2, places, lo.unsqueeze(2).to_broadcast(grid), ALU.is_equal))
                wait()
                do(nc.vector.tensor_tensor(hot1, hot1, idx1.unsqueeze(1).to_broadcast(grid), ALU.mult))
                do(nc.vector.tensor_tensor(hot2, hot2, idx2.unsqueeze(1).to_broadcast(grid), ALU.mult))
                wait()
                do(nc.vector.tensor_reduce(e1, hot1, AX.X, ALU.add))
                do(nc.vector.tensor_reduce(e2, hot2, AX.X, ALU.add))
                wait()
                nc.vector.scalar_tensor_tensor(out=eidx[:, q], in0=e1, scalar=float(NK), in1=e2, op0=ALU.mult,
                                               op1=ALU.add).then_inc(idx_ready, 1)
                yield
                dve.wait_ge(exp_done, n + 1)
                do(nc.vector.reciprocal(small[:, q, 2:3], small[:, q, 1:2]))
                wait()
                do(nc.vector.tensor_scalar(probs[:, q], exps[:, q], small[:, q, 2:3], None, ALU.mult))
                wait()

            def dot(n, t, p, k):
                if k >= 2:
                    dve.wait_ge(dotted, n * TOPK + (k - 1))
                dve.wait_ge(landed[k % RING], n * 32 + 16 * (k // RING + 1))
                nc.vector.scalar_tensor_tensor(out=junk[:, k % 2], in0=slots[k % RING][:, 0:D], scalar=1.0,
                                               in1=h2N[:, bass.ds(t, 1)].rearrange("p a n -> p (a n)"), op0=ALU.mult,
                                               op1=ALU.mult, accum_out=dots[:, p, k:k + 1]).then_inc(dotted, 1)

            def weigh(n, p, k):
                dve.wait_ge(gelued, n * TOPK + (k + 1))
                dve.wait_ge(slot_used, n * TOPK + (k + RING - 3))
                nc.vector.tensor_scalar(diag[:, k % 4], c.ident[:], gelus[:, p, k:k + 1], probs[:, p, k:k + 1], ALU.mult,
                                        ALU.mult).then_inc(diag_ready, 1)

            dve.sem_inc(psum_used, 2)
            dve.sem_inc(x_added, 1)
            dve.wait_ge(iota_d, 1)
            for _ in topk_parts(0, 0):
                pass
            per_unit = cnt[0]
            with dve.Fori(0, nt) as t:
                with dve.Fori(0, PH // 2) as i:
                    for p in range(2):
                        n = t * PH + i * 2 + p
                        base[0], cnt[0] = (n + 1) * per_unit, 0
                        parts = topk_parts(n + 1, 1 - p)
                        for k in range(TOPK):
                            dot(n, t, p, k)
                            if k >= 1:
                                weigh(n, p, k - 1)
                            if k in (3, 5, 7, 9, 14):
                                next(parts, None)
                        weigh(n, p, TOPK - 1)
                        assert cnt[0] == per_unit
                        dve.wait_ge(slot_used, n * TOPK + (TOPK + RING))
                        dve.wait_ge(x_added, n + 1)
                        nc.vector.tensor_tensor(upd, c.psum[:, 1024 * p:1024 * p + D],
                                                gate2[:, bass.ds(t // NT_LAT, 1)].rearrange("p a n -> p (a n)"),
                                                ALU.mult).then_inc(psum_used, 1)
                        dve.wait_ge(psum_used, n + 3)
                        x = c.xs[:, bass.ds(t, 1)].rearrange("p a n -> p (a n)")
                        nc.vector.tensor_tensor(x, x, upd, ALU.add).then_inc(x_added, 1)


def phase_final(c, out):
    nc, io = c.nc, c.io
    tiles = list(range(NT_LAT))
    gain, y = c.at(136, D), c.at(140, NT_LAT, D)
    with Phase(nc) as ph:
        sq, ms, root, steps = norm_sems(ph)
        gain_in, ready, stored = (ph.sem(s) for s in ("gain_landed", "rows_ready", "rows_stored"))

        @ph.block.scalar
        def _(act):
            act_norm(c, act, tiles, sq, ms, root)

        @ph.block.vector
        def _(dve):
            st = Steps(dve, steps)
            dve_norm(c, dve, st, tiles, sq, ms, root)
            dve.wait_ge(gain_in, 16)
            for t in tiles:
                nc.vector.scalar_tensor_tensor(out=y[:, t], in0=c.xs[:, t], scalar=c.stat[:, 0, t:t + 1], in1=gain,
                                               op0=ALU.mult, op1=ALU.mult).then_inc(ready, 1)

        @ph.block.sync
        def _(sp):
            sp.dma_start(gain, io["g_final"].to_broadcast([P, D])).then_inc(gain_in, 16)
            for t in tiles:
                sp.wait_ge(ready, t + 1)
                sp.dma_start(out[t * P:(t + 1) * P, :], y[:, t]).then_inc(stored, 16)
            sp.wait_ge(stored, 16 * NT_LAT)


def build(nc, io, out):
    with ExitStack() as ctx:
        c = Chip(nc, ctx, io)
        phase_load(c)
        for layer in range(DEPTH):
            full = layer < DEPTH - 1
            streams = range(2 if full else 1)
            phase_mod(c, layer)
            phase_norm1(c, layer, list(range(NT)))
            phase_qkv(c, layer, full)
            phase_attention(c, full)
            phase_conv_branches(c, layer, full)
            for length in (L_LAT, L_CTX)[:2 if full else 1]:
                phase_filter_mlp(c, layer, length)
                for order in range(2):
                    phase_spectrum(c, layer, length, order)
                    phase_long_conv(c, length, order)
            col = lambda base, s: lambda k: c.mod[:, base + k, s:s + 1]
            phase_merge(c, layer, full)
            phase_rows(c, [(col(GT1, s), c.at(160 + 4 * s, D)) for s in streams])
            phase_out(c, layer, full)
            rows = []
            for s in streams:
                rows += [((lambda s: lambda k: c.ab[:, 1, k, s:s + 1])(s), c.at(136 + 8 * s, D)),
                         (col(SH2, s), c.at(140 + 8 * s, D)), (col(GT2, s), c.at(128 + 4 * s, D))]
            phase_rows(c, rows)
            phase_norm2(c, full)
            phase_query(c, layer, full)
            phase_experts(c, layer, full)
        phase_final(c, out)


def blocks(w):
    n_l, k, n = w.shape
    return np.ascontiguousarray(w.reshape(n_l, k // P, P, n // P, P).transpose(0, 3, 2, 1, 4))


def mod_blocks(w):
    w = w.reshape(w.shape[0], 2, KD // 2, P, -1, 512)
    return np.ascontiguousarray(w.transpose(0, 4, 1, 3, 2, 5)).reshape(w.shape[0], -1, P, KD // 2 * 512)


def columns(v):
    v = v.reshape(v.shape[0], -1, P)
    return v.transpose(0, 2, 1)


def layouts(a):
    a = {k: np.asarray(v) for k, v in a.items()}
    n_l = DEPTH
    tok = lambda v: np.ascontiguousarray(v.reshape(-1, P, D).transpose(1, 0, 2))
    fil = np.zeros((n_l, P, 4), np.float32)
    for i, k in enumerate(("hy_b1", "hy_f1", "hy_b2", "hy_f2")):
        fil[:, :FH, i] = a[k]
    keys = np.zeros((n_l, 2, DK, PH, 2, NK), np.float32)
    for p in range(2):
        keys[:, p, :, :, p, :] = a["peer_subkeys"][:, :, p].transpose(0, 3, 1, 2)
    out = {
        "x": tok(a["x"]), "ctx": tok(a["ctx"]),
        "cond": np.ascontiguousarray(np.stack([a["c"].reshape(KD, P).T, a["c_ctx"].reshape(KD, P).T], axis=2)),
        "rope": rope_table().reshape(P, NT_LAT, 2, 2, 16), "consts": shape_constants(),
        "cols": np.ascontiguousarray(np.concatenate(
            [columns(a["b_mod"]), columns(a["g_norm1"]), columns(a["g_norm2"]), columns(a["sc_conv_w"]),
             columns(a["hy_conv_w"]), columns(a["hy_conv_b"]), fil], axis=2)),
        "w_mod": mod_blocks(a["w_mod"]), "w_in": blocks(a["w_in"]), "w_out": blocks(a["w_out"]),
        "w_br": np.concatenate([blocks(a[k]) for k in ("w_br_att", "w_br_sc", "w_br_hy")], axis=1),
        "wq": blocks(a["peer_wq"]),
        "keys": keys.reshape(n_l, P, PH, 2 * NK),
        "gains": np.ascontiguousarray(np.concatenate([a["q_gain"]] * HEADS + [a["k_gain"]] * KV_HEADS, axis=1)),
        "hy_w1": a["hy_w1"], "hy_w2": a["hy_w2"], "hy_w3": a["hy_w3"],
        "hy_decay": a["hy_decay"], "hy_bias": a["hy_bias"],
        "g_final": a["g_final"].reshape(1, D),
    }
    for length in (L_LAT, L_CTX):
        out[f"feat{length}"] = filter_features(length)
        out[f"dft{length}"] = dft_tables(length)
    for layer in range(n_l):
        out[f"uv{layer}"] = np.concatenate([a["peer_u"][layer], a["peer_v"][layer]], axis=1)
    return out


def kernel(**inputs):
    import concourse.bacc as bacc
    from concourse.bass_utils import run_bass_kernel_spmd

    nc = bacc.Bacc("TRN2", target_bir_lowering=False, num_devices=1)
    arrays, io = {}, {}
    for name, a in layouts(inputs).items():
        arrays[f"in_{name}"] = a
        io[name] = nc.dram_tensor(f"in_{name}", a.shape, mybir.dt.from_np(a.dtype), kind="ExternalInput").ap()
    io["uv"] = [io.pop(f"uv{layer}") for layer in range(DEPTH)]
    out = nc.dram_tensor("out", (L_LAT, D), F32, kind="ExternalOutput").ap()
    build(nc, io, out)
    r = run_bass_kernel_spmd(nc, [arrays], core_ids=[0])
    return r.results[0]["out"].reshape(1, L_LAT, D)
```

```python
import math
from contextlib import ExitStack

import numpy as np

import concourse.bass as bass
from concourse import mybir

F32 = mybir.dt.float32
F32R = mybir.dt.float32r
U32 = mybir.dt.uint32
I32 = mybir.dt.int32
ALU = mybir.AluOpType
ACT = mybir.ActivationFunctionType
AX = mybir.AxisListType

P = 128
D = 1024
DEPTH = 2
L_LAT, L_CTX = 512, 256
T_ALL = L_LAT + L_CTX
KD = D // P
NT_LAT, NT_CTX = L_LAT // P, L_CTX // P
NT = NT_LAT + NT_CTX
GRID_W = 64
HEADS, KV_HEADS, HD = 8, 2, 64
PAIRS = HEADS // 2
W_BR = 512
KB_BR = W_BR // P
EPS = 1e-6
FH = 64
BANDS = 16
EMB = 1 + 2 * BANDS
B_Q, B_K, B_V = 0, 4, 5
B_SC, B_HY, B_GATE = 6, 18, 30
N_IN = 54
SH1, SC1, GT1, SH2, SC2, GT2 = (KD * i for i in range(6))
N_MOD = 6 * KD
PH, NK, DK, TOPK = 8, 128, 64, 16
N_EXP = NK * NK
RING = 8
C_BMOD, C_G1, C_G2 = 0, N_MOD, N_MOD + KD
C_SCW = C_G2 + KD
C_HYW = C_SCW + 3 * KB_BR
C_HYB = C_HYW + 3 * 3 * KB_BR
C_FIL = C_HYB + 3 * KB_BR
N_COLS = C_FIL + 4

TWO_PI = 2.0 * math.pi
PI_HI = 6.28125
PI_MID = float(np.float32(np.frombuffer(np.array([np.float32(TWO_PI - PI_HI)]).view(np.uint32) & np.uint32(0xFFFFF000), np.float32)[0]))
PI_LO = TWO_PI - PI_HI - PI_MID
ROUND = 1.5 * 2.0 ** 23
PI_F32 = float(np.nextafter(np.float32(math.pi), np.float32(0)))


def k_tiles(table):
    rows, n = table.shape
    return table.reshape(rows // P, P, n).transpose(1, 0, 2).reshape(P, -1)


def dft_tables(length):
    half = length // 2
    freq = np.concatenate([np.arange(0, length, 2), np.arange(1, length, 2)])
    ang = np.pi * ((2 * np.arange(half)[:, None] + 1) * freq[None, :] % (4 * length)) / (2 * length)
    cos, sin = np.cos(ang), -np.sin(ang)
    sin[:, 0] = -(-1.0) ** np.arange(half)
    ang = np.pi * ((np.arange(length)[:, None] * freq[None, :]) % (2 * length)) / length
    parts = [cos, sin, cos.T, sin.T, np.cos(ang), -np.sin(ang)]
    return np.ascontiguousarray(np.concatenate([k_tiles(a) for a in parts], axis=1).astype(np.float32))


def filter_features(length):
    t = np.linspace(0.0, 1.0, length, dtype=np.float32)[:, None]
    w = (2.0 * math.pi * np.arange(length, dtype=np.float32)[:, None] / length).astype(np.float32)
    bands = np.linspace(1e-4, BANDS - 1, BANDS, dtype=np.float32)[None, :]
    z = np.concatenate([t, np.cos(bands * w), -np.sin(bands * w)], axis=-1)
    return np.ascontiguousarray(z.T.astype(np.float32))


def rope_table():
    pos = np.arange(L_LAT)
    inv = np.power(np.float32(10000.0), -np.arange(0, 32, 2, dtype=np.float32) / 32)
    ang = np.stack([(pos // GRID_W)[:, None] * inv, (pos % GRID_W)[:, None] * inv], axis=1)
    t = np.stack([np.cos(ang), np.sin(ang)], axis=1).reshape(NT_LAT, P, 64)
    return np.ascontiguousarray(t.transpose(1, 0, 2).reshape(P, NT_LAT * 64).astype(np.float32))


def shape_constants():
    out = np.zeros((P, 8), np.float32)
    for a, length in ((0, L_LAT), (4, L_CTX)):
        t = np.linspace(0.0, 1.0, length, dtype=np.float32).reshape(-1, P).T
        out[:, a:a + t.shape[1]] = -t
    w = np.zeros((P, 2), np.float32)
    w[:, 0], w[:, 1] = 1.0 / L_LAT, 1.0 / L_CTX
    w[0] *= 0.5
    sign = np.where(np.arange(P) % 2, -1.0, 1.0).astype(np.float32)[:, None]
    return np.concatenate([out, w, sign], axis=1)


class Steps:

    def __init__(self, eng, sem):
        self.eng, self.sem, self.n = eng, sem, 0

    def do(self, ins):
        ins.then_inc(self.sem, 1)
        self.n += 1
        return self.n

    def wait(self, n=None):
        self.eng.wait_ge(self.sem, self.n if n is None else n)


class Phase:

    count = 0

    def __init__(self, nc):
        self.nc, self.sems = nc, []
        Phase.count += 1
        self.tag = f"p{Phase.count}"

    def sem(self, name):
        s = self.nc.alloc_semaphore(f"{name}_{self.tag}")
        self.sems.append(s)
        return s

    def __enter__(self):
        self.stack = ExitStack()
        self.block = self.stack.enter_context(self.nc.Block())
        return self

    def __exit__(self, *err):
        self.stack.__exit__(*err)
        if err[0] is None:
            self.nc.clear_and_free_semaphores(self.sems)
            self.nc.all_engine_barrier(sem_only=True)


class Chip:

    def __init__(self, nc, ctx, io):
        self.nc, self.io = nc, io
        self.arena_at, self.views = (nc.sbuf_base + 31) // 32 * 32, {}
        self.arena = ctx.enter_context(nc.sbuf_tensor("arena", [P, 201 * 256], F32))
        sb = lambda n, s: ctx.enter_context(nc.sbuf_tensor(n, s, F32))
        self.ident = sb("ident", [P, P])
        self.ones = sb("ones", [P, P])
        self.rope = sb("rope", [P, NT_LAT, 2, 2, 16])
        self.cond = sb("cond", [P, KD, 2])
        self.cond4 = ctx.enter_context(nc.sbuf_tensor("cond4", [P, KD, 4], F32R))
        self.cols = sb("cols", [P, N_COLS])
        self.consts = sb("consts", [P, 11])
        self.mod = sb("mod", [P, N_MOD, 2])
        self.ab = sb("ab", [P, 2, KD, 2])
        self.stat = sb("stat", [P, 2, 16])
        self.psum = ctx.enter_context(nc.psum_tensor("psum", [P, 8 * 512], F32))
        self.xs = self.at(0, NT, D)
        self.hT = self.own(24, KD, T_ALL)
        self.hT_low = self.rounded(24, KD, T_ALL)
        self.hT_high = self.rounded(176, KD, T_ALL)

    def at(self, kib, *shape):
        n = int(np.prod(shape))
        v = self.arena[:, int(kib * 256):int(kib * 256) + n]
        return self._shaped(v, shape)

    def own(self, kib, *shape, dtype=F32):
        key = (kib, shape, dtype == F32R)
        if key not in self.views:
            self.views[key] = self.nc.alloc_sbuf_tensor_at(
                f"view{len(self.views)}_at_{int(kib)}", [P, int(np.prod(shape))], dtype,
                offset=self.arena_at + int(kib * 1024))
        return self._shaped(self.views[key][:], shape)

    def rounded(self, kib, *shape):
        return self.own(kib, *shape, dtype=F32R)

    def warm_up(self, ph, pe, times, bank=7):
        warmed = ph.sem("warmed")
        for _ in range(times):
            last = self.nc.tensor.matmul(self.psum[:, bank * 512:bank * 512 + P], self.ident[:], self.ones[:],
                                         start=True, stop=True)
        last.then_inc(warmed, 1)
        pe.wait_ge(warmed, 1)

    @staticmethod
    def _shaped(v, shape):
        if len(shape) == 2:
            return v.rearrange("p (a b) -> p a b", a=shape[0])
        if len(shape) == 3:
            return v.rearrange("p (a b c) -> p a b c", a=shape[0], b=shape[1])
        return v

    def bank(self, b, width=512, parts=P):
        return self.psum[0:parts, b * 512:b * 512 + width]


def phase_load(c):
    nc, io = c.nc, c.io
    with Phase(nc) as ph:
        made, made_ones, cond_in, cond_done = (ph.sem(s) for s in (
            "identity_made", "ones_made", "cond_landed", "cond_done"))

        @ph.block.sync
        def _(sp):
            sp.dma_start(c.cond[:], io["cond"]).then_inc(cond_in, 16)

        @ph.block.gpsimd
        def _(pool):
            nc.gpsimd.memset(c.ident[:], 0.0).then_inc(made, 1)
            pool.wait_ge(made, 1)
            nc.gpsimd.affine_select(out=c.ident[:], in_=c.ident[:], compare_op=ALU.not_equal, fill=1.0,
                                    base=0, pattern=[[-1, P]], channel_multiplier=1).then_inc(made, 1)

        @ph.block.vector
        def _(dve):
            nc.vector.memset(c.ones[:], 1.0).then_inc(made_ones, 1)

        @ph.block.scalar
        def _(act):
            act.wait_ge(cond_in, 16)
            nc.scalar.activation(c.cond[:], c.cond[:], ACT.Silu).then_inc(cond_done, 1)


def split(nc, eng, hi, lo, x):
    return eng.tensor_tensor(lo, x, hi.bitcast(F32), ALU.subtract)


def products(a, b):
    return ((a[0], b[0]), (a[0], b[1]), (a[1], b[0]))


class SplitRing:

    def __init__(self, c, ph, blocks, at=48, slots=4, ahead=0):
        self.c, self.blocks, self.slots, self.ahead = c, blocks, slots, ahead
        self.raw, self.low = c.own(at, slots, KD, P), c.rounded(at, slots, KD, P)
        self.high = c.rounded(at + 4 * slots, slots, KD, P)
        self.landed = [ph.sem(f"w_landed{s}") for s in range(slots)]
        self.high_ready, self.ready = ph.sem("w_high_ready"), ph.sem("w_split")

    def load(self, sp, used):
        for n in range(self.ahead, len(self.blocks)):
            block, kt = self.blocks[n]
            if n >= self.slots:
                sp.wait_ge(used, n - self.slots + 1)
            sp.dma_start(self.raw[:, n % self.slots, 0:kt], block).then_inc(self.landed[n % self.slots], 16)

    def _high(self, eng, op, n):
        s, kt = n % self.slots, self.blocks[n][1]
        eng.wait_ge(self.landed[s], 16 * ((n - self.ahead) // self.slots + 1))
        op(self.high[:, s, 0:kt], self.raw[:, s, 0:kt]).then_inc(self.high_ready, 1)

    def round_one(self, act, n):
        self._high(act, lambda out, x: self.c.nc.scalar.activation(out, x, ACT.Copy), n)

    def round_ahead(self, act, done, used):
        if done >= 0:
            act.wait_ge(used, done + 1)
        for n in range(self.slots) if done < 0 else (done + self.slots,):
            if self.ahead <= n < len(self.blocks):
                self.round_one(act, n)

    def split(self, eng, engine=None, blocks=None):
        nc = self.c.nc
        for n in range(self.ahead, len(self.blocks)) if blocks is None else blocks:
            s, kt = n % self.slots, self.blocks[n][1]
            eng.wait_ge(self.high_ready, n - self.ahead + 1)
            split(nc, engine or nc.gpsimd, self.high[:, s, 0:kt], self.low[:, s, 0:kt],
                  self.raw[:, s, 0:kt]).then_inc(self.ready, 1)

    def prepare(self, pool):
        for n in range(len(self.blocks)):
            self._high(pool, self.c.nc.gpsimd.tensor_copy, n)
            self.split(pool, blocks=(n,))

    def wait(self, pe, n):
        if n >= self.ahead:
            pe.wait_ge(self.ready, n - self.ahead + 1)

    def parts(self, n):
        return self.high[:, n % self.slots], self.low[:, n % self.slots]


def filter_hidden(c):
    return c.at(107, T_ALL)


class FilterMlp:

    def __init__(self, c, ph, layer, width):
        self.c, self.layer, self.width = c, layer, width
        self.z, self.h1, self.h2 = c.at(160, T_ALL), c.at(163, T_ALL), filter_hidden(c)
        self.a, self.r = c.at(166, 2, T_ALL), c.at(172, T_ALL)
        self.w1, self.w2 = c.at(176, FH), c.at(176.25, FH)
        self.landed, self.summed, self.shifted, self.reduced, self.sined, self.steps = (ph.sem(s) for s in (
            "filter_landed", "filter_summed", "angles_ready", "angles_reduced", "sines", "pool_steps"))

    def sync(self, sp):
        io, layer = self.c.io, self.layer
        sp.dma_start(self.z[0:EMB, :], io["feat"]).then_inc(self.landed, 16)
        sp.dma_start(self.w1[0:EMB, :], io["hy_w1"][layer]).then_inc(self.landed, 16)
        sp.dma_start(self.w2[0:FH, :], io["hy_w2"][layer]).then_inc(self.landed, 16)

    def tensor(self, pe, i):
        if i == 0:
            pe.wait_ge(self.landed, 48)
            w, x = self.w1[0:EMB, :], self.z[0:EMB, :]
        else:
            pe.wait_ge(self.sined, 1)
            w, x = self.w2[0:FH, :], self.h1[0:FH, :]
        for lo, hi in ((0, L_LAT), (L_LAT, self.width)):
            if lo < hi:
                last = self.c.nc.tensor.matmul(self.c.psum[0:FH, (2 + 2 * i) * 512 + lo:(2 + 2 * i) * 512 + hi], w,
                                               x[:, lo:hi], start=True, stop=True)
        last.then_inc(self.summed, 1)

    def vector(self, dve, i):
        c, b = self.c, C_FIL + 2 * i
        dve.wait_ge(self.summed, i + 1)
        at = (2 + 2 * i) * 512
        c.nc.vector.tensor_scalar(self.a[0:FH, i, 0:self.width], c.psum[0:FH, at:at + self.width], c.cols[0:FH, b:b + 1],
                                  c.cols[0:FH, b + 1:b + 2], ALU.add, ALU.mult).then_inc(self.shifted, 1)

    def gpsimd(self, pool):
        nc, st = self.c.nc, Steps(pool, self.steps)
        r, w = self.r[0:FH, 0:self.width], slice(0, self.width)
        for i in range(2):
            a, part = self.a[0:FH, i, w], self.z[0:FH, w]
            pool.wait_ge(self.shifted, i + 1)
            if i:
                pool.wait_ge(self.sined, 1)
            st.do(nc.gpsimd.tensor_scalar(r, a, 1.0 / TWO_PI, ROUND, ALU.mult, ALU.add))
            st.wait()
            st.do(nc.gpsimd.tensor_scalar(r, r, ROUND, None, ALU.subtract))
            st.wait()
            for piece in (PI_HI, PI_MID, PI_LO):
                st.do(nc.gpsimd.tensor_scalar(part, r, piece, None, ALU.mult))
                st.wait()
                st.do(nc.gpsimd.tensor_tensor(a, a, part, ALU.subtract))
                st.wait()
            nc.gpsimd.tensor_scalar(r, a, PI_F32, -PI_F32, ALU.min, ALU.max).then_inc(self.reduced, 1)

    def scalar(self, act, i):
        act.wait_ge(self.reduced, i + 1)
        self.c.nc.scalar.activation((self.h1, self.h2)[i][0:FH, 0:self.width], self.r[0:FH, 0:self.width],
                                    ACT.Sin).then_inc(self.sined, 1)


def phase_mod(c, layer, full):
    nc, io = c.nc, c.io
    HALF = KD // 2
    RAW = 7
    chunks = 6 * D // 512
    raw = c.own(24, RAW, HALF * 512)
    hi = c.rounded(80, 2, HALF * 512)
    lo = c.rounded(140, 2, HALF * 512)
    rows = c.at(178, 2, 512)
    sel = c.at(182, 2)
    xn, junk = c.at(116, NT, D), c.at(184, 2, D)
    SQUARES = 16
    with Phase(nc) as ph:
        sq, ms, root = (ph.sem(s) for s in ("squares_summed", "means_ready", "roots_ready"))
        x_in, xn_ready = ph.sem("x_landed"), ph.sem("xn_ready")
        x_loads = [] if layer else [(c.xs[:, 0:NT_LAT, :], io["x"]), (c.xs[:, NT_LAT:NT, :], io["ctx"]),
                                    (c.rope[:], io["rope"]), (c.consts[:], io["consts"])]
        mlp = FilterMlp(c, ph, layer, T_ALL if full else L_LAT)
        w_landed = [ph.sem(f"w_landed{s}") for s in range(RAW)]
        w_split, hi_ready, halves_done, kept, turned, cols_in, cond_split, dve_done = (ph.sem(s) for s in (
            "weights_split", "high_ready", "halves_done", "rows_kept", "rows_turned", "cols_landed",
            "cond_split", "dve_steps"))

        @ph.block.sync
        def _(sp):
            sp.dma_start(c.cols[:], io["cols"][layer]).then_inc(cols_in, 16)
            mlp.sync(sp)
            for n in range(2 * chunks):
                if n >= RAW:
                    sp.wait_ge(w_split, n - RAW + 1)
                sp.dma_start(raw[:, n % RAW], io["w_mod"][layer][n]).then_inc(w_landed[n % RAW], 16)
                if n >= RAW and x_loads:
                    sp.dma_start(*x_loads.pop(0)).then_inc(x_in, 16)

        @ph.block.scalar
        def _(act):
            def keep(q):
                act.wait_ge(halves_done, 2 * q + 2)
                if q >= 2:
                    act.wait_ge(turned, q - 1)
                nc.scalar.activation(rows[0:4, q % 2], c.bank(q % 2, 512, 4), ACT.Copy).then_inc(kept, 1)

            for n in range(2 * chunks):
                act.wait_ge(w_landed[n % RAW], 16 * (n // RAW + 1))
                if n >= 2:
                    act.wait_ge(halves_done, n - 1)
                nc.scalar.activation(hi[:, n % 2], raw[:, n % RAW], ACT.Copy).then_inc(hi_ready, 1)
                if n >= 3 and n % 2:
                    keep((n - 3) // 2)
                if SQUARES <= n < SQUARES + NT:
                    t = n - SQUARES
                    if layer == 0 and t == 0:
                        act.wait_ge(x_in, 64)
                    if t >= 2:
                        act.wait_ge(sq, t - 1)
                    nc.scalar.activation(junk[:, t % 2], c.xs[:, t], ACT.Square,
                                         accum_out=c.stat[:, 0, t:t + 1]).then_inc(sq, 1)
                if n == SQUARES + NT + 1:
                    act.wait_ge(ms, 1)
                    nc.scalar.activation(c.stat[:, 1, 0:NT], c.stat[:, 1, 0:NT], ACT.Sqrt).then_inc(root, 1)
                if n in (12, 23):
                    mlp.scalar(act, n // 23)
            keep(chunks - 1)

        @ph.block.gpsimd
        def _(pool):
            mlp.gpsimd(pool)

        @ph.block.tensor
        def _(pe):
            def turn(q):
                pe.wait_ge(kept, q + 1)
                for j in range(4):
                    at = 7 * 512 + 8 * q + 2 * j
                    last = nc.tensor.matmul(c.psum[:, at:at + 2], rows[0:4, q % 2, j * P:(j + 1) * P], sel[0:4],
                                            start=True, stop=True)
                last.then_inc(turned, 1)

            pe.wait_ge(cond_split, 4)
            for n in range(2 * chunks):
                q, half = n // 2, n % 2
                if half == 0 and q >= 2:
                    pe.wait_ge(kept, q - 1)
                for part, ready in ((hi, hi_ready), (lo, w_split)):
                    pe.wait_ge(ready, n + 1)
                    for k in range(HALF):
                        last = nc.tensor.matmul(c.bank(q % 2, 512, 4), c.cond4[:, half * HALF + k],
                                                part[:, n % 2, k * 512:(k + 1) * 512],
                                                start=(half == 0 and part is hi and k == 0),
                                                stop=(half == 1 and part is lo and k == HALF - 1))
                last.then_inc(halves_done, 1)
                if n in (2, 13):
                    mlp.tensor(pe, n // 13)
                if n >= 3 and half:
                    turn((n - 3) // 2)
            turn(chunks - 1)

        @ph.block.vector
        def _(dve):
            st = Steps(dve, dve_done)
            nc.vector.tensor_copy(c.cond4[:, :, 0:2], c.cond[:]).then_inc(cond_split, 1)
            dve.wait_ge(cond_split, 1)
            split(nc, nc.vector, c.cond4[:, :, 0:2], c.cond4[:, :, 2:4], c.cond[:]).then_inc(cond_split, 1)
            nc.vector.tensor_copy(sel[0:4], c.ident[0:4, 0:2]).then_inc(cond_split, 1)
            dve.wait_ge(cond_split, 3)
            nc.vector.tensor_tensor(sel[0:4], sel[0:4], c.ident[0:4, 2:4], ALU.add).then_inc(cond_split, 1)
            for n in range(2 * chunks):
                dve.wait_ge(hi_ready, n + 1)
                split(nc, nc.vector, hi[:, n % 2], lo[:, n % 2], raw[:, n % RAW]).then_inc(w_split, 1)
                if n == 3:
                    dve.wait_ge(cols_in, 16)
                if n in (3, 14):
                    mlp.vector(dve, n // 14)
                if n == SQUARES + NT:
                    dve.wait_ge(sq, NT)
                    nc.vector.tensor_scalar(c.stat[:, 1, 0:NT], c.stat[:, 0, 0:NT], 1.0 / D, EPS, ALU.mult,
                                            ALU.add).then_inc(ms, 1)
            dve.wait_ge(root, 1)
            st.do(nc.vector.reciprocal(c.stat[:, 0, 0:NT], c.stat[:, 1, 0:NT]))
            st.wait()
            for t in range(NT):
                nc.vector.tensor_scalar(xn[:, t], c.xs[:, t], c.stat[:, 0, t:t + 1], None, ALU.mult).then_inc(xn_ready, 1)
            dve.wait_ge(turned, chunks)
            st.do(nc.vector.tensor_tensor(
                c.mod[:], c.psum[:, 7 * 512:7 * 512 + 2 * N_MOD].rearrange("p (j s) -> p j s", s=2),
                c.cols[:, C_BMOD:C_BMOD + N_MOD].unsqueeze(2).to_broadcast([P, N_MOD, 2]), ALU.add))
            st.wait()
            for n, (sc, g) in enumerate(((SC1, C_G1), (SC2, C_G2))):
                st.do(nc.vector.scalar_tensor_tensor(
                    out=c.ab[:, n], in0=c.mod[:, sc:sc + KD], scalar=1.0,
                    in1=c.cols[:, g:g + KD].unsqueeze(2).to_broadcast([P, KD, 2]), op0=ALU.add, op1=ALU.mult))


def norm_sems(ph):
    return [ph.sem(s) for s in ("squares_summed", "means_ready", "roots_ready", "dve_steps")]


def act_norm(c, act, tiles, sq, ms, root, between=None):
    nc, junk = c.nc, c.at(185, 2, D)
    for i, t in enumerate(tiles):
        if i >= 2:
            act.wait_ge(sq, i - 1)
        nc.scalar.activation(junk[:, i % 2], c.xs[:, t], ACT.Square, accum_out=c.stat[:, 0, i:i + 1]).then_inc(sq, 1)
    if between is not None:
        between(act)
    act.wait_ge(ms, 1)
    nc.scalar.activation(c.stat[:, 1, 0:len(tiles)], c.stat[:, 1, 0:len(tiles)], ACT.Sqrt).then_inc(root, 1)


def dve_norm(c, dve, st, tiles, sq, ms, root):
    nc = c.nc
    n = len(tiles)
    dve.wait_ge(sq, n)
    nc.vector.tensor_scalar(c.stat[:, 1, 0:n], c.stat[:, 0, 0:n], 1.0 / D, EPS, ALU.mult, ALU.add).then_inc(ms, 1)
    dve.wait_ge(root, 1)
    st.do(nc.vector.reciprocal(c.stat[:, 0, 0:n], c.stat[:, 1, 0:n]))
    st.wait()


def qkv_ring(c, ph, layer):
    return SplitRing(c, ph, [(c.io["w_in"][layer][b], KD) for b in range(6)], slots=6)


def phase_norm1(c, layer):
    nc = c.nc
    xn = c.at(116, NT, D)
    jobs = [(k, s) for k in range(KD) for s in range(2)]
    span = [slice(0, L_LAT), slice(L_LAT, T_ALL)]
    with Phase(nc) as ph:
        ring = qkv_ring(c, ph, layer)
        turned, high, value, low = (ph.sem(s) for s in (
            "transposed", "high_ready", "value_ready", "low_ready"))

        @ph.block.sync
        def _(sp):
            ring.load(sp, None)

        @ph.block.gpsimd
        def _(pool):
            ring.split(pool, blocks=range(4))

        @ph.block.scalar
        def _(act):
            for j, (k, s) in enumerate(jobs):
                act.wait_ge(value, j + 1)
                nc.scalar.activation(c.hT_high[:, k, span[s]], c.hT[:, k, span[s]], ACT.Copy).then_inc(high, 1)
                if j % 2 and j // 2 < 6:
                    ring.round_one(act, j // 2)

        @ph.block.vector
        def _(dve):
            def low_part(j):
                k, s = jobs[j]
                dve.wait_ge(high, j + 1)
                split(nc, nc.vector, c.hT_high[:, k, span[s]], c.hT_low[:, k, span[s]], c.hT[:, k, span[s]]).then_inc(low, 1)

            for j, (k, s) in enumerate(jobs):
                dve.wait_ge(turned, j + 1)
                nc.vector.tensor_scalar(c.hT[:, k, span[s]], c.bank(j % 8, (L_LAT, L_CTX)[s]), c.ab[:, 0, k, s:s + 1],
                                        c.mod[:, SH1 + k, s:s + 1], ALU.mult, ALU.add).then_inc(value, 1)
                if j:
                    low_part(j - 1)
            low_part(len(jobs) - 1)
            ring.split(dve, nc.vector, range(4, 6))

        @ph.block.tensor
        def _(pe):
            for j, (k, s) in enumerate(jobs):
                if j >= 8:
                    pe.wait_ge(value, j - 7)
                for i, t in enumerate(range(NT_LAT) if s == 0 else range(NT_LAT, NT)):
                    last = nc.tensor.transpose(c.psum[:, (j % 8) * 512 + i * P:(j % 8) * 512 + (i + 1) * P],
                                               xn[:, t, k * P:(k + 1) * P], c.ident[:])
                last.then_inc(turned, 1)


def phase_qkv(c, layer, full):
    nc, io = c.nc, c.io
    qT, kT, vN = c.at(116, PAIRS, T_ALL), c.at(128, KV_HEADS, T_ALL), c.at(134, NT, P)
    sqb = c.at(143, 2, 640)
    qn = c.at(148, 2, 640)
    qr = c.at(153, 2, 640)
    kd = c.at(158, 2, 256)
    tmp = c.at(160, 4, 320)
    gain = c.at(166, 640)
    w = c.rounded(72, 6, KD, P), c.rounded(48, 6, KD, P)
    ssq = c.at(169, 2, 16)
    rr = c.at(169.5, 2, 16)
    tiles = list(range(NT))
    with Phase(nc) as ph:
        gain_in, proj, sq_d, ms, root, vd, steps, ready, turned, evac = (ph.sem(s) for s in (
            "gain_landed", "projected", "squared", "means_ready", "roots_ready", "v_kept",
            "dve_steps", "qk_ready", "transposed", "evacuated"))
        qk_read = ph.sem("qk_psum_read")

        def q_cols(t):
            return (0 if t < NT_LAT or full else 512, 640)

        @ph.block.sync
        def _(sp):
            sp.dma_start(gain, io["gains"][layer:layer + 1].to_broadcast([P, 640])).then_inc(gain_in, 16)

        @ph.block.tensor
        def _(pe):
            def project(t):
                b = (t % 3) * 2
                if t >= 3:
                    pe.wait_ge(qk_read, t - 2)
                    pe.wait_ge(vd, t - 2)
                pairs = products((c.hT_high, c.hT_low), w)
                for out, lo, hi in ((c.bank(b), 0, 4), (c.bank(b + 1, 256), 4, 6))[0 if q_cols(t)[0] == 0 else 1:]:
                    for k in range(KD):
                        for i, (h, m) in enumerate(pairs):
                            last = nc.tensor.matmul(out, h[:, k, t * P:(t + 1) * P], m[:, lo:hi, k, :],
                                                    start=(k == 0 and i == 0), stop=(k == KD - 1 and i == 2))
                last.then_inc(proj, 1)

            def turn(t):
                b = 6
                pe.wait_ge(ready, t + 1)
                if t >= 1:
                    pe.wait_ge(evac, t)
                if q_cols(t)[0] == 0:
                    for j in range(PAIRS):
                        nc.tensor.transpose(c.psum[:, b * 512 + j * P:b * 512 + (j + 1) * P],
                                            qr[:, t % 2, j * P:(j + 1) * P], c.ident[:])
                for j in range(KV_HEADS):
                    last = nc.tensor.transpose(c.psum[:, (b + 1) * 512 + j * P:(b + 1) * 512 + (j + 1) * P],
                                               kd[:, t % 2, j * P:(j + 1) * P], c.ident[:])
                last.then_inc(turned, 1)

            for t in tiles:
                project(t)
                if t >= 2:
                    turn(t - 2)
            turn(NT - 2)
            turn(NT - 1)

        @ph.block.scalar
        def _(act):
            def keep(t):
                b = 6
                act.wait_ge(turned, t + 1)
                if q_cols(t)[0] == 0:
                    nc.scalar.activation(qT[:, :, t * P:(t + 1) * P], c.bank(b).rearrange("p (a b) -> p a b", a=PAIRS), ACT.Copy)
                nc.scalar.activation(kT[:, :, t * P:(t + 1) * P], c.bank(b + 1, 256).rearrange("p (a b) -> p a b", a=2),
                                     ACT.Copy).then_inc(evac, 1)

            for t in tiles:
                b = (t % 3) * 2
                lo, hi = q_cols(t)
                act.wait_ge(proj, t + 1)
                if t >= 2:
                    act.wait_ge(ms, t - 1)
                nc.scalar.activation(sqb[:, t % 2, lo:hi], c.psum[:, b * 512 + lo:b * 512 + hi], ACT.Square).then_inc(sq_d, 1)
                nc.scalar.activation(vN[:, t], c.psum[:, b * 512 + 640:b * 512 + 768], ACT.Copy).then_inc(vd, 1)
                act.wait_ge(ms, t + 1)
                nc.scalar.activation(ssq[:, t % 2, lo // HD:10], ssq[:, t % 2, lo // HD:10], ACT.Sqrt).then_inc(root, 1)
                if t >= 2:
                    keep(t - 2)
            keep(NT - 2)
            keep(NT - 1)

        @ph.block.vector
        def _(dve):
            st = Steps(dve, steps)

            def means(t):
                p = t % 2
                lo, hi = q_cols(t)
                h0 = lo // HD
                heads = lambda v: v[:, lo:hi].rearrange("p (h d) -> p h d", d=HD)
                dve.wait_ge(sq_d, t + 1)
                if t >= 2:
                    dve.wait_ge(root, t - 1)
                st.wait()
                st.do(nc.vector.tensor_reduce(ssq[:, p, h0:10], heads(sqb[:, p]), AX.X, ALU.add))
                st.wait()
                nc.vector.tensor_scalar(ssq[:, p, h0:10], ssq[:, p, h0:10], 1.0 / HD, EPS, ALU.mult, ALU.add).then_inc(ms, 1)

            means(0)
            dve.wait_ge(gain_in, 16)
            for t in tiles:
                if t + 1 < NT:
                    means(t + 1)
                b, p = (t % 3) * 2, t % 2
                lo, hi = q_cols(t)
                h0, nh = lo // HD, (hi - lo) // HD
                heads = lambda v: v[:, lo:hi].rearrange("p (h d) -> p h d", d=HD)
                dve.wait_ge(root, t + 1)
                st.do(nc.vector.reciprocal(rr[:, p, h0:10], ssq[:, p, h0:10]))
                st.wait()
                if h0 == 0:
                    st.do(nc.vector.tensor_scalar(rr[:, p, 0:HEADS], rr[:, p, 0:HEADS], HD ** -0.5, None, ALU.mult))
                    st.wait()
                nc.vector.tensor_tensor(heads(qn[:, p]), c.psum[:, b * 512 + lo:b * 512 + hi].rearrange("p (h d) -> p h d", d=HD),
                                        rr[:, p, h0:10].unsqueeze(2).to_broadcast([P, nh, HD]), ALU.mult).then_inc(qk_read, 1)
                dve.wait_ge(qk_read, t + 1)
                if t >= 2:
                    dve.wait_ge(turned, t - 1)
                target = qn if t < NT_LAT else qr
                st.do(nc.vector.tensor_tensor(target[:, p, lo:hi], qn[:, p, lo:hi], gain[:, lo:hi], ALU.mult))
                st.wait()
                if t < NT_LAT:
                    half = lambda v, i: v.rearrange("p (g r c) -> p g r c", r=2, c=16)[:, :, i, :].rearrange(
                        "p (h a) c -> p h a c", a=2)
                    table = lambda i: c.rope[:, t, i].unsqueeze(1).to_broadcast([P, 10, 2, 16])
                    w4 = [tmp[:, i].rearrange("p (h a c) -> p h a c", a=2, c=16) for i in range(4)]
                    for i, (h, s) in enumerate(((0, 0), (1, 1), (1, 0), (0, 1))):
                        st.do(nc.vector.tensor_tensor(w4[i], half(qn[:, p], h), table(s), ALU.mult))
                    st.wait()
                    st.do(nc.vector.tensor_tensor(half(qr[:, p], 0), w4[0], w4[1], ALU.subtract))
                    st.do(nc.vector.tensor_tensor(half(qr[:, p], 1), w4[2], w4[3], ALU.add))
                    st.wait()
                nc.vector.tensor_copy(kd[:, p].rearrange("p (v r d) -> p v r d", r=2, d=HD),
                                      qr[:, p, 512:640].rearrange("p (v d) -> p v d", d=HD).unsqueeze(2).to_broadcast(
                                          [P, KV_HEADS, 2, HD])).then_inc(ready, 1)


def conv_jobs():
    jobs = []
    for j in range(KB_BR):
        jobs += [("cg", j, B_SC + KB_BR + j), ("xs", j, B_SC + 2 * KB_BR + j), ("bg", j, B_SC + j)]
    for j in range(KB_BR):
        jobs += [(q, j, B_HY + q * KB_BR + j) for q in range(3)]
    return jobs


def conv_blocks(c, layer):
    return [(c.io["w_in"][layer][b], KD) for _, _, b in conv_jobs()]


def phase_attention(c, layer, full):
    nc = c.nc
    qT, kT, vN = c.at(116, PAIRS, T_ALL), c.at(128, KV_HEADS, T_ALL), c.at(134, NT, P)
    prob = c.at(137, 3, T_ALL)
    pT = c.at(146, 2, NT, L_LAT)
    yT = c.own(80, KB_BR, T_ALL)
    nmax, rsum, rinv = c.at(170, 4), c.at(170.25, 4), c.at(170.5, 4)
    groups = []
    for qs, keys in ((range(NT_LAT), range(NT)), (range(NT_LAT, NT), range(NT_LAT, NT)))[:2 if full else 1]:
        for pair in range(PAIRS):
            for hh in range(2):
                groups.append((pair, hh, list(qs), list(keys)))
    units = [(g, i, q) for g, (_, _, qs, _) in enumerate(groups) for i, q in enumerate(qs)]
    last_unit = [max(u for u, x in enumerate(units) if x[0] == g) for g in range(len(groups))]
    with Phase(nc) as ph:
        scored, maxed, exped, normed, turned, kept, summed, y_kept, steps = (ph.sem(s) for s in (
            "scores_ready", "max_ready", "exp_done", "probs_ready", "probs_turned", "turned_kept",
            "values_summed", "y_kept", "dve_steps"))
        ring = SplitRing(c, ph, conv_blocks(c, layer)[:4])

        @ph.block.sync
        def _(sp):
            ring.load(sp, None)

        @ph.block.gpsimd
        def _(pool):
            ring.prepare(pool)

        @ph.block.tensor
        def _(pe):
            def score(u):
                g, _, q = units[u]
                pair, hh, _, keys = groups[g]
                kv = (2 * pair + hh) // (HEADS // KV_HEADS)
                if u >= 2:
                    pe.wait_ge(exped, u - 1)
                b = (u % 2) * 1024
                r = slice(64 * hh, 64 * hh + 64)
                if keys[0] == 0:
                    nc.tensor.matmul(c.psum[:, b:b + 512], qT[r, pair, q * P:(q + 1) * P], kT[r, kv, 0:512], start=True, stop=True)
                nc.tensor.matmul(c.psum[:, b + 512:b + 768], qT[r, pair, q * P:(q + 1) * P], kT[r, kv, 512:768],
                                 start=True, stop=True).then_inc(scored, 1)

            def turn(u):
                g = units[u][0]
                pe.wait_ge(normed, u + 1)
                if u >= 1:
                    pe.wait_ge(kept, u)
                for kt in groups[g][3]:
                    last = nc.tensor.transpose(c.psum[:, 2048 + kt * P:2048 + (kt + 1) * P], prob[:, u % 3, kt * P:(kt + 1) * P], c.ident[:])
                last.then_inc(turned, 1)

            def values(g):
                pair, hh, qs, keys = groups[g]
                kv = (2 * pair + hh) // (HEADS // KV_HEADS)
                w = len(qs) * P
                pe.wait_ge(kept, last_unit[g] + 1)
                if hh == 0 and g >= 4:
                    pe.wait_ge(y_kept, g // 2 - 1)
                bank = 6 + (g // 2) % 2
                for i, kt in enumerate(keys):
                    last = nc.tensor.matmul(c.psum[64 * hh:64 * hh + 64, bank * 512:bank * 512 + w], vN[:, kt, kv * HD:(kv + 1) * HD],
                                            pT[:, g % 2, kt, 0:w], start=(i == 0), stop=(i == len(keys) - 1))
                last.then_inc(summed, 1)

            for u in range(len(units) + 3):
                if u < len(units):
                    score(u)
                if 2 <= u < len(units) + 2:
                    turn(u - 2)
                if u >= 3 and (u - 3) in last_unit:
                    values(last_unit.index(u - 3))

        @ph.block.vector
        def _(dve):
            st = Steps(dve, steps)
            for u in range(len(units) + 1):
                if u < len(units):
                    lo = groups[units[u][0]][3][0] * P
                    dve.wait_ge(scored, u + 1)
                    nc.vector.tensor_reduce(nmax[:, u % 4:u % 4 + 1], c.psum[:, (u % 2) * 1024 + lo:(u % 2) * 1024 + 768],
                                            AX.X, ALU.max, negate=True).then_inc(maxed, 1)
                if u >= 1:
                    v = u - 1
                    lo = groups[units[v][0]][3][0] * P
                    dve.wait_ge(exped, v + 1)
                    st.do(nc.vector.reciprocal(rinv[:, v % 4:v % 4 + 1], rsum[:, v % 4:v % 4 + 1]))
                    st.wait()
                    nc.vector.tensor_scalar(prob[:, v % 3, lo:768], prob[:, v % 3, lo:768], rinv[:, v % 4:v % 4 + 1], None,
                                            ALU.mult).then_inc(normed, 1)

        @ph.block.scalar
        def _(act):
            def keep(u):
                g, i, q = units[u]
                _, hh, qs, keys = groups[g]
                act.wait_ge(turned, u + 1)
                if g >= 2:
                    act.wait_ge(summed, g - 1)
                nc.scalar.activation(pT[:, g % 2, keys[0]:NT, i * P:(i + 1) * P],
                                     c.psum[:, 2048 + keys[0] * P:2048 + 768].rearrange("p (k q) -> p k q", q=P),
                                     ACT.Copy).then_inc(kept, 1)

            def keep_y(pr):
                pair, _, qs, _ = groups[2 * pr]
                w, q0 = len(qs) * P, qs[0] * P
                act.wait_ge(summed, 2 * pr + 2)
                nc.scalar.activation(yT[:, pair, q0:q0 + w], c.bank(6 + pr % 2, w), ACT.Copy).then_inc(y_kept, 1)

            pairs_done = 0
            for u in range(len(units) + 4):
                if u < len(units):
                    lo = groups[units[u][0]][3][0] * P
                    act.wait_ge(maxed, u + 1)
                    if u >= 3:
                        act.wait_ge(turned, u - 2)
                    nc.scalar.activation(prob[:, u % 3, lo:768], c.psum[:, (u % 2) * 1024 + lo:(u % 2) * 1024 + 768], ACT.Exp,
                                         bias=nmax[:, u % 4:u % 4 + 1], accum_out=rsum[:, u % 4:u % 4 + 1]).then_inc(exped, 1)
                if 2 <= u < len(units) + 2:
                    keep(u - 2)
                if u >= 4 and (u - 4) in last_unit and last_unit.index(u - 4) % 2 == 1:
                    keep_y(pairs_done)
                    pairs_done += 1


def dwconv(c, st, u, src, streams, w0, w2, done):
    nc = c.nc
    for a, n in streams:
        st.do(nc.vector.scalar_tensor_tensor(out=u[:, a + 1:a + n], in0=src[:, a:a + n - 1], scalar=w0,
                                             in1=u[:, a + 1:a + n], op0=ALU.mult, op1=ALU.add))
    st.wait()
    for i, (a, n) in enumerate(streams):
        ins = nc.vector.scalar_tensor_tensor(out=u[:, a:a + n - 1], in0=src[:, a + 1:a + n], scalar=w2,
                                             in1=u[:, a:a + n - 1], op0=ALU.mult, op1=ALU.add)
        if i < len(streams) - 1:
            st.do(ins)
    ins.then_inc(done, 1)


def feature_job(c, w, bank, width, kt, rhs, ahead=None):
    nc = c.nc
    for lo, hi in ((0, 512), (512, width)):
        if hi <= lo:
            continue
        for k in range(kt):
            if ahead is not None and lo == 0:
                ahead(k)
            for i, (a, b) in enumerate(products(w, rhs)):
                last = nc.tensor.matmul(c.psum[:, bank * 512 + lo:bank * 512 + hi], a[:, k], b[:, k, lo:hi],
                                        start=(k == 0 and i == 0), stop=(k == kt - 1 and i == 2))
    return last


def phase_conv_branches(c, layer, full):
    nc, io = c.nc, c.io
    width = T_ALL if full else L_LAT
    streams = [(0, L_LAT), (L_LAT, L_CTX)][:2 if full else 1]
    nt = width // P
    ysc = c.own(92, KB_BR, T_ALL)
    x2T = c.at(140, KB_BR, T_ALL)
    vN, x1N = c.at(116, NT, W_BR), c.at(128, NT, W_BR)
    cgs, cx, yc = c.at(152, 2, T_ALL), c.at(158, 2, T_ALL), c.at(164, 2, T_ALL)
    uu = c.at(170, 2, T_ALL)
    halves = [(a, n // 2) for a, n in streams]
    mirror = c.at(104, 2, T_ALL // 2)
    jobs = conv_jobs()
    H0 = 3 * KB_BR
    turns = [n for n, x in enumerate(jobs) if x[0] in (0, 1)]
    acts = [sum(x[0] != "bg" for x in jobs[:n + 1]) for n in range(len(jobs))]
    SLOTS = 3
    TB = 3072
    with Phase(nc) as ph:
        ring = SplitRing(c, ph, conv_blocks(c, layer), ahead=4)
        restored, proj, a_done, cx_ready, sc_done, conv_done, turned, kept, steps = (ph.sem(s) for s in (
            "restored", "projected", "act_done", "cx_ready", "sc_done", "conv_done", "transposed", "turned_kept", "dve_steps"))
        mirrored = ph.sem("mirrored")

        def cols(base, tap, tile, tiles):
            i = base + tap * tiles + tile
            return c.cols[:, i:i + 1]

        def psum_read(n):
            kind, j, _ = jobs[n]
            return {"cg": (a_done, acts[n]), "xs": (cx_ready, j + 1), "bg": (sc_done, j + 1)}.get(
                kind, (conv_done, n - H0 + 1))

        def slot(n):
            return c.psum[:, (n % SLOTS) * 1024:(n % SLOTS) * 1024 + width]

        @ph.block.sync
        def _(sp):
            ring.load(sp, proj)

        def restore(eng, ks):
            for k in ks:
                eng.tensor_tensor(c.hT[:, k], c.hT_low[:, k].bitcast(F32), c.hT_high[:, k].bitcast(F32), ALU.add).then_inc(restored, 1)

        @ph.block.gpsimd
        def _(pool):
            ring.split(pool)
            pool.wait_ge(proj, len(jobs))
            restore(nc.gpsimd, range(5, KD))

        @ph.block.tensor
        def _(pe):
            def turn(m):
                pe.wait_ge(mirrored, len(halves) * (m + 1))
                if m >= 1:
                    pe.wait_ge(kept, m)
                for a, half in halves:
                    for src, at, to in ((uu, a, a), (mirror, a // 2, a + half)):
                        for i in range(0, half, P):
                            last = nc.tensor.transpose(c.psum[:, TB + to + i:TB + to + i + P],
                                                       src[:, m % 2, at + i:at + i + P], c.ident[:])
                last.then_inc(turned, 1)

            m = 0
            for n in range(len(jobs)):
                ring.wait(pe, n)
                if n >= SLOTS:
                    pe.wait_ge(*psum_read(n - SLOTS))
                feature_job(c, ring.parts(n), 2 * (n % SLOTS), width, KD, (c.hT_high, c.hT_low)).then_inc(proj, 1)
                while m < len(turns) and turns[m] <= n - 2:
                    turn(m)
                    m += 1
            while m < len(turns):
                turn(m)
                m += 1

        @ph.block.scalar
        def _(act):
            def keep(m):
                kind, j, _ = jobs[turns[m]]
                act.wait_ge(turned, m + 1)
                nc.scalar.activation((vN if kind == 0 else x1N)[:, 0:nt, j * P:(j + 1) * P],
                                     c.psum[:, TB:TB + nt * P].rearrange("p (t q) -> p t q", q=P), ACT.Copy).then_inc(kept, 1)

            def turn_round(m):
                act.wait_ge(conv_done, turns[m] - H0 + 1)
                if m >= 2:
                    act.wait_ge(turned, m - 1)
                for a, half in halves:
                    nc.scalar.activation(mirror[:, m % 2, a // 2:a // 2 + half],
                                         uu[:, m % 2, a + 2 * half - 1:a + half - 1:-1], ACT.Copy).then_inc(mirrored, 1)

            m = rounds = 0
            ring.round_ahead(act, -1, proj)
            for n, (kind, j, b) in enumerate(jobs):
                if kind == "cg":
                    act.wait_ge(proj, n + 1)
                    if j >= 2:
                        act.wait_ge(cx_ready, j - 1)
                    nc.scalar.activation(cgs[:, j % 2, 0:width], slot(n), ACT.Copy).then_inc(a_done, 1)
                elif kind == "xs":
                    act.wait_ge(cx_ready, j + 1)
                    if j >= 2:
                        act.wait_ge(sc_done, j - 1)
                    nc.scalar.activation(yc[:, j % 2, 0:width], cx[:, j % 2, 0:width], ACT.Copy,
                                         scale=cols(C_SCW, 1, j, KB_BR)).then_inc(a_done, 1)
                elif kind != "bg":
                    act.wait_ge(proj, n + 1)
                    out = x2T[:, j, 0:width]
                    if kind < 2:
                        i = turns.index(n)
                        out = uu[:, i % 2, 0:width]
                        if i >= 2:
                            act.wait_ge(turned, i - 1)
                    i = kind * KB_BR + j
                    nc.scalar.activation(out, slot(n), ACT.Identity, scale=cols(C_HYW, 1, i, 3 * KB_BR),
                                         bias=c.cols[:, C_HYB + i:C_HYB + i + 1]).then_inc(a_done, 1)
                ring.round_ahead(act, n, proj)
                while rounds < len(turns) and turns[rounds] <= n - 1:
                    turn_round(rounds)
                    rounds += 1
                while m < len(turns) and turns[m] <= n - 2:
                    keep(m)
                    m += 1
            while m < len(turns):
                keep(m)
                m += 1

        @ph.block.vector
        def _(dve):
            st = Steps(dve, steps)
            for n, (kind, j, b) in enumerate(jobs):
                if kind == "xs":
                    dve.wait_ge(proj, n + 1)
                    dve.wait_ge(a_done, acts[n - 1])
                    nc.vector.tensor_tensor(cx[:, j % 2, 0:width], cgs[:, j % 2, 0:width], slot(n), ALU.mult).then_inc(cx_ready, 1)
                    dve.wait_ge(cx_ready, j + 1)
                    dve.wait_ge(a_done, acts[n])
                    dwconv(c, st, yc[:, j % 2], cx[:, j % 2], streams, cols(C_SCW, 0, j, KB_BR), cols(C_SCW, 2, j, KB_BR), steps)
                    st.n += 1
                elif kind == "bg":
                    dve.wait_ge(proj, n + 1)
                    st.wait()
                    nc.vector.tensor_tensor(ysc[:, j, 0:width], yc[:, j % 2, 0:width], slot(n), ALU.mult).then_inc(sc_done, 1)
                elif kind != "cg":
                    out = x2T[:, j] if kind == 2 else uu[:, turns.index(n) % 2]
                    i = kind * KB_BR + j
                    dve.wait_ge(a_done, acts[n])
                    dwconv(c, st, out, slot(n), streams, cols(C_HYW, 0, i, 3 * KB_BR), cols(C_HYW, 2, i, 3 * KB_BR), conv_done)
            dve.wait_ge(proj, len(jobs))
            restore(nc.vector, range(5))


def dft_views(c, length):
    nt, half = length // P, length // 2
    at, out = 48, {}
    for name, tiles, w in (("cos", nt // 2, length), ("sin", nt // 2, length), ("cos_back", nt, half),
                           ("sin_back", nt, half), ("filter_cos", nt, length), ("filter_sin", nt, length)):
        out[name] = c.at(at, tiles, w)
        at += tiles * w / 256
    out["all"] = c.at(48, int((at - 48) * 256))
    return out


def spectrum_views(c, nt):
    return c.at(152, nt, W_BR), c.at(160, nt, W_BR), c.at(168, W_BR)


def spectrum_jobs(nt):
    return [(w, f) for f in range(nt) for w in ("re", "im")] + [("top", 0)]


def phase_spectrum(c, layer, length, order):
    nc, io = c.nc, c.io
    nt = length // P
    which = 0 if length == L_LAT else 1
    tab = dft_views(c, length)
    times = slice(0, L_LAT) if length == L_LAT else slice(L_LAT, T_ALL)
    h2 = filter_hidden(c)[:, times]
    w3, absdec = c.at(152, 2 * W_BR), c.at(190, W_BR)
    win = c.at(156, nt, W_BR)
    rnorm, bias, ab = c.at(192, W_BR), c.at(194, W_BR), [c.at(196, 2 * W_BR), c.at(164, 2 * W_BR)]
    t_order = list(range(1, nt)) + [0]
    hw = c.at(170, nt, 2 * W_BR)
    kre, kim, kre_b = spectrum_views(c, nt)
    jobs = spectrum_jobs(nt)
    with Phase(nc) as ph:
        tab_in, w3_in, dec_in, bias_in, made, abs_d, win_d, hw_d, ab_d, normed, steps, folded, sums, kept = (ph.sem(s) for s in (
            "tables_landed", "w3_landed", "decay_landed", "bias_landed", "filter_made", "decay_abs", "window_done",
            "windowed", "abs_done", "norm_summed", "dve_steps", "folded", "spectrum_summed", "spectrum_kept"))

        @ph.block.sync
        def _(sp):
            sp.dma_start(w3[0:FH, :], io["hy_w3"][layer][:, order * 2 * W_BR:(order + 1) * 2 * W_BR]).then_inc(w3_in, 16)
            sp.dma_start(absdec, io["hy_decay"][layer][order:order + 1].to_broadcast([P, W_BR])).then_inc(dec_in, 16)
            sp.dma_start(bias[0:1, :], io["hy_bias"][layer][order:order + 1]).then_inc(bias_in, 16)
            if order == 0:
                sp.dma_start(tab["all"], io[f"dft{length}"]).then_inc(tab_in, 16)

        @ph.block.tensor
        def _(pe):
            def norm(t):
                pe.wait_ge(ab_d, t + 1)
                for d in range(2):
                    last = nc.tensor.matmul(c.bank(4), c.ones[:], ab[t % 2][:, d * W_BR:(d + 1) * W_BR],
                                            start=(t == 0 and d == 0), stop=(t == nt - 1 and d == 1))
                last.then_inc(normed, 1)

            c.warm_up(ph, pe, 7)
            pe.wait_ge(w3_in, 16)
            for t in range(nt):
                if t >= 2:
                    pe.wait_ge(hw_d, t - 1)
                for d in range(2):
                    last = nc.tensor.matmul(c.bank(2 * (t % 2) + d), h2[0:FH, t * P:(t + 1) * P], w3[0:FH, d * W_BR:(d + 1) * W_BR],
                                            start=True, stop=True)
                last.then_inc(made, 1)
                if t >= 1:
                    norm(t - 1)
            norm(nt - 1)
            if order == 0:
                pe.wait_ge(tab_in, 16)
            for n, (what, ft) in enumerate(jobs):
                if n >= 4:
                    pe.wait_ge(kept, n - 3)
                src = 1 if what == "im" else 0
                for i, t in enumerate(t_order):
                    if n == 0:
                        pe.wait_ge(folded, i + 1)
                    if what == "top":
                        out, table = c.bank(n % 4, 512, 1), c.consts[:, 10:11]
                    else:
                        out, table = c.bank(n % 4), tab["filter_sin" if src else "filter_cos"][:, t, ft * P:(ft + 1) * P]
                    last = nc.tensor.matmul(out, table, hw[:, t, src * W_BR:(src + 1) * W_BR],
                                            start=(i == 0), stop=(i == nt - 1))
                last.then_inc(sums, 1)

        @ph.block.scalar
        def _(act):
            act.wait_ge(dec_in, 16)
            nc.scalar.activation(absdec, absdec, ACT.Abs).then_inc(abs_d, 1)
            act.wait_ge(abs_d, 1)
            for t in range(nt):
                nc.scalar.activation(win[:, t], absdec, ACT.Exp, scale=c.consts[:, 4 * which + t:4 * which + t + 1]).then_inc(win_d, 1)
            for t in range(nt):
                act.wait_ge(hw_d, t + 1)
                if t >= 2:
                    act.wait_ge(normed, t - 1)
                nc.scalar.activation(ab[t % 2], hw[:, t], ACT.Abs).then_inc(ab_d, 1)

        @ph.block.vector
        def _(dve):
            st = Steps(dve, steps)
            for t in range(nt):
                dve.wait_ge(made, t + 1)
                dve.wait_ge(win_d, t + 1)
                nc.vector.tensor_tensor(hw[:, t].rearrange("p (d n) -> p d n", d=2),
                                        c.psum[:, (t % 2) * 1024:(t % 2) * 1024 + 1024].rearrange("p (d n) -> p d n", d=2),
                                        win[:, t].unsqueeze(1).to_broadcast([P, 2, W_BR]), ALU.mult).then_inc(hw_d, 1)
            for t in t_order:
                if t == 0:
                    dve.wait_ge(normed, nt)
                    dve.wait_ge(bias_in, 16)
                    st.do(nc.vector.tensor_tensor(hw[0:1, 0, W_BR:2 * W_BR], c.bank(4, 512, 1), bias[0:1, :], ALU.mult))
                    st.wait()
                else:
                    dve.wait_ge(ab_d, t + 1)
                st.do(nc.vector.tensor_tensor(hw[:, t, 0:W_BR], hw[:, t, 0:W_BR], hw[:, t, W_BR:2 * W_BR], ALU.add))
                st.wait()
                nc.vector.scalar_tensor_tensor(out=hw[:, t, W_BR:2 * W_BR], in0=hw[:, t, W_BR:2 * W_BR], scalar=-2.0,
                                               in1=hw[:, t, 0:W_BR], op0=ALU.mult, op1=ALU.add).then_inc(folded, 1)
            st.do(nc.vector.reciprocal(rnorm, c.bank(4)))
            st.wait()
            for n, (what, ft) in enumerate(jobs):
                rows = P
                if what == "top":
                    rows = 1
                    dve.wait_ge(kept, 1)
                    st.do(nc.vector.tensor_copy(kre_b, kre[:, 0]))
                    st.wait()
                dst = kre_b if what == "top" else (kre if what == "re" else kim)[:, ft]
                wf = c.consts[0:rows, 8 + which:9 + which] if ft == 0 else 1.0 / length
                dve.wait_ge(sums, n + 1)
                nc.vector.scalar_tensor_tensor(out=dst[0:rows], in0=c.bank(n % 4, 512, rows), scalar=wf, in1=rnorm[0:rows],
                                               op0=ALU.mult, op1=ALU.mult).then_inc(kept, 1)


def phase_long_conv(c, length, order):
    nc = c.nc
    nt, h, half = length // P, length // P // 2, length // 2
    t0 = 0 if length == L_LAT else NT_LAT
    tab = dft_views(c, length)
    kre, kim, kre_b = spectrum_views(c, nt)
    vN, x1N, x2T = c.at(116, NT, W_BR), c.at(128, NT, W_BR), c.at(140, KB_BR, T_ALL)
    yhy = c.own(104, KB_BR, T_ALL)
    yre, yim = c.at(170, nt, W_BR), c.at(178, nt, W_BR)
    tmp = c.at(188, 4, W_BR)
    z, image, d = vN[:, t0:t0 + h], vN[:, t0 + h:t0 + nt], c.at(196, h, W_BR)
    s = z
    n_back = h if order == 0 else KB_BR
    with Phase(nc) as ph:
        b_kept, paired, spec, read, prod, steps, back, taken, kept = (ph.sem(x) for x in (
            "b_kept", "pairs_ready", "spectrum_ready", "spectrum_read", "product_ready", "dve_steps", "back_summed",
            "back_taken", "back_kept"))

        def back_parts(n):
            if order == 0:
                return c.bank(4 + 2 * (n % 2)), c.bank(5 + 2 * (n % 2))
            bank = c.bank(4 + n % 4, length)
            return bank[:, 0:half], bank[:, half:length]

        @ph.block.tensor
        def _(pe):
            c.warm_up(ph, pe, 4)
            pe.wait_ge(paired, 2)
            for f in range(nt):
                even = f < h
                if f >= 2:
                    pe.wait_ge(read, f - 1)
                for i, (table, src) in enumerate(((tab["cos"], s if even else d), (tab["sin"], d if even else s))):
                    for t in range(h):
                        last = nc.tensor.matmul(c.bank(2 * (f % 2) + i), table[:, t, f * P:(f + 1) * P], src[:, t],
                                                start=(t == 0), stop=(t == h - 1))
                last.then_inc(spec, 1)
            pe.wait_ge(prod, nt)
            for n in range(n_back):
                if order == 0 and n >= 2:
                    pe.wait_ge(taken, 2 * (n - 1))
                for which, out in enumerate(back_parts(n)):
                    for f in range(nt):
                        y, table = (yre, tab["cos_back"]) if (f < h) == (which == 0) else (yim, tab["sin_back"])
                        if order == 0:
                            x, w = table[:, f, n * P:(n + 1) * P], y[:, f]
                        else:
                            x, w = y[:, f, n * P:(n + 1) * P], table[:, f, :]
                        last = nc.tensor.matmul(out, x, w, start=(f == 0), stop=(f == nt - 1))
                last.then_inc(back, 1)

        @ph.block.scalar
        def _(act):
            act.wait_ge(prod, nt)
            for n in range(n_back):
                act.wait_ge(back, n + 1)
                if n >= 2:
                    act.wait_ge(taken, 2 * (n - 1))
                b = back_parts(n)[1]
                nc.scalar.activation(tmp[:, 3 * (n % 2), 0:W_BR if order == 0 else half], b, ACT.Copy).then_inc(b_kept, 1)

        @ph.block.vector
        def _(dve):
            st = Steps(dve, steps)
            nc.vector.tensor_tensor(d, z, image, ALU.subtract).then_inc(paired, 1)
            dve.wait_ge(paired, 1)
            nc.vector.tensor_tensor(s, z, image, ALU.add).then_inc(paired, 1)
            for f in range(nt):
                ure, uim = c.bank(2 * (f % 2)), c.bank(2 * (f % 2) + 1)
                dve.wait_ge(spec, f + 1)
                if f:
                    dve.wait_ge(prod, f)
                st.do(nc.vector.tensor_tensor(tmp[:, 0], ure, kre[:, f], ALU.mult))
                st.do(nc.vector.tensor_tensor(tmp[:, 1], uim, kim[:, f], ALU.mult))
                st.do(nc.vector.tensor_tensor(tmp[:, 2], ure, kim[:, f], ALU.mult))
                nc.vector.tensor_tensor(tmp[:, 3], uim, kre[:, f] if f else kre_b, ALU.mult).then_inc(read, 1)
                st.wait()
                st.do(nc.vector.tensor_tensor(yre[:, f], tmp[:, 0], tmp[:, 1], ALU.subtract))
                dve.wait_ge(read, f + 1)
                nc.vector.tensor_tensor(yim[:, f], tmp[:, 2], tmp[:, 3], ALU.add).then_inc(prod, 1)
            dve.wait_ge(prod, nt)
            lo = t0 * P
            for n in range(n_back):
                width = W_BR if order == 0 else half
                dve.wait_ge(back, n + 1)
                if n:
                    dve.wait_ge(kept, 2 * n)
                a = back_parts(n)[0]
                b = tmp[:, 3 * (n % 2), 0:width]
                dve.wait_ge(b_kept, n + 1)
                nc.vector.tensor_tensor(tmp[:, 1, 0:width], a, b, ALU.add).then_inc(taken, 1)
                nc.vector.tensor_tensor(tmp[:, 2, 0:width], a, b, ALU.subtract).then_inc(taken, 1)
                if order == 0:
                    outs = ((z[:, n], x1N[:, t0 + n]), (image[:, n], x1N[:, t0 + h + n]))
                else:
                    first, mirrored = slice(lo, lo + half), slice(lo + length - 1, lo + half - 1, -1)
                    outs = tuple((yhy[:, n, r], x2T[:, n, r]) for r in (first, mirrored))
                for i, (out, gate) in enumerate(outs):
                    dve.wait_ge(taken, 2 * n + 1 + i)
                    nc.vector.tensor_tensor(out, tmp[:, 1 + i, 0:width], gate, ALU.mult).then_inc(kept, 1)


class Rows:

    def __init__(self, c, ph, wanted):
        self.c, self.wanted, self.n_all = c, wanted, len(wanted) * KD
        self.diag = c.at(197, 4, P)
        self.made, self.spread, self.kept = (ph.sem(s) for s in ("diagonals_made", "rows_spread", "rows_kept"))

    def vector(self, dve):
        for n in range(self.n_all):
            if n >= 4:
                dve.wait_ge(self.spread, n - 3)
            self.c.nc.vector.tensor_scalar(self.diag[:, n % 4], self.c.ident[:], self.wanted[n // KD][0](n % KD), None,
                                           ALU.mult).then_inc(self.made, 1)

    def tensor(self, pe):
        for n in range(self.n_all):
            w = n // KD
            pe.wait_ge(self.made, n + 1)
            if n % KD == 0 and w >= 4:
                pe.wait_ge(self.kept, w - 3)
            at = (w % 4) * 1024 + (n % KD) * P
            self.c.nc.tensor.matmul(self.c.psum[:, at:at + P], self.c.ones[:], self.diag[:, n % 4], start=True,
                                    stop=True).then_inc(self.spread, 1)
        pe.wait_ge(self.kept, len(self.wanted))

    def scalar(self, act):
        for w, (_, dst) in enumerate(self.wanted):
            act.wait_ge(self.spread, (w + 1) * KD)
            self.c.nc.scalar.activation(dst, self.c.psum[:, (w % 4) * 1024:(w % 4 + 1) * 1024], ACT.Copy).then_inc(self.kept, 1)


def phase_merge(c, layer, full):
    nc, io = c.nc, c.io
    width = T_ALL if full else L_LAT
    ys = [c.own(at, KB_BR, T_ALL) for at in (80, 92, 104)]
    y_high = [c.rounded(at, KB_BR, T_ALL) for at in (152, 188, 152)]
    h_high = c.rounded(164, KD, T_ALL)
    y_low = [c.rounded(at, KB_BR, T_ALL) for at in (80, 92, 104)]
    mT = c.own(116, KD, T_ALL)
    sig, tmp = c.own(140, 2, T_ALL), c.own(146, 2, T_ALL)
    gates = [(br, i) for br in range(3) for i in range(KD)]
    n_all = 2 * len(gates)
    SLOTS = 4
    AHEAD = (0, 2, KD + 2)
    with Phase(nc) as ph:
        blocks = []
        for br, i in gates:
            blocks += [(io["w_in"][layer][B_GATE + br * KD + i], KD), (io["w_br"][layer][br * KD + i], KB_BR)]
        ring = SplitRing(c, ph, blocks)
        proj, sig_d, gated, steps, h_rounded, h_split, y_rounded, y_split = (ph.sem(s) for s in (
            "projected", "sigmoid_done", "gated", "dve_steps", "h_high_ready", "h_split", "y_high_ready", "y_split"))

        @ph.block.sync
        def _(sp):
            ring.load(sp, proj)

        @ph.block.gpsimd
        def _(pool):
            ring.split(pool)

        @ph.block.tensor
        def _(pe):
            c.warm_up(ph, pe, 14)
            for n in range(n_all):
                (br, i), is_y = gates[n // 2], n % 2
                ring.wait(pe, n)
                if n >= SLOTS:
                    pe.wait_ge(gated if is_y else sig_d, (n - SLOTS) // 2 + 1)
                if is_y:
                    pe.wait_ge(y_split, br + 1)
                    job = feature_job(c, ring.parts(n), 2 * (n % SLOTS), width, KB_BR, (y_high[br], y_low[br]))
                else:
                    job = feature_job(c, ring.parts(n), 2 * (n % SLOTS), width, KD, (h_high, c.hT_low),
                                      (lambda k: pe.wait_ge(h_split, k + 1)) if n == 0 else None)
                job.then_inc(proj, 1)

        def slot(n):
            return c.psum[:, (n % SLOTS) * 1024:(n % SLOTS) * 1024 + width]

        @ph.block.scalar
        def _(act):
            def round_y(br):
                if br == 2:
                    act.wait_ge(proj, 2 * KD)
                nc.scalar.activation(y_high[br][:, :, 0:width], ys[br][:, :, 0:width], ACT.Copy).then_inc(y_rounded, 1)

            for k in range(KD):
                nc.scalar.activation(h_high[:, k, 0:width], c.hT[:, k, 0:width], ACT.Copy).then_inc(h_rounded, 1)
            ring.round_ahead(act, -1, proj)
            for g in range(len(gates)):
                if g in AHEAD:
                    round_y(AHEAD.index(g))
                act.wait_ge(proj, 2 * g + 1)
                if g >= 2:
                    act.wait_ge(gated, g - 1)
                nc.scalar.activation(sig[:, g % 2, 0:width], slot(2 * g), ACT.Sigmoid).then_inc(sig_d, 1)
                ring.round_ahead(act, 2 * g, proj)
                ring.round_ahead(act, 2 * g + 1, proj)

        @ph.block.vector
        def _(dve):
            def split_y(br):
                y = ys[br][:, :, 0:width]
                dve.wait_ge(y_rounded, br + 1)
                split(nc, nc.vector, y_high[br][:, :, 0:width], y_low[br][:, :, 0:width], y).then_inc(y_split, 1)

            st = Steps(dve, steps)
            for k in range(KD):
                dve.wait_ge(h_rounded, k + 1)
                split(nc, nc.vector, h_high[:, k, 0:width], c.hT_low[:, k, 0:width], c.hT[:, k, 0:width]).then_inc(h_split, 1)
            for g, (br, i) in enumerate(gates):
                if g in AHEAD:
                    split_y(AHEAD.index(g))
                dve.wait_ge(proj, 2 * g + 2)
                dve.wait_ge(sig_d, g + 1)
                if br:
                    st.wait()
                dst = tmp[:, g % 2, 0:width] if br else mT[:, i, 0:width]
                nc.vector.tensor_tensor(dst, sig[:, g % 2, 0:width], slot(2 * g + 1), ALU.mult).then_inc(gated, 1)
                if br:
                    dve.wait_ge(gated, g + 1)
                    st.do(nc.vector.tensor_tensor(mT[:, i, 0:width], mT[:, i, 0:width], dst, ALU.add))


def phase_out(c, layer, full):
    nc, io = c.nc, c.io
    mT, m_low, m_high = c.own(116, KD, T_ALL), c.rounded(116, KD, T_ALL), c.rounded(168, KD, T_ALL)
    rows = [c.at(160, D), c.at(164, D)]
    tmp = c.at(152, 2, D)
    nt = NT if full else NT_LAT
    width = nt * P
    with Phase(nc) as ph:
        gt1 = Rows(c, ph, [((lambda s: lambda k: c.mod[:, GT1 + k, s:s + 1])(s), rows[s]) for s in range(2 if full else 1)])
        ring = SplitRing(c, ph, [(io["w_out"][layer][b], KD) for b in range(KD)], slots=KD)
        w = ring.high, ring.low
        m_rounded, m_split, proj, scaled, steps = (ph.sem(s) for s in (
            "m_high_ready", "m_split", "projected", "scaled", "dve_steps"))

        @ph.block.sync
        def _(sp):
            ring.load(sp, None)

        @ph.block.gpsimd
        def _(pool):
            ring.split(pool)

        @ph.block.scalar
        def _(act):
            for k in range(KD):
                nc.scalar.activation(m_high[:, k, 0:width], mT[:, k, 0:width], ACT.Copy).then_inc(m_rounded, 1)
                if k == 3:
                    gt1.scalar(act)
            ring.round_ahead(act, -1, proj)

        @ph.block.tensor
        def _(pe):
            gt1.tensor(pe)
            for t in range(nt):
                if t >= 4:
                    pe.wait_ge(scaled, t - 3)
                for h in range(2):
                    if t == 0:
                        pe.wait_ge(ring.ready, 4 * h + 4)
                    for k in range(KD):
                        if t == 0 and h == 0:
                            pe.wait_ge(m_split, k + 1)
                        for i, (a, b) in enumerate(products((m_high, m_low), w)):
                            last = nc.tensor.matmul(c.bank(2 * (t % 4) + h), a[:, k, t * P:(t + 1) * P],
                                                    b[:, 4 * h:4 * h + 4, k, :], start=(k == 0 and i == 0),
                                                    stop=(k == KD - 1 and i == 2))
                last.then_inc(proj, 1)

        @ph.block.vector
        def _(dve):
            st = Steps(dve, steps)
            gt1.vector(dve)
            for k in range(KD):
                dve.wait_ge(m_rounded, k + 1)
                split(nc, nc.vector, m_high[:, k, 0:width], m_low[:, k, 0:width], mT[:, k, 0:width]).then_inc(m_split, 1)
            dve.wait_ge(gt1.kept, len(gt1.wanted))
            for t in range(nt):
                dve.wait_ge(proj, t + 1)
                if t >= 2:
                    st.wait()
                nc.vector.tensor_tensor(tmp[:, t % 2], c.psum[:, (t % 4) * 1024:(t % 4 + 1) * 1024],
                                        rows[0 if t < NT_LAT else 1], ALU.mult).then_inc(scaled, 1)
                dve.wait_ge(scaled, t + 1)
                st.do(nc.vector.tensor_tensor(c.xs[:, t], c.xs[:, t], tmp[:, t % 2], ALU.add))


def query_blocks(c, layer):
    return [(c.io["wq"][layer][h], KD) for h in range(PH)]


def phase_norm2(c, layer, full):
    nc = c.nc
    tiles = list(range(NT if full else NT_LAT))
    h2N = c.at(80, NT, D)
    high = c.rounded(160, KD, T_ALL)
    rows_a, rows_b = [c.at(136, D), c.at(144, D)], [c.at(140, D), c.at(148, D)]
    col = lambda base, s: lambda k: c.mod[:, base + k, s:s + 1]
    wanted = []
    for s in range(2 if full else 1):
        wanted += [((lambda s: lambda k: c.ab[:, 1, k, s:s + 1])(s), rows_a[s]), (col(SH2, s), rows_b[s]),
                   (col(GT2, s), c.at(128 + 4 * s, D))]
    with Phase(nc) as ph:
        mod_rows = Rows(c, ph, wanted)
        ring = SplitRing(c, ph, query_blocks(c, layer)[:4])
        sq, ms, root, steps = norm_sems(ph)
        ready, turned, kept, low = (ph.sem(s) for s in ("h2_ready", "transposed", "high_kept", "low_kept"))

        @ph.block.sync
        def _(sp):
            ring.load(sp, None)

        @ph.block.gpsimd
        def _(pool):
            ring.prepare(pool)

        def turned_tile(t):
            return c.psum[:, (t % 4) * 1024:(t % 4 + 1) * 1024].rearrange("p (k q) -> p k q", q=P)

        @ph.block.scalar
        def _(act):
            act_norm(c, act, tiles, sq, ms, root, between=mod_rows.scalar)
            for t in tiles:
                act.wait_ge(turned, t + 1)
                nc.scalar.activation(high[:, :, t * P:(t + 1) * P], turned_tile(t), ACT.Copy).then_inc(kept, 1)

        @ph.block.vector
        def _(dve):
            def low_part(t):
                dve.wait_ge(kept, t + 1)
                split(nc, nc.vector, high[:, :, t * P:(t + 1) * P], c.hT_low[:, :, t * P:(t + 1) * P],
                      turned_tile(t)).then_inc(low, 1)

            st = Steps(dve, steps)
            mod_rows.vector(dve)
            dve_norm(c, dve, st, tiles, sq, ms, root)
            dve.wait_ge(mod_rows.kept, len(wanted))
            for t in tiles:
                s = 0 if t < NT_LAT else 1
                st.do(nc.vector.scalar_tensor_tensor(out=h2N[:, t], in0=c.xs[:, t], scalar=c.stat[:, 0, t:t + 1], in1=rows_a[s],
                                                     op0=ALU.mult, op1=ALU.mult))
                st.wait()
                nc.vector.tensor_tensor(h2N[:, t], h2N[:, t], rows_b[s], ALU.add).then_inc(ready, 1)
                if t:
                    low_part(t - 1)
            low_part(tiles[-1])

        @ph.block.tensor
        def _(pe):
            mod_rows.tensor(pe)
            for t in tiles:
                pe.wait_ge(ready, t + 1)
                if t >= 4:
                    pe.wait_ge(low, t - 3)
                for k in range(KD):
                    last = nc.tensor.transpose(c.psum[:, (t % 4) * 1024 + k * P:(t % 4) * 1024 + (k + 1) * P],
                                               h2N[:, t, k * P:(k + 1) * P], c.ident[:])
                last.then_inc(turned, 1)


def phase_query(c, layer, full):
    nc, io = c.nc, c.io
    width = T_ALL if full else L_LAT
    nt = width // P
    qT = c.at(104, PH, T_ALL)
    keys = c.at(185, PH, 2 * NK)
    scores = c.at(136, NT * PH + 1, 2 * NK)
    h2_high = c.rounded(160, KD, T_ALL)
    units = [(t, h) for t in range(nt) for h in range(PH)]
    with Phase(nc) as ph:
        ring = SplitRing(c, ph, query_blocks(c, layer), ahead=4)
        keys_in, proj, kept, scored, score_kept, pad = (ph.sem(s) for s in (
            "keys_landed", "projected", "query_kept", "scored", "scores_kept", "pad_set"))

        @ph.block.sync
        def _(sp):
            ring.load(sp, proj)
            sp.dma_start(keys, io["keys"][layer]).then_inc(keys_in, 16)

        @ph.block.gpsimd
        def _(pool):
            ring.split(pool)
            pool.wait_ge(proj, PH)
            nc.gpsimd.memset(scores[:, len(units)], 0.0).then_inc(pad, 1)

        @ph.block.tensor
        def _(pe):
            for h in range(PH):
                ring.wait(pe, h)
                if h >= 2:
                    pe.wait_ge(kept, h - 1)
                feature_job(c, ring.parts(h), 2 * (h % 2), width, KD, (h2_high, c.hT_low)).then_inc(proj, 1)
            pe.wait_ge(keys_in, 16)
            pe.wait_ge(kept, PH)
            for u, (t, h) in enumerate(units):
                if u >= 8:
                    pe.wait_ge(score_kept, u // 2 - 3)
                at = 2048 + (u % 8) * 256
                nc.tensor.matmul(c.psum[:, at:at + 256], qT[:, h, t * P:(t + 1) * P], keys[:, h, :],
                                 start=True, stop=True).then_inc(scored, 1)

        @ph.block.scalar
        def _(act):
            ring.round_ahead(act, -1, proj)
            for h in range(PH):
                ring.round_ahead(act, h, proj)
                act.wait_ge(proj, h + 1)
                nc.scalar.activation(qT[:, h, 0:width], c.psum[:, (h % 2) * 1024:(h % 2) * 1024 + width],
                                     ACT.Copy).then_inc(kept, 1)
            for u in range(0, len(units), 2):
                at = 2048 + (u % 8) * 256
                act.wait_ge(scored, u + 2)
                nc.scalar.activation(scores[:, u:u + 2], c.psum[:, at:at + 512].rearrange("p (u n) -> p u n", u=2),
                                     ACT.Copy).then_inc(score_kept, 1)


def phase_experts(c, layer, full):
    nc, io = c.nc, c.io
    nt = NT if full else NT_LAT
    h2N = c.at(80, NT, D)
    gate2 = c.at(128, 2, D)
    scores = c.at(136, NT * PH + 1, 2 * NK)
    slots = [c.at(24 + 8 * i, 2 * D) for i in range(7)] + [c.at(104, 2 * D)]
    junk = c.at(112, 2, D)
    dots, gelus, probs, exps = (c.at(120 + 0.25 * i, 2, TOPK) for i in range(4))
    diag = c.at(121, 4, P)
    top1, top2, topc, e1, e2, iota = (c.at(123 + 0.125 * i, TOPK) for i in range(6))
    idx1, idx2, idxc, hi, lo = (c.at(124 + 0.125 * i, TOPK).bitcast(U32) for i in range(5))
    small = c.at(124.75, 2, 8)
    eidx = c.at(125, 2, TOPK).bitcast(U32)
    sc, cut = c.at(126, 2 * NK), c.at(127, 2 * NK)
    cand, cand_cut, hot1, hot2 = (c.at(185 + i, TOPK, TOPK) for i in range(4))
    upd = c.at(189, D)
    LOWEST = -3.0e38
    table = io["uv"][layer]
    with Phase(nc) as ph:
        landed = [ph.sem(f"slot_landed{s}") for s in range(RING)]
        (iota_d, idx_ready, slot_used, turn, dotted, gelued, diag_ready, psum_used, x_added, exp_ready, exp_done,
         steps, order) = (ph.sem(s) for s in (
             "iota_made", "indices_ready", "slot_used", "turn", "dot_ready", "gelu_done", "diagonal_ready",
             "sum_taken", "x_added", "topk_ready", "exp_done", "dve_steps", "order"))

        @ph.block.gpsimd
        def _(pool):
            nc.gpsimd.iota(iota, pattern=[[1, TOPK]], base=0, channel_multiplier=0,
                           allow_small_or_imprecise_dtypes=True).then_inc(iota_d, 1)
            with pool.Fori(0, nt) as t:
                with pool.Fori(0, PH // 2) as i:
                    for p in range(2):
                        n = t * PH + i * 2 + p
                        pool.wait_ge(idx_ready, n + 1)
                        pool.sem_inc(turn, 1)
                        for k in range(TOPK):
                            pool.wait_ge(slot_used, n * TOPK + (k + 1))
                            pool.sem_inc(turn, 1)
                            nc.gpsimd.indirect_dma_start(
                                out=slots[k % RING], out_offset=None, in_=table,
                                in_offset=bass.IndirectOffsetOnAxis(ap=eidx[:, p, k:k + 1], axis=0)
                            ).then_inc(landed[k % RING], 16)

        @ph.block.tensor
        def _(pe):
            pe.sem_inc(slot_used, RING)
            with pe.Fori(0, nt) as t:
                with pe.Fori(0, PH // 2) as i:
                    for p in range(2):
                        n = t * PH + i * 2 + p
                        pe.wait_ge(psum_used, n + 1)
                        for k in range(TOPK):
                            pe.wait_ge(diag_ready, n * TOPK + (k + 1))
                            for h in range(2):
                                last = nc.tensor.matmul(c.bank(2 * p + h), diag[:, k % 4],
                                                        slots[k % RING][:, D + h * 512:D + (h + 1) * 512],
                                                        start=(k == 0), stop=(k == TOPK - 1))
                            last.then_inc(slot_used, 1)

        @ph.block.scalar
        def _(act):
            def softmax_exp(n, p):
                act.wait_ge(exp_ready, n + 1)
                nc.scalar.activation(exps[:, p], topc, ACT.Exp, bias=small[:, p, 0:1], accum_out=small[:, p, 1:2]).then_inc(exp_done, 1)

            softmax_exp(0, 0)
            with act.Fori(0, nt) as t:
                with act.Fori(0, PH // 2) as i:
                    for p in range(2):
                        n = t * PH + i * 2 + p
                        for k in range(TOPK):
                            act.wait_ge(dotted, n * TOPK + (k + 1))
                            nc.scalar.activation(gelus[:, p, k:k + 1], dots[:, p, k:k + 1], ACT.Gelu).then_inc(gelued, 1)
                            if k == 12:
                                softmax_exp(n + 1, 1 - p)

        @ph.block.vector
        def _(dve):
            base, cnt = [0], [0]

            def do(ins):
                ins.then_inc(steps, 1)
                cnt[0] += 1

            def wait(apart=False):
                dve.wait_ge(steps, base[0] + cnt[0])
                if apart:
                    dve.sem_inc(order, 1)

            def top16(vals, cutv, top, idx):
                do(nc.vector.max(top[:, 0:8], vals))
                wait(True)
                do(nc.vector.max_index(idx[:, 0:8], top[:, 0:8], vals))
                do(nc.vector.match_replace(cutv, top[:, 0:8], vals, LOWEST))
                wait(True)
                do(nc.vector.max(top[:, 8:16], cutv))
                wait(True)
                do(nc.vector.max_index(idx[:, 8:16], top[:, 8:16], cutv))

            def topk_parts(n, q):
                do(nc.vector.tensor_copy(sc, scores[:, bass.ds(n, 1)].rearrange("p a n -> p (a n)")))
                wait(True)
                top16(sc[:, 0:NK], cut[:, 0:NK], top1, idx1)
                yield
                top16(sc[:, NK:], cut[:, NK:], top2, idx2)
                wait()
                yield
                grid = [P, TOPK, TOPK]
                do(nc.vector.tensor_tensor(cand, top1.unsqueeze(2).to_broadcast(grid), top2.unsqueeze(1).to_broadcast(grid), ALU.add))
                wait(True)
                top16(cand.rearrange("p a b -> p (a b)"), cand_cut.rearrange("p a b -> p (a b)"), topc, idxc)
                wait()
                nc.vector.tensor_scalar(small[:, q, 0:1], topc[:, 0:1], -1.0, None, ALU.mult).then_inc(exp_ready, 1)
                yield
                do(nc.vector.tensor_scalar(hi, idxc, 4, None, ALU.logical_shift_right))
                do(nc.vector.tensor_scalar(lo, idxc, 15, None, ALU.bitwise_and))
                wait()
                places = iota.unsqueeze(1).to_broadcast(grid)
                do(nc.vector.tensor_tensor(hot1, places, hi.unsqueeze(2).to_broadcast(grid), ALU.is_equal))
                do(nc.vector.tensor_tensor(hot2, places, lo.unsqueeze(2).to_broadcast(grid), ALU.is_equal))
                wait()
                do(nc.vector.tensor_tensor(hot1, hot1, idx1.unsqueeze(1).to_broadcast(grid), ALU.mult))
                do(nc.vector.tensor_tensor(hot2, hot2, idx2.unsqueeze(1).to_broadcast(grid), ALU.mult))
                wait()
                do(nc.vector.tensor_reduce(e1, hot1, AX.X, ALU.add))
                do(nc.vector.tensor_reduce(e2, hot2, AX.X, ALU.add))
                wait()
                nc.vector.scalar_tensor_tensor(out=eidx[:, q], in0=e1, scalar=float(NK), in1=e2, op0=ALU.mult,
                                               op1=ALU.add).then_inc(idx_ready, 1)
                yield
                dve.wait_ge(exp_done, n + 1)
                do(nc.vector.reciprocal(small[:, q, 2:3], small[:, q, 1:2]))
                wait()
                do(nc.vector.tensor_scalar(probs[:, q], exps[:, q], small[:, q, 2:3], None, ALU.mult))
                wait()

            def dot(n, t, p, k):
                if k >= 2:
                    dve.wait_ge(dotted, n * TOPK + (k - 1))
                dve.wait_ge(landed[k % RING], n * 32 + 16 * (k // RING + 1))
                nc.vector.scalar_tensor_tensor(out=junk[:, k % 2], in0=slots[k % RING][:, 0:D], scalar=1.0,
                                               in1=h2N[:, bass.ds(t, 1)].rearrange("p a n -> p (a n)"), op0=ALU.mult,
                                               op1=ALU.mult, accum_out=dots[:, p, k:k + 1]).then_inc(dotted, 1)

            def weigh(n, p, k):
                dve.wait_ge(gelued, n * TOPK + (k + 1))
                dve.wait_ge(slot_used, n * TOPK + (k + RING - 3))
                nc.vector.tensor_scalar(diag[:, k % 4], c.ident[:], gelus[:, p, k:k + 1], probs[:, p, k:k + 1], ALU.mult,
                                        ALU.mult).then_inc(diag_ready, 1)

            dve.sem_inc(psum_used, 2)
            dve.sem_inc(x_added, 1)
            dve.wait_ge(iota_d, 1)
            for _ in topk_parts(0, 0):
                pass
            per_unit = cnt[0]
            with dve.Fori(0, nt) as t:
                with dve.Fori(0, PH // 2) as i:
                    for p in range(2):
                        n = t * PH + i * 2 + p
                        base[0], cnt[0] = (n + 1) * per_unit, 0
                        parts = topk_parts(n + 1, 1 - p)
                        for k in range(TOPK):
                            dot(n, t, p, k)
                            if k >= 1:
                                weigh(n, p, k - 1)
                            if k in (3, 5, 7, 9, 14):
                                next(parts, None)
                        weigh(n, p, TOPK - 1)
                        assert cnt[0] == per_unit
                        dve.wait_ge(slot_used, n * TOPK + (TOPK + RING))
                        dve.wait_ge(x_added, n + 1)
                        nc.vector.tensor_tensor(upd, c.psum[:, 1024 * p:1024 * p + D],
                                                gate2[:, bass.ds(t // NT_LAT, 1)].rearrange("p a n -> p (a n)"),
                                                ALU.mult).then_inc(psum_used, 1)
                        dve.wait_ge(psum_used, n + 3)
                        x = c.xs[:, bass.ds(t, 1)].rearrange("p a n -> p (a n)")
                        nc.vector.tensor_tensor(x, x, upd, ALU.add).then_inc(x_added, 1)


def phase_final(c, out):
    nc, io = c.nc, c.io
    tiles = list(range(NT_LAT))
    gain, y = c.at(136, D), c.at(140, NT_LAT, D)
    with Phase(nc) as ph:
        sq, ms, root, steps = norm_sems(ph)
        gain_in, ready, stored = (ph.sem(s) for s in ("gain_landed", "rows_ready", "rows_stored"))

        @ph.block.scalar
        def _(act):
            act_norm(c, act, tiles, sq, ms, root)

        @ph.block.vector
        def _(dve):
            st = Steps(dve, steps)
            dve_norm(c, dve, st, tiles, sq, ms, root)
            dve.wait_ge(gain_in, 16)
            for t in tiles:
                nc.vector.scalar_tensor_tensor(out=y[:, t], in0=c.xs[:, t], scalar=c.stat[:, 0, t:t + 1], in1=gain,
                                               op0=ALU.mult, op1=ALU.mult).then_inc(ready, 1)

        @ph.block.sync
        def _(sp):
            sp.dma_start(gain, io["g_final"].to_broadcast([P, D])).then_inc(gain_in, 16)
            for t in tiles:
                sp.wait_ge(ready, t + 1)
                sp.dma_start(out[t * P:(t + 1) * P, :], y[:, t]).then_inc(stored, 16)
            sp.wait_ge(stored, 16 * NT_LAT)


def build(nc, io, out):
    with ExitStack() as ctx:
        c = Chip(nc, ctx, io)
        phase_load(c)
        for layer in range(DEPTH):
            full = layer < DEPTH - 1
            phase_mod(c, layer, full)
            phase_norm1(c, layer)
            phase_qkv(c, layer, full)
            phase_attention(c, layer, full)
            phase_conv_branches(c, layer, full)
            for length in (L_LAT, L_CTX)[:2 if full else 1]:
                for order in range(2):
                    phase_spectrum(c, layer, length, order)
                    phase_long_conv(c, length, order)
            phase_merge(c, layer, full)
            phase_out(c, layer, full)
            phase_norm2(c, layer, full)
            phase_query(c, layer, full)
            phase_experts(c, layer, full)
        phase_final(c, out)


def blocks(w):
    n_l, k, n = w.shape
    return np.ascontiguousarray(w.reshape(n_l, k // P, P, n // P, P).transpose(0, 3, 2, 1, 4))


def mod_blocks(w):
    w = w.reshape(w.shape[0], 2, KD // 2, P, -1, 512)
    return np.ascontiguousarray(w.transpose(0, 4, 1, 3, 2, 5)).reshape(w.shape[0], -1, P, KD // 2 * 512)


def columns(v):
    v = v.reshape(v.shape[0], -1, P)
    return v.transpose(0, 2, 1)


def layouts(a):
    a = {k: np.asarray(v) for k, v in a.items()}
    n_l = DEPTH
    tok = lambda v: np.ascontiguousarray(v.reshape(-1, P, D).transpose(1, 0, 2))
    fil = np.zeros((n_l, P, 4), np.float32)
    for i, k in enumerate(("hy_b1", "hy_f1", "hy_b2", "hy_f2")):
        fil[:, :FH, i] = a[k]
    keys = np.zeros((n_l, 2, DK, PH, 2, NK), np.float32)
    for p in range(2):
        keys[:, p, :, :, p, :] = a["peer_subkeys"][:, :, p].transpose(0, 3, 1, 2)
    out = {
        "x": tok(a["x"]), "ctx": tok(a["ctx"]),
        "cond": np.ascontiguousarray(np.stack([a["c"].reshape(KD, P).T, a["c_ctx"].reshape(KD, P).T], axis=2)),
        "rope": rope_table().reshape(P, NT_LAT, 2, 2, 16), "consts": shape_constants(),
        "cols": np.ascontiguousarray(np.concatenate(
            [columns(a["b_mod"]), columns(a["g_norm1"]), columns(a["g_norm2"]), columns(a["sc_conv_w"]),
             columns(a["hy_conv_w"]), columns(a["hy_conv_b"]), fil], axis=2)),
        "w_mod": mod_blocks(a["w_mod"]), "w_in": blocks(a["w_in"]), "w_out": blocks(a["w_out"]),
        "w_br": np.concatenate([blocks(a[k]) for k in ("w_br_att", "w_br_sc", "w_br_hy")], axis=1),
        "wq": blocks(a["peer_wq"]),
        "keys": keys.reshape(n_l, P, PH, 2 * NK),
        "gains": np.ascontiguousarray(np.concatenate([a["q_gain"]] * HEADS + [a["k_gain"]] * KV_HEADS, axis=1)),
        "hy_w1": a["hy_w1"], "hy_w2": a["hy_w2"], "hy_w3": a["hy_w3"],
        "hy_decay": a["hy_decay"], "hy_bias": a["hy_bias"],
        "g_final": a["g_final"].reshape(1, D),
    }
    out["feat"] = np.concatenate([filter_features(n) for n in (L_LAT, L_CTX)], axis=1)
    for length in (L_LAT, L_CTX):
        out[f"dft{length}"] = dft_tables(length)
    for layer in range(n_l):
        out[f"uv{layer}"] = np.concatenate([a["peer_u"][layer], a["peer_v"][layer]], axis=1)
    return out


def kernel(**inputs):
    import concourse.bacc as bacc
    from concourse.bass_utils import run_bass_kernel_spmd

    nc = bacc.Bacc("TRN2", target_bir_lowering=False, num_devices=1)
    arrays, io = {}, {}
    for name, a in layouts(inputs).items():
        arrays[f"in_{name}"] = a
        io[name] = nc.dram_tensor(f"in_{name}", a.shape, mybir.dt.from_np(a.dtype), kind="ExternalInput").ap()
    io["uv"] = [io.pop(f"uv{layer}") for layer in range(DEPTH)]
    out = nc.dram_tensor("out", (L_LAT, D), F32, kind="ExternalOutput").ap()
    build(nc, io, out)
    r = run_bass_kernel_spmd(nc, [arrays], core_ids=[0])
    return r.results[0]["out"].reshape(1, L_LAT, D)
```
